# Optimizing a Trainium2 kernel written in Bass

```python
import math
import jax
import jax.numpy as jnp
from jax import lax
import numpy as np

D_MODEL = 1024
BATCH = 1
SEQ = 512
DEPTH = 2

N_MIXERS = 4
HEAD_DIM = 64
ROPE_THETA = 10000.0
NORM_EPS = 1e-6
PLE_DIM = 256
Q_BLOCK = 128
NEG_INF = -1e30

DIFF_HEADS = D_MODEL // (2 * HEAD_DIM)
DIFF_VDIM = 2 * HEAD_DIM
DIFF_IN = 4 * DIFF_HEADS * HEAD_DIM + DIFF_HEADS * DIFF_VDIM
DIFF_OUT = DIFF_HEADS * DIFF_VDIM
DIFF_LAMBDA_STD = 0.1

NSA_HEADS = D_MODEL // HEAD_DIM
NSA_GROUPS = 4
NSA_CMP_LEN = 32
NSA_CMP_STRIDE = 16
NSA_CMP_HIDDEN = 128
NSA_SLC_BLOCK = 64
NSA_TOPN = 16
NSA_N_LOCAL = 2
NSA_WINDOW = 512
NSA_Q_CHUNK = 16
NSA_FORCE_BONUS = 1e4
NSA_IN = NSA_HEADS * HEAD_DIM + 6 * NSA_GROUPS * HEAD_DIM + 3 * NSA_HEADS
NSA_OUT = NSA_HEADS * HEAD_DIM

MOBA_HEADS = D_MODEL // HEAD_DIM
MOBA_BLOCK = 256
MOBA_TOPK = 3
MOBA_Q_CHUNK = 8
MOBA_IN = 3 * MOBA_HEADS * HEAD_DIM
MOBA_OUT = MOBA_HEADS * HEAD_DIM

DIL_PATTERNS = ((128, 1), (512, 4), (2048, 16))
DIL_HEADS = 8
DIL_Q_BLOCK = 64
DIL_IN = len(DIL_PATTERNS) * 3 * DIL_HEADS * HEAD_DIM
DIL_OUT = DIL_HEADS * HEAD_DIM

D_FF = 2816
CONV_WIDTH = 3

kernel_name = "hybrid_interleaved_sparse_attn_trunk"

def _layers_of(kind):
    return len(range(kind, DEPTH, N_MIXERS))

def rms_norm(x, g):
    xf = x.astype(jnp.float32)
    y = xf * lax.rsqrt(jnp.mean(xf * xf, axis=-1, keepdims=True) + NORM_EPS)
    return (y * g.astype(jnp.float32)).astype(x.dtype)

def rope_tables(positions):
    inv = ROPE_THETA ** (-jnp.arange(0, HEAD_DIM, 2, dtype=jnp.float32) / HEAD_DIM)
    ang = positions.astype(jnp.float32)[..., None] * inv
    return jnp.cos(ang)[:, :, None, :], jnp.sin(ang)[:, :, None, :]

def apply_rope(x, cos, sin):
    xf = x.astype(jnp.float32)
    x1, x2 = jnp.split(xf, 2, axis=-1)
    return jnp.concatenate([x1 * cos - x2 * sin, x2 * cos + x1 * sin], axis=-1).astype(x.dtype)

def masked_softmax(s, mask):
    s = jnp.where(mask, s.astype(jnp.float32), NEG_INF)
    m = jnp.max(s, axis=-1, keepdims=True)
    e = jnp.where(mask, jnp.exp(s - m), 0.0)
    return e / jnp.maximum(jnp.sum(e, axis=-1, keepdims=True), 1e-30)

def diff_attention(h, w_in, w_out, lam_q1, lam_k1, lam_q2, lam_k2, subln_g, cos, sin, lambda_init):
    B, S, _ = h.shape
    H, dk, dv = DIFF_HEADS, HEAD_DIM, DIFF_VDIM
    q, k, v = jnp.split(h @ w_in, [2 * H * dk, 4 * H * dk], axis=-1)
    q = apply_rope(q.reshape(B, S, 2 * H, dk), cos, sin).reshape(B, S, H, 2, dk)
    k = apply_rope(k.reshape(B, S, 2 * H, dk), cos, sin).reshape(B, S, H, 2, dk)
    v = v.reshape(B, S, H, dv)
    f32 = jnp.float32
    lam = (jnp.exp(jnp.sum(lam_q1.astype(f32) * lam_k1.astype(f32)))
           - jnp.exp(jnp.sum(lam_q2.astype(f32) * lam_k2.astype(f32))) + lambda_init)
    scale = dk ** -0.5
    nblk = S // Q_BLOCK
    q_blocks = q.reshape(B, nblk, Q_BLOCK, H, 2, dk).transpose(1, 0, 2, 3, 4, 5)
    key_pos = jnp.arange(S)

    def block(args):
        qi, start = args
        s = jnp.einsum('bqhcd,bkhcd->bhcqk', qi, k) * scale
        qpos = start + jnp.arange(Q_BLOCK)
        p = masked_softmax(s, key_pos[None, :] <= qpos[:, None])
        a = p[:, :, 0] - lam * p[:, :, 1]
        return jnp.einsum('bhqk,bkhd->bqhd', a.astype(v.dtype), v)

    o = lax.map(block, (q_blocks, jnp.arange(nblk) * Q_BLOCK))
    o = o.transpose(1, 0, 2, 3, 4).reshape(B, S, H, dv)
    o = rms_norm(o, subln_g) * (1.0 - lambda_init)
    return o.reshape(B, S, H * dv) @ w_out

def nsa_attention(h, w_in, w_out, ck_pos, ck_w1, ck_w2, cv_pos, cv_w1, cv_w2, cos, sin):
    B, S, _ = h.shape
    H, G, dk = NSA_HEADS, NSA_GROUPS, HEAD_DIM
    R = H // G
    kvw = G * dk
    splits = np.cumsum([H * dk, kvw, kvw, kvw, kvw, kvw, kvw]).tolist()
    q, kc, vc, ks, vs, kw, vw, g_logits = jnp.split(h @ w_in, splits, axis=-1)
    q = apply_rope(q.reshape(B, S, H, dk), cos, sin)
    kc = apply_rope(kc.reshape(B, S, G, dk), cos, sin)
    ks = apply_rope(ks.reshape(B, S, G, dk), cos, sin)
    kw = apply_rope(kw.reshape(B, S, G, dk), cos, sin)
    vc, vs, vw = (t_.reshape(B, S, G, dk) for t_ in (vc, vs, vw))
    gates = jax.nn.sigmoid(g_logits.astype(jnp.float32)).reshape(B, S, G, R, 3)
    qg = q.reshape(B, S, G, R, dk)
    scale = dk ** -0.5
    t = jnp.arange(S)

    n_cmp = (S - NSA_CMP_LEN) // NSA_CMP_STRIDE + 1
    cidx = np.arange(n_cmp)[:, None] * NSA_CMP_STRIDE + np.arange(NSA_CMP_LEN)[None, :]

    def compress(z, pos, w1, w2):
        zb = z[:, cidx] + pos[:, None, :]
        hid = jax.nn.gelu(jnp.einsum('bnlgd,ldf->bngf', zb, w1))
        return jnp.einsum('bngf,fd->bngd', hid, w2)

    k_cmp = compress(kc, ck_pos, ck_w1, ck_w2)
    v_cmp = compress(vc, cv_pos, cv_w1, cv_w2)
    s_c = jnp.einsum('bsgrd,bngd->bgrsn', qg, k_cmp) * scale
    cmask = jnp.asarray(cidx[:, -1])[None, :] <= t[:, None]
    p_c = masked_softmax(s_c, cmask)
    o_c = jnp.einsum('bgrsn,bngd->bsgrd', p_c.astype(v_cmp.dtype), v_cmp)

    bs = NSA_SLC_BLOCK
    n_slc = S // bs
    s_start = np.arange(n_slc) * bs
    overlap = ((cidx[:, 0][:, None] <= (s_start + bs - 1)[None, :])
               & (cidx[:, -1][:, None] >= s_start[None, :])).astype(np.float32)
    imp = jnp.einsum('bgrsn,nj->bgsj', p_c, jnp.asarray(overlap))
    cur = t // bs
    jb = jnp.arange(n_slc)
    causal_ok = jb[None, :] <= cur[:, None]
    back = cur[:, None] - jb[None, :]
    forced = (jb[None, :] == 0) | ((back >= 0) & (back < NSA_N_LOCAL))
    score = jnp.where(causal_ok, imp + jnp.where(forced, NSA_FORCE_BONUS, 0.0), NEG_INF)
    n_top = min(NSA_TOPN, n_slc)
    top_val, top_idx = lax.top_k(score, n_top)
    top_ok = top_val > 0.5 * NEG_INF

    ks_blk = ks.reshape(B, n_slc, bs, G, dk).transpose(0, 3, 1, 2, 4)
    vs_blk = vs.reshape(B, n_slc, bs, G, dk).transpose(0, 3, 1, 2, 4)
    qc = NSA_Q_CHUNK
    nch = S // qc
    q_ch = qg.reshape(B, nch, qc, G, R, dk).transpose(1, 0, 3, 4, 2, 5)
    idx_ch = top_idx.reshape(B, G, nch, qc, n_top).transpose(2, 0, 1, 3, 4)
    ok_ch = top_ok.reshape(B, G, nch, qc, n_top).transpose(2, 0, 1, 3, 4)
    b_ix = jnp.arange(B)[:, None, None, None]
    g_ix = jnp.arange(G)[None, :, None, None]
    m_sel = n_top * bs

    def slc_chunk(args):
        qi, idx, ok, start = args
        kg = ks_blk[b_ix, g_ix, idx]
        vg = vs_blk[b_ix, g_ix, idx]
        s = jnp.einsum('bgrqd,bgqnkd->bgrqnk', qi, kg) * scale
        kpos = idx[..., None] * bs + jnp.arange(bs)
        qpos = start + jnp.arange(qc)
        mask = ok[..., None] & (kpos <= qpos[None, None, :, None, None])
        p = masked_softmax(s.reshape(B, G, R, qc, m_sel), mask.reshape(B, G, 1, qc, m_sel))
        return jnp.einsum('bgrqm,bgqmd->bqgrd', p.astype(vg.dtype), vg.reshape(B, G, qc, m_sel, dk))

    o_s = lax.map(slc_chunk, (q_ch, idx_ch, ok_ch, jnp.arange(nch) * qc))
    o_s = o_s.transpose(1, 0, 2, 3, 4, 5).reshape(B, S, G, R, dk)

    W = NSA_WINDOW
    kw_p = jnp.pad(kw, ((0, 0), (W, 0), (0, 0), (0, 0)))
    vw_p = jnp.pad(vw, ((0, 0), (W, 0), (0, 0), (0, 0)))
    nqb = S // Q_BLOCK
    q_blk = qg.reshape(B, nqb, Q_BLOCK, G, R, dk).transpose(1, 0, 2, 3, 4, 5)

    def win_block(args):
        qi, start = args
        kk = lax.dynamic_slice_in_dim(kw_p, start, W + Q_BLOCK, axis=1)
        vv = lax.dynamic_slice_in_dim(vw_p, start, W + Q_BLOCK, axis=1)
        s = jnp.einsum('bqgrd,bkgd->bgrqk', qi, kk) * scale
        qpos = start + jnp.arange(Q_BLOCK)
        kpos = start - W + jnp.arange(W + Q_BLOCK)
        dist = qpos[:, None] - kpos[None, :]
        mask = (dist >= 0) & (dist < W) & (kpos[None, :] >= 0)
        p = masked_softmax(s, mask)
        return jnp.einsum('bgrqk,bkgd->bqgrd', p.astype(vv.dtype), vv)

    o_w = lax.map(win_block, (q_blk, jnp.arange(nqb) * Q_BLOCK))
    o_w = o_w.transpose(1, 0, 2, 3, 4, 5).reshape(B, S, G, R, dk)

    o = (o_c * gates[..., 0:1] + o_s * gates[..., 1:2] + o_w * gates[..., 2:3]).astype(h.dtype)
    return o.reshape(B, S, H * dk) @ w_out

def moba_attention(h, w_in, w_out, cos, sin):
    B, S, _ = h.shape
    H, dk, L = MOBA_HEADS, HEAD_DIM, MOBA_BLOCK
    q, k, v = jnp.split(h @ w_in, 3, axis=-1)
    q = apply_rope(q.reshape(B, S, H, dk), cos, sin)
    k = apply_rope(k.reshape(B, S, H, dk), cos, sin)
    v = v.reshape(B, S, H, dk)
    scale = dk ** -0.5
    nb = -(-S // L)
    pad = nb * L - S
    k_p = jnp.pad(k, ((0, 0), (0, pad), (0, 0), (0, 0)))
    v_p = jnp.pad(v, ((0, 0), (0, pad), (0, 0), (0, 0)))
    k_blk = k_p.reshape(B, nb, L, H, dk).transpose(0, 3, 1, 2, 4)
    v_blk = v_p.reshape(B, nb, L, H, dk).transpose(0, 3, 1, 2, 4)
    k_mean = jnp.mean(k_blk.astype(jnp.float32), axis=3).astype(k.dtype)
    t = jnp.arange(S)
    past = jnp.arange(nb)[None, :] < (t // L)[:, None]
    gate = jnp.where(past, jnp.einsum('bshd,bhjd->bhsj', q, k_mean).astype(jnp.float32), NEG_INF)
    n_top = max(min(MOBA_TOPK, nb - 1), 1)
    top_val, top_idx = lax.top_k(gate, n_top)
    top_ok = top_val > 0.5 * NEG_INF
    qc = MOBA_Q_CHUNK
    nch = S // qc
    q_ch = q.reshape(B, nch, qc, H, dk).transpose(1, 0, 3, 2, 4)
    idx_ch = top_idx.reshape(B, H, nch, qc, n_top).transpose(2, 0, 1, 3, 4)
    ok_ch = top_ok.reshape(B, H, nch, qc, n_top).transpose(2, 0, 1, 3, 4)
    b_ix = jnp.arange(B)[:, None, None, None]
    h_ix = jnp.arange(H)[None, :, None, None]
    m_sel = n_top * L

    def chunk(args):
        qi, idx, ok, start = args
        kg = k_blk[b_ix, h_ix, idx]
        vg = v_blk[b_ix, h_ix, idx]
        s_sel = jnp.einsum('bhqd,bhqnkd->bhqnk', qi, kg).reshape(B, H, qc, m_sel) * scale
        mask_sel = jnp.broadcast_to(ok[..., None], (B, H, qc, n_top, L)).reshape(B, H, qc, m_sel)
        blk_start = (start // L) * L
        ko = lax.dynamic_slice_in_dim(k_p, blk_start, L, axis=1)
        vo = lax.dynamic_slice_in_dim(v_p, blk_start, L, axis=1)
        s_own = jnp.einsum('bhqd,bkhd->bhqk', qi, ko) * scale
        qpos = start + jnp.arange(qc)
        kpos = blk_start + jnp.arange(L)
        mask_own = jnp.broadcast_to(kpos[None, :] <= qpos[:, None], (B, H, qc, L))
        p = masked_softmax(jnp.concatenate([s_sel, s_own], axis=-1),
                           jnp.concatenate([mask_sel, mask_own], axis=-1)).astype(v.dtype)
        return (jnp.einsum('bhqm,bhqmd->bqhd', p[..., :m_sel], vg.reshape(B, H, qc, m_sel, dk))
                + jnp.einsum('bhqk,bkhd->bqhd', p[..., m_sel:], vo))

    o = lax.map(chunk, (q_ch, idx_ch, ok_ch, jnp.arange(nch) * qc))
    o = o.transpose(1, 0, 2, 3, 4).reshape(B, S, H * dk)
    return o @ w_out

def dilated_attention(h, w_in, w_out, cos, sin):
    B, S, _ = h.shape
    Hg, dk = DIL_HEADS, HEAD_DIM
    n_g = len(DIL_PATTERNS)
    proj = (h @ w_in).reshape(B, S, n_g, 3, Hg, dk)
    q = apply_rope(proj[:, :, :, 0].reshape(B, S, n_g * Hg, dk), cos, sin).reshape(B, S, n_g, Hg, dk)
    k = apply_rope(proj[:, :, :, 1].reshape(B, S, n_g * Hg, dk), cos, sin).reshape(B, S, n_g, Hg, dk)
    v = proj[:, :, :, 2]
    k_grp = [k[:, :, g] for g in range(n_g)]
    v_grp = [v[:, :, g] for g in range(n_g)]
    scale = dk ** -0.5
    qb = DIL_Q_BLOCK
    nqb = S // qb
    q_blk = q.reshape(B, nqb, qb, n_g, Hg, dk).transpose(1, 0, 2, 3, 4, 5)

    def block(args):
        qi, start = args
        qpos = start + jnp.arange(qb)
        outs, lses = [], []
        for g, (win, dil) in enumerate(DIL_PATTERNS):
            n_off = win // dil + 1
            kpos = qpos[:, None] - dil * jnp.arange(n_off)[None, :]
            valid = kpos >= 0
            kpc = jnp.maximum(kpos, 0)
            kg = k_grp[g][:, kpc]
            vg = v_grp[g][:, kpc]
            s = jnp.einsum('bqhd,bqjhd->bhqj', qi[:, :, g], kg).astype(jnp.float32) * scale
            s = jnp.where(valid, s, NEG_INF)
            m = jnp.max(s, axis=-1, keepdims=True)
            e = jnp.exp(s - m)
            den = jnp.sum(e, axis=-1, keepdims=True)
            outs.append(jnp.einsum('bhqj,bqjhd->bqhd', (e / den).astype(vg.dtype), vg))
            lses.append((m + jnp.log(den))[..., 0])
        alpha = jax.nn.softmax(jnp.stack(lses, axis=-1), axis=-1).transpose(0, 2, 1, 3)
        o = outs[0] * alpha[..., 0:1]
        for g in range(1, n_g):
            o = o + outs[g] * alpha[..., g:g + 1]
        return o.astype(h.dtype)

    o = lax.map(block, (q_blk, jnp.arange(nqb) * qb))
    o = o.transpose(1, 0, 2, 3, 4).reshape(B, S, Hg * dk)
    return o @ w_out

def conv_ffn(h, w_up, conv_w, conv_b, w_down):
    S = h.shape[1]
    u = h @ w_up
    u_pad = jnp.pad(u, ((0, 0), (CONV_WIDTH - 1, 0), (0, 0)))
    c = conv_b + u_pad[:, 0:S] * conv_w[0]
    for j in range(1, CONV_WIDTH):
        c = c + u_pad[:, j:j + S] * conv_w[j]
    gate, val = jnp.split(c, 2, axis=-1)
    return (jax.nn.gelu(gate, approximate=True) * val) @ w_down

def setup_inputs(seed: int = 0) -> dict:
    key = jax.random.key(seed)
    keys = iter(jax.random.split(key, 40))
    f32 = jnp.float32

    def dense(shape, fan_in):
        return jax.random.normal(next(keys), shape, f32) * (fan_in ** -0.5)

    def gain(shape):
        return 1.0 + 0.05 * jax.random.normal(next(keys), shape, f32)

    def small(shape, std):
        return std * jax.random.normal(next(keys), shape, f32)

    nA, nB, nC, nD = (_layers_of(kd) for kd in range(N_MIXERS))
    x = jax.random.normal(next(keys), (BATCH, SEQ, D_MODEL), f32)
    p = jax.random.normal(next(keys), (DEPTH, BATCH, SEQ, PLE_DIM), f32)
    start = jax.random.randint(next(keys), (BATCH, 1), 0, 4096, dtype=jnp.int32)
    positions = start + jnp.arange(SEQ, dtype=jnp.int32)[None, :]
    return {
        'x': x,
        'p': p,
        'positions': positions,
        'norm_gains': gain((DEPTH, 4, D_MODEL)),
        'ple_norm_g': gain((DEPTH, D_MODEL)),
        'ple_gate_w': dense((DEPTH, D_MODEL, D_MODEL), D_MODEL),
        'ple_proj_w': dense((DEPTH, PLE_DIM, D_MODEL), PLE_DIM),
        'ffn_w_up': dense((DEPTH, D_MODEL, 2 * D_FF), D_MODEL),
        'ffn_conv_w': dense((DEPTH, CONV_WIDTH, 2 * D_FF), CONV_WIDTH),
        'ffn_conv_b': small((DEPTH, 2 * D_FF), 0.01),
        'ffn_w_down': dense((DEPTH, D_FF, D_MODEL), D_FF),
        'diff_w_in': dense((nA, D_MODEL, DIFF_IN), D_MODEL),
        'diff_w_out': dense((nA, DIFF_OUT, D_MODEL), DIFF_OUT),
        'diff_lam_q1': small((nA, HEAD_DIM), DIFF_LAMBDA_STD),
        'diff_lam_k1': small((nA, HEAD_DIM), DIFF_LAMBDA_STD),
        'diff_lam_q2': small((nA, HEAD_DIM), DIFF_LAMBDA_STD),
        'diff_lam_k2': small((nA, HEAD_DIM), DIFF_LAMBDA_STD),
        'diff_subln_g': gain((nA, DIFF_VDIM)),
        'nsa_w_in': dense((nB, D_MODEL, NSA_IN), D_MODEL),
        'nsa_w_out': dense((nB, NSA_OUT, D_MODEL), NSA_OUT),
        'nsa_ck_pos': small((nB, NSA_CMP_LEN, HEAD_DIM), 0.1),
        'nsa_ck_w1': dense((nB, NSA_CMP_LEN, HEAD_DIM, NSA_CMP_HIDDEN), NSA_CMP_LEN * HEAD_DIM),
        'nsa_ck_w2': dense((nB, NSA_CMP_HIDDEN, HEAD_DIM), NSA_CMP_HIDDEN),
        'nsa_cv_pos': small((nB, NSA_CMP_LEN, HEAD_DIM), 0.1),
        'nsa_cv_w1': dense((nB, NSA_CMP_LEN, HEAD_DIM, NSA_CMP_HIDDEN), NSA_CMP_LEN * HEAD_DIM),
        'nsa_cv_w2': dense((nB, NSA_CMP_HIDDEN, HEAD_DIM), NSA_CMP_HIDDEN),
        'moba_w_in': dense((nC, D_MODEL, MOBA_IN), D_MODEL),
        'moba_w_out': dense((nC, MOBA_OUT, D_MODEL), MOBA_OUT),
        'dil_w_in': dense((nD, D_MODEL, DIL_IN), D_MODEL),
        'dil_w_out': dense((nD, DIL_OUT, D_MODEL), DIL_OUT),
    }

def reference(x, p, positions, norm_gains, ple_norm_g, ple_gate_w, ple_proj_w,
              ffn_w_up, ffn_conv_w, ffn_conv_b, ffn_w_down,
              diff_w_in, diff_w_out, diff_lam_q1, diff_lam_k1, diff_lam_q2, diff_lam_k2, diff_subln_g,
              nsa_w_in, nsa_w_out, nsa_ck_pos, nsa_ck_w1, nsa_ck_w2, nsa_cv_pos, nsa_cv_w1, nsa_cv_w2,
              moba_w_in, moba_w_out, dil_w_in, dil_w_out):
    cos, sin = rope_tables(positions)
    for i in range(DEPTH):
        kind, j = i % N_MIXERS, i // N_MIXERS
        hn = rms_norm(x, norm_gains[i, 0])
        if kind == 0:
            lambda_init = 0.8 - 0.6 * math.exp(-0.3 * i)
            y = diff_attention(hn, diff_w_in[j], diff_w_out[j], diff_lam_q1[j], diff_lam_k1[j],
                               diff_lam_q2[j], diff_lam_k2[j], diff_subln_g[j], cos, sin, lambda_init)
        elif kind == 1:
            y = nsa_attention(hn, nsa_w_in[j], nsa_w_out[j], nsa_ck_pos[j], nsa_ck_w1[j], nsa_ck_w2[j],
                              nsa_cv_pos[j], nsa_cv_w1[j], nsa_cv_w2[j], cos, sin)
        elif kind == 2:
            y = moba_attention(hn, moba_w_in[j], moba_w_out[j], cos, sin)
        else:
            y = dilated_attention(hn, dil_w_in[j], dil_w_out[j], cos, sin)
        x = x + rms_norm(y, norm_gains[i, 1])
        hn = rms_norm(x, norm_gains[i, 2])
        f = conv_ffn(hn, ffn_w_up[i], ffn_conv_w[i], ffn_conv_b[i], ffn_w_down[i])
        x = x + rms_norm(f, norm_gains[i, 3])
        gate = jax.nn.sigmoid(rms_norm(x, ple_norm_g[i]) @ ple_gate_w[i])
        x = x + gate * (p[i] @ ple_proj_w[i])
    return x


_drawn_inputs = setup_inputs


def setup_inputs(seed=0):
    import zlib

    import numpy as np

    out = dict(_drawn_inputs(seed))
    spreads = {}
    factors = {'ple_norm_g': 7.611, 'ffn_conv_b': 5.053, 'nsa_ck_pos': 8.0}
    for name, (base, spread) in spreads.items():
        noise = np.random.default_rng([zlib.crc32(name.encode()), seed]).standard_normal(out[name].shape)
        drawn = base * np.exp(spread * noise) if base else spread * noise
        out[name] = jnp.asarray(drawn.astype(out[name].dtype))
    for name, factor in factors.items():
        out[name] = (out[name] * factor).astype(out[name].dtype)
    return out
```

```python
from contextlib import ExitStack, contextmanager
import math

import numpy as np

import concourse.bass as bass
import concourse.mybir as mybir

F32 = mybir.dt.float32
F32R = mybir.dt.float32r
BF16 = mybir.dt.bfloat16
I32 = mybir.dt.int32
ALU = mybir.AluOpType
ACT = mybir.ActivationFunctionType
AX = mybir.AxisListType

P = 128
SEQ = 512
D = 1024
TT = SEQ // P
KT = D // P
HEAD = 64
HALF = D // 2
LAYERS = 2
EPS = 1e-6
SCALE = HEAD ** -0.5
MASKED = -1e30
THETA = 10000.0

DIFF_HEADS = D // (2 * HEAD)
LAMBDA_INIT = 0.8 - 0.6 * math.exp(-0.3 * 0)

GROUPS = 4
GHEADS = D // HEAD // GROUPS
CMP_LEN = 32
CMP_STRIDE = 16
N_CMP = (SEQ - CMP_LEN) // CMP_STRIDE + 1
N_PAD = 32
CMP_HIDDEN = 128

FF = 2816
FT = FF // P
PLE = 256

RING = 4
RAW = 2
PLAN, _at = {}, 0
for _name, _n in (("v", 8), ("qk", 2 * DIFF_HEADS), ("out0", 8), ("up0", 2 * FT), ("down0", FT),
                  ("gate0a", 4), ("ple0", 2), ("gate0b", 4),
                  ("cmp", GROUPS), ("branch", 1), ("group", 4 * GROUPS), ("out1", 8), ("up1", 2 * FT),
                  ("down1", FT), ("gate1a", 4), ("ple1", 2), ("gate1b", 4)):
    PLAN[_name] = _at
    _at += _n
UNITS = _at

C_INV, C_SIGN, C_IDENT, C_CAUSAL, C_CMP = 0, 1, 2, 2 + P, 2 + 2 * P
C_ALL = C_CMP + TT * N_PAD
GAINS = 5
TWO_PI = 2 * math.pi
PI_1 = 6.28125
PI_2 = float(np.float32(TWO_PI - PI_1))
PI_3 = float(np.float32(TWO_PI - PI_1 - PI_2))
ROUND = 1.5 * 2.0 ** 23
PI_MAX = float(np.nextafter(np.float32(math.pi), np.float32(0)))


class Chain:

    def __init__(self, engine, sem):
        self.engine, self.sem, self.base, self.n = engine, sem, 0, 0

    def step(self, ins):
        ins.then_inc(self.sem, 1)
        self.n += 1

    def link(self, ins):
        self.step(ins)
        self.engine.wait_ge(self.sem, self.base + self.n)

    @contextmanager
    def loop(self, start, end, per):
        before = self.base + self.n
        with self.engine.Fori(start, end) as i:
            self.base, self.n = before + per * (i - start), 0
            yield i
            assert self.n == per, (self.n, per)
        self.base, self.n = before + per * (end - start), 0


def trunk(nc, x_in, w_in, const_in, gain_in, conv_in, subln_in, lam_in, pos_in, pT_in, w1_in,
          cpos_in, w2_in, out):
    ctx = ExitStack()
    with ctx:
        def sb(name, shape, dt=F32, on=ctx):
            return on.enter_context(nc.sbuf_tensor(name, shape, dt))

        x = sb("x", [P, TT, D])
        nT_hi = sb("nT_hi", [P, KT, SEQ], F32R)
        nT_lo = sb("nT_lo", [P, KT, SEQ], F32R)
        w_raw = [sb(f"w_raw{i}", [P, D]) for i in range(RAW)]
        w_hi = [sb(f"w_hi{i}", [P, D], F32R) for i in range(RING)]
        w_lo = [sb(f"w_lo{i}", [P, D], F32R) for i in range(RING)]
        cosT = sb("cosT", [P, SEQ])
        sinT = sb("sinT", [P, SEQ])
        g_pre = sb("g_pre", [P, D])
        g_post = sb("g_post", [P, D])
        xn = sb("xn", [P, D])
        ident = sb("ident", [P, P])
        ident_b = sb("ident_b", [P, P], BF16)
        causal_b = sb("causal_b", [P, P], BF16)
        conv = sb("conv", [P, 4 * 2 * FT])
        eps = sb("eps", [P, 1])
        ss = sb("ss", [P, TT])
        std = sb("std", [P, TT])
        rinv = sb("rinv", [P, TT])
        yss = sb("yss", [P, 2, TT])
        yst = sb("yst", [P, 3, TT])
        subg = sb("subg", [P, 1])
        neg_lam = sb("neg_lam", [P, 1])
        lam = sb("lam", [P, 4])
        junk = sb("junk", [P, D], BF16)
        y0 = sb("y0", [P, TT, HALF])

        mx = sb("mx", [P, TT, 2])
        nm = sb("nm", [P, TT, 2])
        sums = sb("sums", [P, 2, TT, 2])
        st1 = sb("st1", [P, 4])
        osum = sb("osum", [P, 4, TT])
        st2 = sb("st2", [P, 2, TT, 2])
        cst = sb("cst", [P, 3, TT * GHEADS])

        def overlay(*parts):
            with ExitStack() as on:
                return [sb(*part, on=on) for part in parts]

        const, pos_i, ang, turn, red, lam_v, lam_p = overlay(
            ("const", [P, C_ALL], F32), ("pos_i", [P, SEQ], I32), ("ang", [P, SEQ], F32),
            ("turn", [P, SEQ], F32), ("red", [P, SEQ], F32), ("lam_v", [P, 4, HEAD], F32), ("lam_p", [P, 2, HEAD], F32))
        (V, oT0_hi, oT0_lo, qT0, qT1, kT0, kT1, sh, t1, t2, pr, amix, pT, o_raw, o_nrm, o_sq) = overlay(
            ("V", [P, TT, D], F32), ("oT0_hi", [P, KT, SEQ], F32R), ("oT0_lo", [P, KT, SEQ], F32R),
            ("qT0", [P, SEQ], F32), ("qT1", [P, SEQ], F32), ("kT0", [P, SEQ], F32), ("kT1", [P, SEQ], F32),
            ("sh", [P, SEQ], F32), ("t1", [P, SEQ], F32), ("t2", [P, SEQ], F32),
            ("pr", [P, 2, 2, SEQ], F32), ("amix", [P, 2, SEQ], F32), ("pT", [P, 2, SEQ], F32),
            ("o_raw", [P, TT, P], F32), ("o_nrm", [P, TT, P], F32), ("o_sq", [P, TT, P], F32))
        qT, kT = [qT0, qT1], [kT0, kT1]
        hT_hi, hT_lo = overlay(("hT_hi", [P, FT, SEQ], F32R), ("hT_lo", [P, FT, SEQ], F32R))
        pe_raw, pe_hi, pe_lo, sg = overlay(
            ("pe_raw", [P, 2, SEQ], F32), ("pe_hi", [P, 2, SEQ], F32R), ("pe_lo", [P, 2, SEQ], F32R),
            ("sg", [P, TT, HALF], F32))
        keep1 = [("oT1_hi", [P, KT, SEQ], F32R), ("oT1_lo", [P, KT, SEQ], F32R),
                 ("kcmp", [HEAD, GROUPS, N_PAD], F32), ("Vblk", [P, GROUPS, GHEADS * HEAD], F32),
                 ("gates", [P, TT, 3 * D // HEAD], F32)]
        (oT1_hi, oT1_lo, kcmp, Vblk, gates, w1, zb, hid_k, hid_v, cpos, w2, ksh, kt1, kt2, kr) = overlay(
            *keep1, ("w1", [P, CMP_LEN, CMP_HIDDEN], F32), ("zb", [P, GROUPS, N_CMP, CMP_LEN], F32),
            ("hid_k", [P, GROUPS, N_PAD], F32), ("hid_v", [P, GROUPS, N_PAD], F32),
            ("cpos", [P, CMP_LEN], F32), ("w2", [P, 2, HEAD], F32),
            ("ksh", [HEAD, SEQ], F32), ("kt1", [HEAD, SEQ], F32), ("kt2", [HEAD, SEQ], F32),
            ("kr", [HEAD, SEQ], F32))
        (_, _, _, _, _, cm, Vg, vT, KK, Qa0, Qa1, Qx0, Qx1, gsh, gt1, gt2, gp, gpT, sc, pc, pcT, oc,
         og, opair) = overlay(
            *[("again_" + n, s, d) for n, s, d in keep1],
            ("cm", [P, 2, TT * N_PAD], F32),
            ("Vg", [P, TT, P], F32), ("vT", [P, SEQ], F32), ("KK", [P, SEQ], F32),
            ("Qa0", [P, SEQ], F32), ("Qa1", [P, SEQ], F32), ("Qx0", [P, SEQ], F32), ("Qx1", [P, SEQ], F32),
            ("gsh", [P, SEQ], F32), ("gt1", [P, SEQ], F32), ("gt2", [P, SEQ], F32),
            ("gp", [P, 2, 2, SEQ], F32), ("gpT", [P, 2, 2, SEQ], F32),
            ("sc", [P, TT, GHEADS, N_PAD], F32), ("pc", [P, TT, GHEADS, N_PAD], F32),
            ("pcT", [P, TT, P], F32), ("oc", [P, TT, GHEADS, HEAD], F32),
            ("og", [P, TT, P], F32), ("opair", [P, TT, P], F32))
        Qa, Qx = [Qa0, Qa1], [Qx0, Qx1]
        PS = [ctx.enter_context(nc.psum_tensor(f"bank{i}", [P, 512], F32)) for i in range(8)]
        A, B = PS[:4], PS[4:]
        names = """
        x_in consts_in gain_in gpost_in conv_in lamv_in pos_in sub_in
        w_in0 w_in1 w_hi_done w_lo_done units_done tile_done
        consts_ready ang_ready rope_in rope_tab lam_sum lam_exp lam_ready start_done
        std_done xn_done xT_done nhi_done nlo_done x_updated
        y0_done ystd_done v_done
        rope_done scores_done negmax_done probs_done mix_done mixT_done pT_done pv_done
        oraw_done ovar_done orinv_done onrm_done oT_done oThi_done oTlo_done
        aff_done gateconv_done conv_done gelu_done h_done hhi_done hlo_done
        ple_in pehi_done pelo_done sig_done xhalf_done
        cmpw_in zb_done hid_done gelc_done kv_done kvc_done gates_done pad_ready cm_in
        groupkv_done gqx_done vT_done vTt_done vg_done
        csc_done cexp_in cexp_done cp_done cpT_done cpTc_done coc_done oc_done
        gscores_done gnegmax_done gprobs_done gT_done gpTa_done gpTv_done gpv_done
        oread_done opair_done goT_done goThi_done goTlo_done
        out_done chain_act chain_dve chain_pool
        """.split()
        S = {n: ctx.enter_context(nc.semaphore(n)) for n in names}
        block = ctx.enter_context(nc.Block())

        def tok(t):
            return slice(t * P, (t + 1) * P)

        @block.sync
        def _(sp):
            def load(u, slot, turn_):
                sp.dma_start(w_raw[slot][:, :], w_in[u]).then_inc(S[f"w_in{slot}"], 16)

            for t in range(TT):
                sp.dma_start(x[:, t, :], x_in[:, t, :]).then_inc(S["x_in"], 16)
            sp.dma_start(w_raw[0][:, :], w_in[0, :, :]).then_inc(S["w_in0"], 16)
            sp.dma_start(w_raw[1][:, :], w_in[1, :, :]).then_inc(S["w_in1"], 16)
            with sp.Fori(1, UNITS // RAW) as i:
                for r in range(RAW):
                    sp.wait_ge(S["w_lo_done"], i * RAW + (r + 1 - RAW))
                    sp.dma_start(w_raw[r][:, :], w_in[bass.ds(i * RAW + r, 1), :, :].rearrange("a p n -> (a p) n"))\
                        .then_inc(S[f"w_in{r}"], 16)
            for u in range(UNITS // RAW * RAW, UNITS):
                sp.wait_ge(S["w_lo_done"], u + 1 - RAW)
                sp.dma_start(w_raw[u % RAW][:, :], w_in[u, :, :]).then_inc(S[f"w_in{u % RAW}"], 16)
            for t in range(TT):
                sp.wait_ge(S["x_updated"], 4 * (3 * LAYERS - 1) + t + 1)
                sp.dma_start(out[:, t, :], x[:, t, :]).then_inc(S["out_done"], 16)
            sp.wait_ge(S["out_done"], 16 * TT)

        @block.gpsimd
        def _(pool):
            def low(k, slot, u1):
                pool.wait_ge(S["w_hi_done"], u1)
                pool.tensor_tensor(w_lo[slot][:, :], w_raw[k % RAW][:, :], w_hi[slot][:, :].bitcast(F32),
                                   ALU.subtract).then_inc(S["w_lo_done"], 1)

            with pool.Fori(0, UNITS // RING) as i:
                for k in range(RING):
                    low(k, k, i * RING + (k + 1))
            for u in range(UNITS // RING * RING, UNITS):
                low(u, u % RING, u + 1)

        @block.scalar
        def _(act):
            chain = Chain(act, S["chain_act"])
            link = chain.link

            def signal(ins, name, value):
                ins.then_inc(S[name], 1)
                act.wait_ge(S[name], value)

            def w_high(u, i=0, per=0):
                if u >= UNITS:
                    return
                if u >= RING:
                    act.wait_ge(S["units_done"], u + 1 - RING + per * i)
                act.wait_ge(S[f"w_in{u % RAW}"], 16 * (u // RAW + 1) + 16 * (per // RAW) * i)
                act.activation(w_hi[u % RING][:, :], w_raw[u % RAW][:, :], ACT.Copy).then_inc(S["w_hi_done"], 1)

            def stats(q, t):
                if q == 0:
                    act.wait_ge(S["x_in"], 16 * TT)
                else:
                    act.wait_ge(S["x_updated"], 4 * (q - 1) + t + 1)
                link(act.activation(junk[:, :], x[:, t, :], ACT.Square, accum_out=ss[:, t:t + 1]))
                signal(act.activation(std[:, t:t + 1], ss[:, t:t + 1], ACT.Sqrt, bias=eps[:, :], scale=1.0 / D),
                       "std_done", 4 * q + t + 1)

            def nT_high(q, t):
                for b in range(2):
                    act.wait_ge(S["xT_done"], 8 * q + 2 * t + b + 1)
                    signal(act.activation(nT_hi[:, 4 * b:4 * b + 4, tok(t)],
                                          B[b][:, :].rearrange("p (k n) -> p k n", k=4), ACT.Copy),
                           "nhi_done", 8 * q + 2 * t + b + 1)

            def gains(q, r):
                if q:
                    act.wait_ge(S["nlo_done"], 8 * q)
                act.dma_start(g_pre[:, :], gain_in[GAINS * (q // 3) + 2 * (q % 3), :, :]).then_inc(S["gain_in"], 16)
                if r is not None:
                    act.dma_start(g_post[:, :], gain_in[GAINS * (r // 2) + 1 + 2 * (r % 2), :, :])\
                        .then_inc(S["gpost_in"], 16)

            def output_norm(r, phase, name, n, q):
                U = PLAN[name]
                for k in range(n // 2):
                    w_high(U + k + RING)
                for t in range(TT):
                    act.wait_ge(S["y0_done"], 4 * r + t + 1)
                    link(act.activation(junk[:, 0:HALF], y0[:, t, :], ACT.Square, accum_out=yss[:, 0, t:t + 1]))
                    link(act.activation(yst[:, 0, t:t + 1], yss[:, 0, t:t + 1], ACT.Identity, bias=eps[:, :],
                                        scale=1.0 / D))
                for k in range(n // 2, n - 4):
                    w_high(U + k + RING)

                def y_std(t):
                    if t < TT - 1:
                        act.wait_ge(S["tile_done"], 3 * phase + t + 1)
                    else:
                        act.wait_ge(S["units_done"], U + n)
                    link(act.activation(junk[:, 0:HALF], A[t][:, :], ACT.Square, accum_out=yss[:, 1, t:t + 1]))
                    signal(act.activation(yst[:, 1, t:t + 1], yss[:, 1, t:t + 1], ACT.Sqrt,
                                          bias=yst[:, 0, t:t + 1], scale=1.0 / D), "ystd_done", 4 * r + t + 1)
                y_std(0)
                stats(q, 0)
                for t in range(1, TT):
                    y_std(t)
                    nT_high(q, t - 1)
                    stats(q, t)
                w_high(U + n)
                w_high(U + n + 1)
                nT_high(q, TT - 1)
                w_high(U + n + 2)
                w_high(U + n + 3)

            def mlp(layer, name):
                U = PLAN[name]

                def pair(i, p, peeled):
                    j = 2 * i + p
                    slot = (U + 2 * p) % RING
                    del slot
                    if not peeled:
                        act.wait_ge(S["hlo_done"], FT * layer + j - 1)

                    def affine(v, dst, bank):
                        act.wait_ge(S["units_done"], U + 2 * j + v + 1)
                        f = j + v * FT
                        signal(act.activation(dst, bank[:, :], ACT.Identity, bias=conv[:, bass.ds(4 * f + 3, 1)],
                                              scale=conv[:, bass.ds(4 * f + 2, 1)]),
                               "aff_done", 2 * FT * layer + 2 * j + v + 1)
                    affine(0, y0[:, p, :], A[2 * p])
                    w_high(U + RING + 2 * p, i, RING)
                    affine(1, y0[:, 2 + p, :], A[2 * p + 1])
                    act.wait_ge(S["gateconv_done"], FT * layer + j + 1)
                    signal(act.activation(y0[:, p, :], y0[:, p, :], ACT.Gelu_apprx_tanh), "gelu_done",
                           FT * layer + j + 1)
                    w_high(U + RING + 2 * p + 1, i, RING)
                    act.wait_ge(S["h_done"], FT * layer + j + 1)
                    signal(act.activation(hT_hi[:, bass.ds(j, 1), :].rearrange("p a n -> p (a n)"),
                                          y0[:, 2 + p, :], ACT.Copy), "hhi_done", FT * layer + j + 1)
                if layer == 0:
                    pass
                for p in range(2):
                    pair(0, p, True)
                with chain.loop(1, FT // 2, 0) as i:
                    for p in range(2):
                        pair(i, p, False)

            def embed(layer, q, phase):
                Ua, Up, Ub = (PLAN[f"gate{layer}a"], PLAN[f"ple{layer}"], PLAN[f"gate{layer}b"])
                act.wait_ge(S["units_done"], Ua)
                act.dma_start(pe_raw[:, :, :], pT_in[layer, :, :, :]).then_inc(S["ple_in"], 16)
                act.wait_ge(S["ple_in"], 16 * (layer + 1))
                signal(act.activation(pe_hi[:, :, :], pe_raw[:, :, :], ACT.Copy), "pehi_done", layer + 1)
                for k in range(4):
                    w_high(Ua + k + RING)

                def sigmoid(half, t, bank):
                    signal(act.activation(sg[:, t, :], bank[t][:, :], ACT.Sigmoid), "sig_done",
                           8 * layer + 4 * half + t + 1)
                for t in range(TT):
                    sigmoid(0, t, A)
                for k in range(2):
                    w_high(Up + k + RING)

                def second(t):
                    if t < TT - 1:
                        act.wait_ge(S["tile_done"], 3 * phase + t + 1)
                    else:
                        act.wait_ge(S["units_done"], Ub + 4)
                    act.wait_ge(S["xhalf_done"], 4 * layer + t + 1)
                    sigmoid(1, t, B)
                if layer == LAYERS - 1:
                    for t in range(TT):
                        second(t)
                    return
                second(0)
                stats(q, 0)
                second(1)
                stats(q, 1)
                second(2)
                nT_high(q, 0)
                stats(q, 2)
                second(3)
                nT_high(q, 1)
                stats(q, 3)
                w_high(Ub + 4)
                w_high(Ub + 5)
                nT_high(q, 2)
                w_high(Ub + 6)
                nT_high(q, 3)
                w_high(Ub + 7)

            act.dma_start(const[:, :], const_in).then_inc(S["consts_in"], 16)
            gains(0, 0)
            act.dma_start(pos_i[:, :], pos_in).then_inc(S["pos_in"], 16)
            act.dma_start(lam_v[:, :, :], lam_in).then_inc(S["lamv_in"], 16)
            act.dma_start(subg[:, :], subln_in).then_inc(S["sub_in"], 16)
            act.dma_start(conv[:, :], conv_in[0, :, :]).then_inc(S["conv_in"], 16)
            act.wait_ge(S["consts_ready"], 4)
            stats(0, 0)
            w_high(0)
            stats(0, 1)
            w_high(1)
            nT_high(0, 0)
            stats(0, 2)
            w_high(2)
            nT_high(0, 1)
            stats(0, 3)
            w_high(3)
            nT_high(0, 2)
            nT_high(0, 3)
            act.wait_ge(S["rope_in"], 1)
            signal(act.activation(sinT[:, :], red[:, :], ACT.Sin, scale=const[:, C_SIGN:C_SIGN + 1]), "rope_tab", 1)
            act.wait_ge(S["rope_in"], 2)
            signal(act.activation(cosT[:, :], turn[:, :], ACT.Sin), "rope_tab", 2)
            act.wait_ge(S["lam_sum"], 1)
            signal(act.activation(lam[:, 2:4], lam[:, 0:2], ACT.Exp), "lam_exp", 1)
            for u in range(8):
                w_high(PLAN["v"] + u + RING)

            def exps(h, qt):
                for c in range(2):
                    act.wait_ge(S["negmax_done"], 4 * h + qt + 1)
                    if not (isinstance(h, int) and h == 0 and qt < 2):
                        act.wait_ge(S["mix_done"], 4 * h + qt - 1)
                    n = (qt + 1) * P
                    signal(act.activation(pr[:, qt % 2, c, 0:n], B[2 * (qt % 2) + c][:, 0:n], ACT.Exp,
                                          bias=nm[:, qt, c:c + 1], scale=SCALE,
                                          accum_out=sums[:, par(h), qt, c:c + 1]),
                           "probs_done", 8 * h + 2 * qt + c + 1)

            parity = [0]

            def par(h):
                return parity[0]

            def p_turned(h, qt):
                act.wait_ge(S["mixT_done"], 4 * h + qt + 1)
                if not (isinstance(h, int) and h == 0 and qt < 2):
                    act.wait_ge(S["pv_done"], 4 * h + qt - 1)
                n = (qt + 1) * P
                signal(act.activation(pT[:, qt % 2, 0:n], A[2][:, 0:n], ACT.Copy), "pT_done", 4 * h + qt + 1)

            def o_rinv(h):
                act.wait_ge(S["ovar_done"], h + 1)
                link(act.activation(osum[:, 1, :], osum[:, 0, :], ACT.Ln))
                signal(act.activation(osum[:, 2, :], osum[:, 1, :], ACT.Exp, scale=-0.5), "orinv_done", h + 1)

            def oT_high(h):
                act.wait_ge(S["oT_done"], h + 1)
                signal(act.activation(oT0_hi[:, bass.ds(h, 1), :].rearrange("p a n -> p (a n)"), A[2][:, :],
                                      ACT.Identity, scale=subg[:, :]), "oThi_done", h + 1)

            def head(h, p, first=False, last=False, i=0, per=0, u=0):
                parity[0] = p
                exps(h, 0)
                exps(h, 1)
                p_turned(h, 0)
                if not first:
                    o_rinv(h - 1)
                exps(h, 2)
                if not first:
                    oT_high(h - 1)
                p_turned(h, 1)
                exps(h, 3)
                if not last:
                    w_high(u, i, per)
                p_turned(h, 2)
                if not last:
                    w_high(u + 1, i, per)
                p_turned(h, 3)

            UH = PLAN["qk"] + RING
            w_high(UH)
            w_high(UH + 1)
            act.wait_ge(S["lam_ready"], 1)
            head(0, 0, first=True, u=UH + 2)
            with chain.loop(0, (DIFF_HEADS - 2) // 2, 2) as i:
                for p in range(2):
                    head(2 * i + (p + 1), (p + 1) % 2, i=i, per=4, u=UH + 4 + 2 * p)
            head(DIFF_HEADS - 1, 1, last=True)
            o_rinv(DIFF_HEADS - 1)
            oT_high(DIFF_HEADS - 1)

            gains(1, None)
            output_norm(0, 0, "out0", 8, 1)
            gains(2, 1)
            mlp(0, "up0")
            output_norm(1, 1, "down0", FT, 2)
            gains(3, 2)
            act.dma_start(conv[:, :], conv_in[1, :, :]).then_inc(S["conv_in"], 16)
            embed(0, 3, 2)

            act.dma_start(w1[:, :, :], w1_in).then_inc(S["cmpw_in"], 16)
            act.dma_start(cpos[:, :], cpos_in).then_inc(S["cmpw_in"], 16)
            act.dma_start(w2[:, :, :], w2_in).then_inc(S["cmpw_in"], 16)
            gains(4, None)
            for k in range(GROUPS + 1):
                w_high(PLAN["cmp"] + RING + k)
            act.wait_ge(S["units_done"], PLAN["branch"] + 1)
            signal(act.activation(gates[:, :, :], B[2][:, 0:TT * 48].rearrange("p (t n) -> p t n", t=TT), ACT.Sigmoid),
                   "gates_done", 1)
            act.wait_ge(S["hid_done"], 2)
            act.wait_ge(S["pad_ready"], 1)
            for kv, dst in enumerate((hid_k, hid_v)):
                signal(act.activation(dst[:, :, 0:N_CMP], B[kv][:, 0:GROUPS * N_CMP].rearrange("p (g n) -> p g n", g=GROUPS),
                                      ACT.Gelu_apprx_tanh), "gelc_done", kv + 1)
            act.wait_ge(S["kv_done"], 2)
            link(act.activation(kcmp[:, :, :], B[3][0:HEAD, 0:P].rearrange("p (g n) -> p g n", g=GROUPS), ACT.Copy))
            for h in range(GHEADS):
                signal(act.activation(Vblk[32 * h:32 * h + 32, :, HEAD * h:HEAD * h + HEAD],
                                      B[3][0:N_PAD, P:P + GROUPS * HEAD].rearrange("p (g n) -> p g n", g=GROUPS),
                                      ACT.Copy), "kvc_done", h + 1)
            act.dma_start(cm[:, 0, :], const_in[:, C_CMP:C_ALL]).then_inc(S["cm_in"], 16)

            def group(g, first, i=0, u=0, per=0):
                def step(h, qt):
                    return 16 * g + 4 * h + qt

                def gexps(h, qt):
                    n = (qt + 1) * P
                    for c in range(2):
                        act.wait_ge(S["gnegmax_done"], step(h, qt) + 1)
                        if not (first and h == 0 and qt < 2):
                            act.wait_ge(S["gT_done"], 2 * step(h, qt) - 2)
                        signal(act.activation(gp[:, qt % 2, c, 0:n], B[2 * (qt % 2) + c][:, 0:n], ACT.Exp,
                                              bias=nm[:, qt, c:c + 1], scale=SCALE,
                                              accum_out=sums[:, h % 2, qt, c:c + 1]),
                               "gprobs_done", 2 * step(h, qt) + c + 1)

                def gp_turned(h, qt):
                    n = (qt + 1) * P
                    act.wait_ge(S["gT_done"], 2 * step(h, qt) + 1)
                    if not (first and h == 0 and qt < 2):
                        act.wait_ge(S["gpv_done"], step(h, qt) - 1)
                    signal(act.activation(gpT[:, qt % 2, 0, 0:n], A[2][:, 0:n], ACT.Copy), "gpTa_done",
                           step(h, qt) + 1)

                def goT_high(pair):
                    act.wait_ge(S["goT_done"], 2 * g + pair + 1)
                    signal(act.activation(oT1_hi[:, bass.ds(2 * g + pair, 1), :].rearrange("p a n -> p (a n)"),
                                          A[2][:, :], ACT.Copy), "goThi_done", 2 * g + pair + 1)

                for k in range(4):
                    w_high(u + k, i, per)
                for n in range(2):
                    act.wait_ge(S["groupkv_done"], 3 * g + 2 + n)
                    link(act.activation(Qx[n][0:HEAD, :], Qa[n][HEAD:P, :], ACT.Copy))
                    signal(act.activation(Qx[n][HEAD:P, :], Qa[n][0:HEAD, :], ACT.Copy), "gqx_done", 2 * g + n + 1)
                act.wait_ge(S["units_done"], PLAN["group"] + 4 * g + 4)
                signal(act.activation(vT[:, :], A[1][:, :], ACT.Copy), "vT_done", g + 1)
                act.wait_ge(S["vTt_done"], g + 1)
                signal(act.activation(Vg[:, :, :], B[0][:, :].rearrange("p (t n) -> p t n", t=TT), ACT.Copy),
                       "vg_done", g + 1)
                act.wait_ge(S["cexp_in"], g + 1)
                signal(act.activation(pc[:, :, :, :], sc[:, :, :, :], ACT.Exp, scale=SCALE), "cexp_done", g + 1)
                act.wait_ge(S["cpT_done"], g + 1)
                signal(act.activation(pcT[:, :, :], A[3][:, :].rearrange("p (t n) -> p t n", t=TT), ACT.Copy),
                       "cpTc_done", g + 1)
                seq = [(h, qt) for h in range(GHEADS) for qt in range(TT)]
                gexps(*seq[0])
                gexps(*seq[1])
                for n, (h, qt) in enumerate(seq):
                    gp_turned(h, qt)
                    if n + 2 < len(seq):
                        gexps(*seq[n + 2])
                    if (h, qt) == (2, 1):
                        goT_high(0)
                goT_high(1)

            UG = PLAN["group"] + RING
            group(0, True, u=UG)
            with chain.loop(1, GROUPS, 2) as g:
                group(g, False, i=g, u=UG, per=4)

            output_norm(2, 3, "out1", 8, 4)
            gains(5, 3)
            mlp(1, "up1")
            output_norm(3, 4, "down1", FT, 5)
            embed(1, None, 5)

        @block.vector
        def _(dve):
            chain = Chain(dve, S["chain_dve"])
            link = chain.link

            def signal(ins, name, value):
                ins.then_inc(S[name], 1)
                dve.wait_ge(S[name], value)

            def prepare(q, t):
                if t:
                    dve.wait_ge(S["xT_done"], 8 * q + 2 * t)
                else:
                    dve.wait_ge(S["gain_in"], 16 * (q + 1))
                dve.wait_ge(S["std_done"], 4 * q + t + 1)
                link(dve.reciprocal(rinv[:, t:t + 1], std[:, t:t + 1]))
                signal(dve.scalar_tensor_tensor(xn[:, :], x[:, t, :], rinv[:, t:t + 1], g_pre[:, :], ALU.mult,
                                                ALU.mult), "xn_done", 4 * q + t + 1)

            def nT_low(q, t):
                for b in range(2):
                    dve.wait_ge(S["nhi_done"], 8 * q + 2 * t + b + 1)
                    signal(dve.tensor_tensor(nT_lo[:, 4 * b:4 * b + 4, tok(t)],
                                             B[b][:, :].rearrange("p (k n) -> p k n", k=4),
                                             nT_hi[:, 4 * b:4 * b + 4, tok(t)].bitcast(F32), ALU.subtract),
                           "nlo_done", 8 * q + 2 * t + b + 1)

            def output_norm(r, phase, name, n, q):
                U = PLAN[name]
                dve.wait_ge(S["units_done"], U + n // 2)
                for t in range(TT):
                    signal(dve.tensor_copy(y0[:, t, :], B[t][:, :]), "y0_done", 4 * r + t + 1)
                dve.wait_ge(S["gpost_in"], 16 * (r + 1))

                def update(t):
                    if t:
                        dve.wait_ge(S["xT_done"], 8 * q + 2 * t)
                    dve.wait_ge(S["ystd_done"], 4 * r + t + 1)
                    link(dve.reciprocal(yst[:, 2, t:t + 1], yst[:, 1, t:t + 1]))
                    link(dve.scalar_tensor_tensor(xn[:, 0:HALF], y0[:, t, :], yst[:, 2, t:t + 1],
                                                  g_post[:, 0:HALF], ALU.mult, ALU.mult))
                    link(dve.scalar_tensor_tensor(xn[:, HALF:D], A[t][:, :], yst[:, 2, t:t + 1],
                                                  g_post[:, HALF:D], ALU.mult, ALU.mult))
                    signal(dve.tensor_tensor(x[:, t, :], x[:, t, :], xn[:, :], ALU.add), "x_updated",
                           4 * phase + t + 1)
                update(0)
                prepare(q, 0)
                for t in range(1, TT):
                    update(t)
                    nT_low(q, t - 1)
                    prepare(q, t)
                nT_low(q, TT - 1)

            def rope(bank, dst, name, value, rows=slice(0, P), tmp=None):
                s_, a_, b_ = tmp
                chain.step(dve.tensor_tensor(a_, bank[rows, :], cosT[rows, :], ALU.mult))
                link(dve.stream_shuffle(s_, bank[rows, :], [(n + 16) % 32 for n in range(32)]))
                link(dve.tensor_tensor(b_, s_, sinT[rows, :], ALU.mult))
                signal(dve.tensor_tensor(dst, a_, b_, ALU.add), name, value)

            def mlp(layer, name):
                U = PLAN[name]
                del U

                def pair(i, p):
                    j = 2 * i + p

                    def taps(v, dst, bank):
                        f = j + v * FT
                        dve.wait_ge(S["aff_done"], 2 * FT * layer + 2 * j + v + 1)
                        link(dve.scalar_tensor_tensor(dst[:, 1:SEQ], bank[:, 0:SEQ - 1], conv[:, bass.ds(4 * f + 1, 1)],
                                                      dst[:, 1:SEQ], ALU.mult, ALU.add))
                        last = dve.scalar_tensor_tensor(dst[:, 2:SEQ], bank[:, 0:SEQ - 2], conv[:, bass.ds(4 * f, 1)],
                                                        dst[:, 2:SEQ], ALU.mult, ALU.add)
                        signal(last, ("gateconv_done", "conv_done")[v], FT * layer + j + 1)
                    taps(0, y0[:, p, :], A[2 * p])
                    taps(1, y0[:, 2 + p, :], A[2 * p + 1])
                    dve.wait_ge(S["gelu_done"], FT * layer + j + 1)
                    signal(dve.tensor_tensor(y0[:, 2 + p, :], y0[:, 2 + p, :], y0[:, p, :], ALU.mult), "h_done",
                           FT * layer + j + 1)
                    dve.wait_ge(S["hhi_done"], FT * layer + j + 1)
                    signal(dve.tensor_tensor(hT_lo[:, bass.ds(j, 1), :].rearrange("p a n -> p (a n)"), y0[:, 2 + p, :],
                                             hT_hi[:, bass.ds(j, 1), :].rearrange("p a n -> p (a n)").bitcast(F32),
                                             ALU.subtract), "hlo_done", FT * layer + j + 1)
                dve.wait_ge(S["conv_in"], 16 * (layer + 1))
                with chain.loop(0, FT // 2, 4) as i:
                    for p in range(2):
                        pair(i, p)

            def embed(layer, q, phase):
                Up = PLAN[f"ple{layer}"]
                dve.wait_ge(S["pehi_done"], layer + 1)
                signal(dve.tensor_tensor(pe_lo[:, :, :], pe_raw[:, :, :], pe_hi[:, :, :].bitcast(F32), ALU.subtract),
                       "pelo_done", layer + 1)
                dve.wait_ge(S["units_done"], Up + 1)
                for t in range(TT):
                    dve.wait_ge(S["sig_done"], 8 * layer + t + 1)
                    link(dve.tensor_tensor(sg[:, t, :], sg[:, t, :], B[t][:, :], ALU.mult))
                    signal(dve.tensor_tensor(x[:, t, 0:HALF], x[:, t, 0:HALF], sg[:, t, :], ALU.add), "xhalf_done",
                           4 * layer + t + 1)
                dve.wait_ge(S["units_done"], Up + 2)

                def second(t):
                    dve.wait_ge(S["sig_done"], 8 * layer + 4 + t + 1)
                    link(dve.tensor_tensor(sg[:, t, :], sg[:, t, :], A[t][:, :], ALU.mult))
                    signal(dve.tensor_tensor(x[:, t, HALF:D], x[:, t, HALF:D], sg[:, t, :], ALU.add), "x_updated",
                           4 * phase + t + 1)
                if layer == LAYERS - 1:
                    for t in range(TT):
                        second(t)
                    return
                second(0)
                prepare(q, 0)
                second(1)
                prepare(q, 1)
                nT_low(q, 0)
                second(2)
                prepare(q, 2)
                nT_low(q, 1)
                second(3)
                prepare(q, 3)
                nT_low(q, 2)
                nT_low(q, 3)

            dve.memset(eps[:, :], EPS).then_inc(S["consts_ready"], 1)
            dve.wait_ge(S["consts_in"], 16)
            dve.tensor_copy(ident[:, :], const[:, C_IDENT:C_IDENT + P]).then_inc(S["consts_ready"], 1)
            dve.tensor_copy(ident_b[:, :], const[:, C_IDENT:C_IDENT + P]).then_inc(S["consts_ready"], 1)
            dve.tensor_copy(causal_b[:, :], const[:, C_CAUSAL:C_CAUSAL + P]).then_inc(S["consts_ready"], 1)
            dve.wait_ge(S["consts_ready"], 4)
            prepare(0, 0)
            prepare(0, 1)
            nT_low(0, 0)
            prepare(0, 2)
            nT_low(0, 1)
            prepare(0, 3)
            nT_low(0, 2)
            nT_low(0, 3)
            dve.wait_ge(S["pos_in"], 16)
            link(dve.tensor_copy(ang[:, :], pos_i[:, :]))
            link(dve.tensor_scalar(ang[:, :], ang[:, :], const[:, C_INV:C_INV + 1], None, ALU.mult))
            for n, (r, shift) in enumerate(((red, 0.0), (turn, 0.25))):
                k = cosT if n == 0 else ang
                k = cosT
                link(dve.tensor_scalar(k[:, :], ang[:, :], 1.0 / TWO_PI, shift, ALU.mult, ALU.add))
                link(dve.tensor_scalar(k[:, :], k[:, :], ROUND, None, ALU.add))
                link(dve.tensor_scalar(k[:, :], k[:, :], ROUND, None, ALU.subtract))
                link(dve.scalar_tensor_tensor(r[:, :], k[:, :], -PI_1, ang[:, :], ALU.mult, ALU.add))
                link(dve.scalar_tensor_tensor(r[:, :], k[:, :], -PI_2, r[:, :], ALU.mult, ALU.add))
                link(dve.scalar_tensor_tensor(r[:, :], k[:, :], -PI_3, r[:, :], ALU.mult, ALU.add))
                link(dve.tensor_scalar(r[:, :], r[:, :], shift * TWO_PI, None, ALU.add))
                signal(dve.tensor_scalar(r[:, :], r[:, :], PI_MAX, -PI_MAX, ALU.min, ALU.max), "rope_in", n + 1)
            dve.wait_ge(S["lamv_in"], 16)
            dve.wait_ge(S["sub_in"], 16)
            for n in range(2):
                link(dve.tensor_tensor(lam_p[:, n, :], lam_v[:, 2 * n, :], lam_v[:, 2 * n + 1, :], ALU.mult))
            signal(dve.tensor_reduce(lam[:, 0:2], lam_p[:, :, :], AX.X, ALU.add), "lam_sum", 1)
            dve.wait_ge(S["lam_exp"], 1)
            link(dve.tensor_tensor(neg_lam[:, :], lam[:, 3:4], lam[:, 2:3], ALU.subtract))
            link(dve.tensor_scalar(neg_lam[:, :], neg_lam[:, :], -LAMBDA_INIT, None, ALU.add))
            signal(dve.tensor_scalar(subg[:, :], subg[:, :], 1.0 - LAMBDA_INIT, None, ALU.mult), "lam_ready", 1)
            dve.wait_ge(S["rope_tab"], 2)

            for half in range(2):
                dve.wait_ge(S["units_done"], PLAN["v"] + 4 * (half + 1))
                for t in range(TT):
                    signal(dve.tensor_copy(V[:, t, half * HALF:(half + 1) * HALF], (A, B)[half][t][:, :]), "v_done",
                           4 * half + t + 1)

            def maxima(h, qt, scores, negmax, step):
                n = (qt + 1) * P
                for c in range(2):
                    dve.wait_ge(S[scores], 2 * step + c + 1)
                    link(dve.tensor_reduce(mx[:, qt, c:c + 1], B[2 * (qt % 2) + c][:, 0:n], AX.X, ALU.max))
                signal(dve.tensor_scalar(nm[:, qt, :], mx[:, qt, :], -SCALE, None, ALU.mult), negmax, step + 1)

            def mix(h, p, qt):
                n = (qt + 1) * P
                dve.wait_ge(S["probs_done"], 8 * h + 2 * qt + 2)
                link(dve.tensor_scalar(st1[:, 0:1], sums[:, p, qt, 1:2], 1e-30, None, ALU.max))
                link(dve.reciprocal(st1[:, 1:2], st1[:, 0:1]))
                link(dve.scalar_tensor_tensor(st1[:, 2:3], sums[:, p, qt, 0:1], neg_lam[:, :], st1[:, 1:2],
                                              ALU.mult, ALU.mult))
                if not (isinstance(h, int) and h == 0 and qt < 2):
                    dve.wait_ge(S["mixT_done"], 4 * h + qt - 1)
                signal(dve.scalar_tensor_tensor(amix[:, qt % 2, 0:n], pr[:, qt % 2, 1, 0:n], st1[:, 2:3],
                                                pr[:, qt % 2, 0, 0:n], ALU.mult, ALU.add),
                       "mix_done", 4 * h + qt + 1)

            def o_variance(h, p):
                dve.wait_ge(S["pv_done"], 4 * h + 4)
                signal(dve.tensor_copy(o_raw[:, :, :], A[3][:, :].rearrange("p (t n) -> p t n", t=TT)),
                       "oraw_done", h + 1)
                link(dve.tensor_tensor(o_sq[:, :, :], o_raw[:, :, :], o_raw[:, :, :], ALU.mult))
                link(dve.tensor_reduce(osum[:, 0, :], o_sq[:, :, :], AX.X, ALU.add))
                link(dve.tensor_scalar(st2[:, 0, :, 0], sums[:, p, :, 0], 1e-30, None, ALU.max))
                link(dve.reciprocal(osum[:, 3, :], st2[:, 0, :, 0]))
                link(dve.tensor_tensor(osum[:, 0, :], osum[:, 0, :], osum[:, 3, :], ALU.mult))
                link(dve.tensor_tensor(osum[:, 0, :], osum[:, 0, :], osum[:, 3, :], ALU.mult))
                signal(dve.tensor_scalar(osum[:, 0, :], osum[:, 0, :], 1.0 / P, EPS, ALU.mult, ALU.add),
                       "ovar_done", h + 1)

            def o_normed(h):
                dve.wait_ge(S["orinv_done"], h + 1)
                link(dve.tensor_tensor(osum[:, 3, :], osum[:, 3, :], osum[:, 2, :], ALU.mult))
                signal(dve.tensor_tensor(o_nrm[:, :, :], o_raw[:, :, :],
                                         osum[:, 3, :].unsqueeze(2).broadcast_to([P, TT, P]), ALU.mult),
                       "onrm_done", h + 1)

            def oT_low(h):
                dve.wait_ge(S["oThi_done"], h + 1)
                signal(dve.scalar_tensor_tensor(
                    oT0_lo[:, bass.ds(h, 1), :].rearrange("p a n -> p (a n)"), A[2][:, :], subg[:, :],
                    oT0_hi[:, bass.ds(h, 1), :].rearrange("p a n -> p (a n)").bitcast(F32), ALU.mult, ALU.subtract),
                    "oTlo_done", h + 1)

            def head_rope(h, p, k):
                dve.wait_ge(S["units_done"], PLAN["qk"] + 2 * h + k + 1)
                rope(A[k], (qT, kT)[k][p][:, :], "rope_done", 2 * h + k + 1, tmp=(sh[:, :], t1[:, :], t2[:, :]))

            def head(h, p, first=False, last=False):
                maxima(h, 0, "scores_done", "negmax_done", 4 * h)
                maxima(h, 1, "scores_done", "negmax_done", 4 * h + 1)
                mix(h, p, 0)
                if not first:
                    o_variance(h - 1, 1 - p)
                maxima(h, 2, "scores_done", "negmax_done", 4 * h + 2)
                if not first:
                    o_normed(h - 1)
                mix(h, p, 1)
                if not first:
                    oT_low(h - 1)
                maxima(h, 3, "scores_done", "negmax_done", 4 * h + 3)
                mix(h, p, 2)
                if not last:
                    head_rope(h + 1, 1 - p, 0)
                mix(h, p, 3)
                if not last:
                    head_rope(h + 1, 1 - p, 1)

            head_rope(0, 0, 0)
            head_rope(0, 0, 1)
            head(0, 0, first=True)
            with chain.loop(0, (DIFF_HEADS - 2) // 2, 2 * (8 + 12 + 6 + 6 + 1)) as i:
                for p in range(2):
                    head(2 * i + (p + 1), (p + 1) % 2)
            head(DIFF_HEADS - 1, 1, last=True)
            o_variance(DIFF_HEADS - 1, 1)
            o_normed(DIFF_HEADS - 1)
            oT_low(DIFF_HEADS - 1)

            output_norm(0, 0, "out0", 8, 1)
            mlp(0, "up0")
            output_norm(1, 1, "down0", FT, 2)
            embed(0, 3, 2)

            dve.wait_ge(S["cmpw_in"], 48)
            link(dve.memset(hid_k[:, :, N_CMP:N_PAD], 0.0))
            link(dve.memset(hid_v[:, :, N_CMP:N_PAD], 0.0))
            signal(dve.memset(Vblk[:, :, :], 0.0), "pad_ready", 1)
            for g in range(GROUPS):
                dve.wait_ge(S["units_done"], PLAN["cmp"] + g + 1)
                keys, values = slice(0, HEAD), slice(HEAD, P)
                link(dve.stream_shuffle(ksh[:, :], A[g][keys, :], [(n + 16) % 32 for n in range(32)]))
                link(dve.tensor_tensor(kt1[:, :], A[g][keys, :], cosT[keys, :], ALU.mult))
                link(dve.tensor_tensor(kt2[:, :], ksh[:, :], sinT[keys, :], ALU.mult))
                link(dve.tensor_tensor(kr[:, :], kt1[:, :], kt2[:, :], ALU.add))
                for rows, src in ((keys, kr), (values, A[g])):
                    for m in range(CMP_LEN // CMP_STRIDE):
                        win = (src[:, :] if rows is keys else src[rows, :]).rearrange("p (n l) -> p n l", l=CMP_STRIDE)
                        ls = slice(m * CMP_STRIDE, (m + 1) * CMP_STRIDE)
                        signal(dve.tensor_tensor(
                            zb[rows, g, :, ls], win[:, m:m + N_CMP, :],
                            cpos[rows, ls].unsqueeze(1).broadcast_to([HEAD, N_CMP, CMP_STRIDE]), ALU.add),
                            "zb_done", 4 * g + 2 * (rows is values) + m + 1)
            dve.wait_ge(S["cm_in"], 16)
            link(dve.tensor_scalar(cm[:, 1, :], cm[:, 0, :], -MASKED, MASKED, ALU.mult, ALU.add))

            def group(g, first):
                def step(h, qt):
                    return 16 * g + 4 * h + qt

                U = PLAN["group"]
                tmp = (gsh[:, :], gt1[:, :], gt2[:, :])
                for n, dst in enumerate((KK, Qa[0], Qa[1])):
                    dve.wait_ge(S["units_done"], U + 4 * g + (n + 1))
                    rope((A[0], A[2], A[3])[n], dst[:, :], "groupkv_done", 3 * g + n + 1, tmp=tmp)
                dve.wait_ge(S["csc_done"], g + 1)
                flat = "p t h n -> p (t h) n"

                def over_heads(mask):
                    return mask.rearrange("p (t n) -> p t n", t=TT)
                s4 = B[2][:, :].rearrange("p (t h n) -> p t h n", t=TT, h=GHEADS)
                for h in range(GHEADS):
                    link(dve.tensor_tensor(sc[:, :, h, :], s4[:, :, h, :], over_heads(cm[:, 1, :]), ALU.add))
                link(dve.tensor_reduce(cst[:, 0, :], sc[:, :, :, :].rearrange(flat), AX.X, ALU.max))
                signal(dve.tensor_tensor(sc[:, :, :, :].rearrange(flat), sc[:, :, :, :].rearrange(flat),
                                         cst[:, 0, :].unsqueeze(2).broadcast_to([P, TT * GHEADS, N_PAD]), ALU.subtract),
                       "cexp_in", g + 1)
                dve.wait_ge(S["cexp_done"], g + 1)
                for h in range(GHEADS):
                    link(dve.tensor_tensor(pc[:, :, h, :], pc[:, :, h, :], over_heads(cm[:, 0, :]), ALU.mult))
                signal(dve.tensor_reduce(cst[:, 1, :], pc[:, :, :, :].rearrange(flat), AX.X, ALU.add), "cp_done", g + 1)
                link(dve.tensor_scalar(cst[:, 1, :], cst[:, 1, :], 1e-30, None, ALU.max))
                link(dve.reciprocal(cst[:, 2, :], cst[:, 1, :]))
                for t in range(TT):
                    link(dve.tensor_tensor(cst[:, 2, t * GHEADS:(t + 1) * GHEADS], cst[:, 2, t * GHEADS:(t + 1) * GHEADS],
                                           gates[:, t, bass.ds(12 * g, 12)].rearrange("p (h b) -> p h b", b=3)[:, :, 0],
                                           ALU.mult))
                dve.wait_ge(S["coc_done"], g + 1)
                for m, bank in enumerate((A[0], A[3])):
                    src = bank[:, :].rearrange("p (th n) -> p th n", n=HEAD)
                    dst = oc[:, 2 * m:2 * m + 2, :, :].rearrange("p t h n -> p (t h) n")
                    signal(dve.tensor_tensor(dst, src, cst[:, 2, 8 * m:8 * m + 8].unsqueeze(2).broadcast_to([P, 8, HEAD]),
                                             ALU.mult), "oc_done", 2 * g + m + 1)

                def gp_turned(h, qt):
                    n = (qt + 1) * P
                    dve.wait_ge(S["gT_done"], 2 * step(h, qt) + 2)
                    signal(dve.tensor_copy(gpT[:, qt % 2, 1, 0:n], A[3][:, 0:n]), "gpTv_done", step(h, qt) + 1)

                def post(h):
                    dve.wait_ge(S["gpv_done"], step(h, TT - 1) + 1)
                    link(dve.tensor_scalar(st2[:, 0, :, :], sums[:, h % 2, :, :], 1e-30, None, ALU.max))
                    link(dve.reciprocal(st2[:, 1, :, :], st2[:, 0, :, :]))
                    link(dve.tensor_tensor(st2[:, 0, :, :], st2[:, 1, :, :], gates[:, :, bass.ds(12 * g + (3 * h + 1), 2)],
                                           ALU.mult))
                    signal(dve.tensor_tensor(og[:, :, :].rearrange("p t (b n) -> p (t b) n", b=2),
                                             A[h % 2][:, :].rearrange("p (tb n) -> p tb n", n=HEAD),
                                             st2[:, 0, :, :].rearrange("p t b -> p (t b)").unsqueeze(2)
                                             .broadcast_to([P, 2 * TT, HEAD]), ALU.mult), "oread_done", 4 * g + h + 1)
                    link(dve.tensor_tensor(og[:, :, 0:HEAD], og[:, :, 0:HEAD], og[:, :, HEAD:P], ALU.add))
                    if h == 2:
                        dve.wait_ge(S["goT_done"], 2 * g + 1)
                    signal(dve.tensor_tensor(opair[:, :, HEAD * (h % 2):HEAD * (h % 2) + HEAD], og[:, :, 0:HEAD],
                                             oc[:, :, h, :], ALU.add), "opair_done", 4 * g + h + 1)

                def goT_low(pair):
                    dve.wait_ge(S["goThi_done"], 2 * g + pair + 1)
                    signal(dve.tensor_tensor(
                        oT1_lo[:, bass.ds(2 * g + pair, 1), :].rearrange("p a n -> p (a n)"), A[2][:, :],
                        oT1_hi[:, bass.ds(2 * g + pair, 1), :].rearrange("p a n -> p (a n)").bitcast(F32), ALU.subtract),
                        "goTlo_done", 2 * g + pair + 1)

                seq = [(h, qt) for h in range(GHEADS) for qt in range(TT)]
                maxima(None, seq[0][1], "gscores_done", "gnegmax_done", step(*seq[0]))
                maxima(None, seq[1][1], "gscores_done", "gnegmax_done", step(*seq[1]))
                for n, (h, qt) in enumerate(seq):
                    gp_turned(h, qt)
                    if n + 2 < len(seq):
                        maxima(None, seq[n + 2][1], "gscores_done", "gnegmax_done", step(*seq[n + 2]))
                    if h and qt == 0:
                        post(h - 1)
                    if (h, qt) == (2, 1):
                        goT_low(0)
                post(GHEADS - 1)
                goT_low(1)

            group(0, True)
            with chain.loop(1, GROUPS, 3 * 3 + 5 + 4 + 2 + TT + 16 * 2 + 4 * 4) as g:
                group(g, False)

            output_norm(2, 3, "out1", 8, 4)
            mlp(1, "up1")
            output_norm(3, 4, "down1", FT, 5)
            embed(1, None, 5)

        @block.tensor
        def _(pe):
            def weights(u, u0=None):
                pe.wait_ge(S["w_lo_done"], u)

            def transpose(dst, src):
                return pe.matmul(dst, src, ident[:, :], start=True, stop=True, is_transpose=True)

            def transposes(q, t):
                pe.wait_ge(S["xn_done"], 4 * q + t + 1)
                if t:
                    pe.wait_ge(S["nlo_done"], 8 * q + 2 * t)
                for b in range(2):
                    for k in range(4):
                        m = transpose(B[b][:, k * P:(k + 1) * P], xn[:, (4 * b + k) * P:(4 * b + k + 1) * P])
                    m.then_inc(S["xT_done"], 1)

            def features(bank, slot, rhs_hi, rhs_lo, part=None, n_k=KT):
                steps = [(k, pas) for k in range(n_k) for pas in range(3)]
                if part is not None:
                    steps = steps[8 * part:8 * part + 8]
                for k, pas in steps:
                    w = (w_hi, w_hi, w_lo)[pas][slot]
                    r = (rhs_hi, rhs_lo, rhs_hi)[pas]
                    m = pe.matmul(bank[:, :], w[:, k * P:(k + 1) * P], r[:, k, :], start=(k, pas) == (0, 0),
                                  stop=(k, pas) == (n_k - 1, 2))
                return m

            def tokens(bank, slot, c, lhs_hi, lhs_lo, kk, t, n_k):
                for pas in range(3):
                    w = (w_hi, w_lo, w_hi)[pas][slot]
                    a = (lhs_hi, lhs_hi, lhs_lo)[pas]
                    m = pe.matmul(bank[:, :], a[:, kk, tok(t)], w[:, c * HALF:(c + 1) * HALF],
                                  start=(kk, pas) == (0, 0), stop=(kk, pas) == (n_k - 1, 2))
                return m

            def by_unit(U, units, banks, lhs_hi, lhs_lo, n_k, before=None):
                for n in units:
                    weights(U + n + 1)
                    if before:
                        before(n)
                    for c in range(2):
                        kk = 2 * n + c - (n_k if 2 * n >= n_k else 0)
                        for t in range(TT):
                            m = tokens(banks[t], (U + n) % RING, c, lhs_hi, lhs_lo, kk, t, n_k)
                    m.then_inc(S["units_done"], 1)

            def by_tile(U, units, banks, lhs_hi, lhs_lo, n_k, between, free=None):
                weights(U + units[-1] + 1)
                for t in range(TT):
                    if free:
                        free(t)
                    for n in units:
                        for c in range(2):
                            kk = 2 * n + c - (n_k if 2 * n >= n_k else 0)
                            m = tokens(banks[t], (U + n) % RING, c, lhs_hi, lhs_lo, kk, t, n_k)
                        if t == TT - 1:
                            m.then_inc(S["units_done"], 1)
                    if t < TT - 1:
                        m.then_inc(S["tile_done"], 1)
                    between(t)

            def output(U, n, q, lhs_hi, lhs_lo, n_k, r, before=None):
                by_unit(U, range(n // 2), B, lhs_hi, lhs_lo, n_k, before)
                by_unit(U, range(n // 2, n - 4), A, lhs_hi, lhs_lo, n_k)

                def between(t):
                    if t == 1:
                        pe.wait_ge(S["y0_done"], 4 * r + 4)
                    if t:
                        transposes(q, t - 1)
                by_tile(U, range(n - 4, n), A, lhs_hi, lhs_lo, n_k, between)
                transposes(q, TT - 1)

            def mlp(layer, name, q):
                U = PLAN[name]
                pe.wait_ge(S["nlo_done"], 8 * q + 8)

                def pair(i, p, peeled):
                    if not peeled:
                        pe.wait_ge(S["conv_done"], FT * layer + 2 * i + (p - 1))
                    for v in range(2):
                        weights(U + (2 * p + v + 1) + 4 * i)
                        features(A[2 * p + v], (U + 2 * p + v) % RING, nT_hi, nT_lo).then_inc(S["units_done"], 1)
                for p in range(2):
                    pair(0, p, True)
                with pe.Fori(1, FT // 2) as i:
                    for p in range(2):
                        pair(i, p, False)

            def down(layer, name, q, r):
                def hidden(n):
                    pe.wait_ge(S["hlo_done"], FT * layer + min(2 * n + 2, FT))
                output(PLAN[name], FT, q, hT_hi, hT_lo, FT, r, hidden)

            def embed(layer, q, after_q):
                Ua, Up, Ub = PLAN[f"gate{layer}a"], PLAN[f"ple{layer}"], PLAN[f"gate{layer}b"]
                pe.wait_ge(S["nlo_done"], 8 * after_q + 8)
                by_unit(Ua, range(4), A, nT_hi, nT_lo, KT)
                pe.wait_ge(S["pelo_done"], layer + 1)
                for half, banks in enumerate((B, A)):
                    weights(Up + half + 1)
                    for t in range(TT):
                        if half:
                            pe.wait_ge(S["sig_done"], 8 * layer + t + 1)
                        for c in range(2):
                            m = tokens(banks[t], (Up + half) % RING, c, pe_hi, pe_lo, c, t, 2)
                    m.then_inc(S["units_done"], 1)

                def free(t):
                    pe.wait_ge(S["xhalf_done"], 4 * layer + t + 1)

                def between(t):
                    if q is None:
                        return
                    if t == 2:
                        pe.wait_ge(S["sig_done"], 8 * layer + 6)
                        transposes(q, 0)
                    if t == 3:
                        for n in range(1, TT):
                            transposes(q, n)
                by_tile(Ub - 4, range(4, 8), B, nT_hi, nT_lo, KT, between, free)

            pe.wait_ge(S["consts_ready"], 4)
            for t in range(TT):
                transposes(0, t)
            pe.wait_ge(S["nlo_done"], 8)
            by_unit(PLAN["v"], range(4), A, nT_hi, nT_lo, KT)
            by_unit(PLAN["v"], range(4, 8), B, nT_hi, nT_lo, KT)

            def project(h, part, p, U0):
                k = part // 3
                if part % 3 == 0:
                    pe.wait_ge(S["w_lo_done"], PLAN["qk"] + 2 * h + k + 1)
                    if not (isinstance(h, int) and h == 0):
                        pe.wait_ge(S["rope_done"], 2 * h + k - 1)
                m = features(A[k], (PLAN["qk"] + 2 * p + k) % RING, nT_hi, nT_lo, part % 3)
                if part % 3 == 2:
                    m.then_inc(S["units_done"], 1)

            def scores(h, p, qt):
                n = (qt + 1) * P
                if not (isinstance(h, int) and h == 0 and qt < 2):
                    pe.wait_ge(S["probs_done"], 8 * h + 2 * qt - 2)
                for c in range(2):
                    rows = slice(HEAD * c, HEAD * c + HEAD)
                    pe.matmul(B[2 * (qt % 2) + c][:, 0:n], qT[p][rows, tok(qt)], kT[p][rows, 0:n], start=True,
                              stop=False)
                for c in range(2):
                    pe.matmul(B[2 * (qt % 2) + c][:, n - P:n], ident_b[:, :], causal_b[:, :], start=False,
                              stop=True).then_inc(S["scores_done"], 1)

            def turn_mix(h, qt):
                pe.wait_ge(S["mix_done"], 4 * h + qt + 1)
                if not (isinstance(h, int) and h == 0 and qt == 0):
                    pe.wait_ge(S["pT_done"], 4 * h + qt)
                for kb in range(qt + 1):
                    m = transpose(A[2][:, kb * P:(kb + 1) * P], amix[:, qt % 2, kb * P:(kb + 1) * P])
                m.then_inc(S["mixT_done"], 1)

            def values(h, qt):
                pe.wait_ge(S["pT_done"], 4 * h + qt + 1)
                if qt == 0 and not (isinstance(h, int) and h == 0):
                    pe.wait_ge(S["oraw_done"], h)
                for kb in range(qt + 1):
                    m = pe.matmul(A[3][:, tok(qt)], pT[:, qt % 2, kb * P:(kb + 1) * P],
                                  V[:, kb, bass.ds(h * P, P)], start=kb == 0, stop=kb == qt)
                m.then_inc(S["pv_done"], 1)

            def turn_o(h):
                pe.wait_ge(S["onrm_done"], h + 1)
                for t in range(TT):
                    m = transpose(A[2][:, tok(t)], o_nrm[:, t, :])
                m.then_inc(S["oT_done"], 1)

            def head(h, p, first=False, last=False):
                def proj(*parts):
                    if not last:
                        for part in parts:
                            project(h + 1, part, 1 - p, None)
                pe.wait_ge(S["rope_done"], 2 * h + 2)
                scores(h, p, 0)
                scores(h, p, 1)
                proj(0)
                turn_mix(h, 0)
                scores(h, p, 2)
                proj(1)
                values(h, 0)
                if not first:
                    turn_o(h - 1)
                    pe.wait_ge(S["oTlo_done"], h)
                turn_mix(h, 1)
                scores(h, p, 3)
                proj(2, 3)
                values(h, 1)
                turn_mix(h, 2)
                proj(4, 5)
                values(h, 2)
                turn_mix(h, 3)
                values(h, 3)

            pe.wait_ge(S["v_done"], 4)
            for part in range(6):
                project(0, part, 0, None)
            pe.wait_ge(S["v_done"], 8)
            head(0, 0, first=True)
            with pe.Fori(0, (DIFF_HEADS - 2) // 2) as i:
                for p in range(2):
                    head(2 * i + (p + 1), (p + 1) % 2)
            head(DIFF_HEADS - 1, 1, last=True)
            turn_o(DIFF_HEADS - 1)
            pe.wait_ge(S["oTlo_done"], DIFF_HEADS)
            output(PLAN["out0"], 8, 1, oT0_hi, oT0_lo, KT, 0)
            mlp(0, "up0", 1)
            down(0, "down0", 2, 1)
            embed(0, 3, 2)

            pe.wait_ge(S["nlo_done"], 8 * 3 + 8)
            U = PLAN["cmp"]
            for g in range(GROUPS):
                weights(U + g + 1)
                features(A[g], (U + g) % RING, nT_hi, nT_lo).then_inc(S["units_done"], 1)
            U = PLAN["branch"]
            weights(U + 1)
            slot = U % RING
            for t in range(TT):
                for k in range(KT):
                    for pas in range(3):
                        w = (w_hi, w_lo, w_hi)[pas][slot]
                        a = (nT_hi, nT_hi, nT_lo)[pas]
                        m = pe.matmul(B[2][:, 48 * t:48 * t + 48], a[:, k, tok(t)], w[:, k * P:k * P + 48],
                                      start=(k, pas) == (0, 0), stop=(k, pas) == (KT - 1, 2))
            m.then_inc(S["units_done"], 1)
            pe.wait_ge(S["cmpw_in"], 48)
            pe.wait_ge(S["zb_done"], 4 * GROUPS)
            for el in range(CMP_LEN):
                for kv in range(2):
                    rows = slice(HEAD * kv, HEAD * kv + HEAD)
                    m = pe.matmul(B[kv][:, 0:GROUPS * N_CMP], w1[rows, el, :], zb[rows, :, :, el],
                                  start=el == 0, stop=el == CMP_LEN - 1)
                    if el == CMP_LEN - 1:
                        m.then_inc(S["hid_done"], 1)
            pe.wait_ge(S["gelc_done"], 2)
            pe.matmul(B[3][0:HEAD, 0:P], w2[:, 0, :], hid_k[:, :, :].rearrange("p g n -> p (g n)"), start=True,
                      stop=True).then_inc(S["kv_done"], 1)
            for g in range(GROUPS):
                m = pe.matmul(B[3][0:N_PAD, P + HEAD * g:P + HEAD * g + HEAD], hid_v[:, g, :], w2[:, 1, :],
                              start=True, stop=True)
            m.then_inc(S["kv_done"], 1)
            pe.wait_ge(S["kvc_done"], GHEADS)

            def group(g, first):
                def step(h, qt):
                    return 16 * g + 4 * h + qt

                U = PLAN["group"]
                if not first:
                    pe.wait_ge(S["goTlo_done"], 2 * g)
                for n, bank in enumerate((A[0], A[2], A[3], A[1])):
                    weights(4 * g + (U + n + 1))
                    features(bank, (U + n) % RING, nT_hi, nT_lo).then_inc(S["units_done"], 1)
                pe.wait_ge(S["vT_done"], g + 1)
                for t in range(TT):
                    m = transpose(B[0][:, tok(t)], vT[:, tok(t)])
                m.then_inc(S["vTt_done"], 1)
                pe.wait_ge(S["gqx_done"], 2 * g + 2)
                for t in range(TT):
                    for h in range(GHEADS):
                        q = (Qa, Qx)[h % 2][h // 2]
                        m = pe.matmul(B[2][:, (t * GHEADS + h) * N_PAD:(t * GHEADS + h + 1) * N_PAD],
                                      q[0:HEAD, tok(t)], kcmp[:, bass.ds(g, 1), :].rearrange("p a n -> p (a n)"),
                                      start=True, stop=True)
                m.then_inc(S["csc_done"], 1)
                pe.wait_ge(S["cp_done"], g + 1)
                for t in range(TT):
                    m = transpose(A[3][:, tok(t)], pc[:, t, :, :].rearrange("p h n -> p (h n)"))
                m.then_inc(S["cpT_done"], 1)
                pe.wait_ge(S["cpTc_done"], g + 1)
                for t in range(TT):
                    m = pe.matmul((A[0], A[3])[t // 2][:, 256 * (t % 2):256 * (t % 2) + 256], pcT[:, t, :],
                                  Vblk[:, bass.ds(g, 1), :].rearrange("p a n -> p (a n)"), start=True, stop=True)
                m.then_inc(S["coc_done"], 1)

                def gscores(h, qt):
                    n = (qt + 1) * P
                    if h == 0 and qt < 2:
                        pass
                    else:
                        pe.wait_ge(S["gprobs_done"], 2 * step(h, qt) - 2)
                    for c in range(2):
                        rows = slice(HEAD * c, HEAD * c + HEAD)
                        q = (Qa, Qx)[(h + c) % 2][h // 2]
                        pe.matmul(B[2 * (qt % 2) + c][:, 0:n], q[rows, tok(qt)], KK[rows, 0:n], start=True, stop=False)
                    for c in range(2):
                        pe.matmul(B[2 * (qt % 2) + c][:, n - P:n], ident_b[:, :], causal_b[:, :], start=False,
                                  stop=True).then_inc(S["gscores_done"], 1)

                def gturn(h, qt):
                    pe.wait_ge(S["gprobs_done"], 2 * step(h, qt) + 2)
                    if not (first and h == 0 and qt == 0):
                        pe.wait_ge(S["gpTa_done"], step(h, qt))
                        pe.wait_ge(S["gpTv_done"], step(h, qt))
                    for c in range(2):
                        for kb in range(qt + 1):
                            m = transpose(A[2 + c][:, kb * P:(kb + 1) * P], gp[:, qt % 2, c, kb * P:(kb + 1) * P])
                        m.then_inc(S["gT_done"], 1)

                def gvalues(h, qt):
                    pe.wait_ge(S["gpTa_done"], step(h, qt) + 1)
                    pe.wait_ge(S["gpTv_done"], step(h, qt) + 1)
                    if qt == 0 and h >= 2:
                        pe.wait_ge(S["oread_done"], 4 * g + h - 1)
                    for c in range(2):
                        for kb in range(qt + 1):
                            m = pe.matmul(A[h % 2][:, qt * P + HEAD * c:qt * P + HEAD * c + HEAD],
                                          gpT[:, qt % 2, c, kb * P:(kb + 1) * P], Vg[:, kb, HEAD * c:HEAD * c + HEAD],
                                          start=kb == 0, stop=kb == qt)
                    m.then_inc(S["gpv_done"], 1)

                def gturn_o(pair):
                    pe.wait_ge(S["opair_done"], 4 * g + 2 * pair + 2)
                    for t in range(TT):
                        m = transpose(A[2][:, tok(t)], opair[:, t, :])
                    m.then_inc(S["goT_done"], 1)
                    pe.wait_ge(S["goTlo_done"], 2 * g + pair + 1)

                seq = [(h, qt) for h in range(GHEADS) for qt in range(TT)]
                pe.wait_ge(S["vg_done"], g + 1)
                pe.wait_ge(S["oc_done"], 2 * g + 2)
                gscores(*seq[0])
                gscores(*seq[1])
                for n, (h, qt) in enumerate(seq):
                    gturn(h, qt)
                    if n + 2 < len(seq):
                        gscores(*seq[n + 2])
                    gvalues(h, qt)
                    if (h, qt) == (2, 1):
                        gturn_o(0)
                gturn_o(1)

            group(0, True)
            with pe.Fori(1, GROUPS) as g:
                group(g, False)
            output(PLAN["out1"], 8, 4, oT1_hi, oT1_lo, KT, 2)
            mlp(1, "up1", 4)
            down(1, "down1", 5, 3)
            embed(1, None, 5)


def by_features(w):
    k, n = w.shape
    return w.reshape(k // P, P, n // P, P).transpose(2, 1, 0, 3).reshape(n // P, P, D)


def by_tokens(w):
    k = w.shape[0]
    return w.reshape(k // (2 * P), 2, P, 2, HALF).transpose(3, 0, 2, 1, 4).reshape(-1, P, D)


def rotary(w):
    k, n = w.shape
    return w.reshape(k, n // HEAD, 2, 2, 16).transpose(0, 1, 3, 2, 4).reshape(k, n)


def pack(i):
    H = 2 * DIFF_HEADS * HEAD
    dw = i["diff_w_in"][0]
    units = [by_tokens(dw[:, 2 * H:])]
    q, k = by_features(rotary(dw[:, :H])), by_features(rotary(dw[:, H:2 * H]))
    units.append(np.stack([q, k], 1).reshape(-1, P, D))
    nw = i["nsa_w_in"][0]
    kv = GROUPS * HEAD
    at = D + kv * np.arange(7)
    part = {n: nw[:, at[j]:at[j + 1]] for j, n in enumerate(("kc", "vc", "ks", "vs", "kw", "vw"))}
    for n in ("kc", "ks", "kw"):
        part[n] = rotary(part[n])
    pair = lambda a, b, g: np.concatenate([part[a][:, g * HEAD:(g + 1) * HEAD], part[b][:, g * HEAD:(g + 1) * HEAD]], 1)
    for layer in range(LAYERS):
        if layer == 1:
            units += [by_features(pair("kc", "vc", g)) for g in range(GROUPS)]
            wide = np.zeros((D, P), np.float32)
            wide[:, :3 * D // HEAD] = nw[:, at[6]:]
            units.append(by_features(wide))
            nq = by_features(rotary(nw[:, :D]))
            for g in range(GROUPS):
                units += [by_features(pair("ks", "kw", g)), nq[2 * g:2 * g + 2], by_features(pair("vs", "vw", g))]
        units.append(by_tokens((i["diff_w_out"], i["nsa_w_out"])[layer][0]))
        up = by_features(i["ffn_w_up"][layer])
        units.append(np.stack([up[:FT], up[FT:]], 1).reshape(-1, P, D))
        units.append(by_tokens(i["ffn_w_down"][layer]))
        gate = by_tokens(i["ple_gate_w"][layer])
        units += [gate[:4], by_tokens(i["ple_proj_w"][layer]), gate[4:]]
    return np.concatenate(units, 0)


def constants():
    c = np.zeros((P, C_ALL), np.float32)
    row = np.arange(P) % HEAD
    freq = 16 * (row // 32) + row % 16
    c[:, C_INV] = np.float32(THETA) ** (-(2 * freq).astype(np.float32) / np.float32(HEAD))
    c[:, C_SIGN] = np.where(row % 32 < 16, -1.0, 1.0)
    c[:, C_IDENT:C_IDENT + P] = np.eye(P)
    c[:, C_CAUSAL:C_CAUSAL + P] = np.where(np.arange(P)[None, :] <= np.arange(P)[:, None], 0.0, MASKED)
    t = np.arange(TT)[None, :, None] * P + np.arange(P)[:, None, None]
    last = np.arange(N_PAD) * CMP_STRIDE + CMP_LEN - 1
    ok = (last <= t) & (np.arange(N_PAD) < N_CMP)
    c[:, C_CMP:] = ok.reshape(P, TT * N_PAD)
    return c


def kernel(**inputs):
    import concourse.bacc as bacc
    from concourse.bass_utils import run_bass_kernel_spmd as run

    i = {k: np.asarray(v) for k, v in inputs.items()}
    perm = np.arange(HEAD).reshape(2, 2, 16).transpose(1, 0, 2).reshape(-1)
    gains = np.concatenate([i["norm_gains"], i["ple_norm_g"][:, None]], 1).reshape(LAYERS * GAINS, 1, D)
    taps = np.concatenate([i["ffn_conv_w"], i["ffn_conv_b"][:, None]], 1)
    arrays = {
        "x": i["x"].reshape(TT, P, D).transpose(1, 0, 2),
        "w": pack(i),
        "const": constants(),
        "gains": np.broadcast_to(gains, (LAYERS * GAINS, P, D)),
        "conv": taps.reshape(LAYERS, 4, 2 * FT, P).transpose(0, 3, 2, 1).reshape(LAYERS, P, 8 * FT),
        "subln": i["diff_subln_g"][0].reshape(P, 1),
        "lam": np.broadcast_to(np.stack([i[f"diff_lam_{n}"][0] for n in ("q1", "k1", "q2", "k2")])[None], (P, 4, HEAD)),
        "pos": np.broadcast_to(i["positions"].reshape(1, SEQ), (P, SEQ)),
        "pT": i["p"][:, 0].reshape(LAYERS, SEQ, 2, P).transpose(0, 3, 2, 1),
        "w1": np.concatenate([i["nsa_ck_w1"][0].transpose(1, 0, 2)[perm], i["nsa_cv_w1"][0].transpose(1, 0, 2)], 0),
        "cpos": np.concatenate([i["nsa_ck_pos"][0].T[perm], i["nsa_cv_pos"][0].T], 0),
        "w2": np.stack([i["nsa_ck_w2"][0][:, perm], i["nsa_cv_w2"][0]], 1),
    }
    nc = bacc.Bacc("TRN2", target_bir_lowering=False, num_devices=1)
    feeds, args = {}, []
    for name, a in arrays.items():
        feeds["in_" + name] = np.ascontiguousarray(a)
        args.append(nc.dram_tensor("in_" + name, a.shape, mybir.dt.from_np(a.dtype), kind="ExternalInput").ap())
    out = nc.dram_tensor("out", (P, TT, D), F32, kind="ExternalOutput").ap()
    trunk(nc, *args, out)
    got = run(nc, [feeds], core_ids=[0]).results[0]["out"]
    return got.transpose(1, 0, 2).reshape(1, SEQ, D)
```

```python
from contextlib import ExitStack, contextmanager
import math

import numpy as np

import concourse.bass as bass
import concourse.mybir as mybir

F32 = mybir.dt.float32
F32R = mybir.dt.float32r
BF16 = mybir.dt.bfloat16
I32 = mybir.dt.int32
ALU = mybir.AluOpType
ACT = mybir.ActivationFunctionType
AX = mybir.AxisListType

P = 128
SEQ = 512
D = 1024
TT = SEQ // P
KT = D // P
HEAD = 64
HALF = D // 2
LAYERS = 2
EPS = 1e-6
SCALE = HEAD ** -0.5
MASKED = -1e30
THETA = 10000.0

NEWTON = 3
DIFF_HEADS = D // (2 * HEAD)
LAMBDA_INIT = 0.8 - 0.6 * math.exp(-0.3 * 0)

GROUPS = 4
GHEADS = D // HEAD // GROUPS
ORDER = (0, 3, 1, 2)
CMP_LEN = 32
CMP_STRIDE = 16
N_CMP = (SEQ - CMP_LEN) // CMP_STRIDE + 1
N_PAD = 32
CMP_HIDDEN = 128

FF = 2816
FT = FF // P
PLE = 256

RING = 4
RAW = 2
PLAN, _at = {}, 0
for _name, _n in (("v", 8), ("qk", 2 * DIFF_HEADS), ("out0", 8), ("up0", 2 * FT), ("down0", FT),
                  ("gate0a", 4), ("ple0", 2), ("gate0b", 4),
                  ("cmp", GROUPS), ("branch", 1), ("group", 4 * GROUPS), ("out1", 8), ("up1", 2 * FT),
                  ("down1", FT), ("gate1a", 4), ("ple1", 2), ("gate1b", 4)):
    PLAN[_name] = _at
    _at += _n
UNITS = _at

C_INV, C_SIGN, C_IDENT, C_CAUSAL, C_CMP = 0, 1, 2, 2 + P, 2 + 2 * P
C_ALL = C_CMP + TT * N_PAD
GAINS = 5
TWO_PI = 2 * math.pi
PI_1 = 6.28125
PI_2 = float(np.float32(TWO_PI - PI_1))
PI_3 = float(np.float32(TWO_PI - PI_1 - PI_2))
ROUND = 1.5 * 2.0 ** 23
PI_MAX = float(np.nextafter(np.float32(math.pi), np.float32(0)))


class Chain:

    def __init__(self, engine, sem):
        self.engine, self.sem, self.base, self.n = engine, sem, 0, 0

    def step(self, ins):
        ins.then_inc(self.sem, 1)
        self.n += 1

    def link(self, ins):
        self.step(ins)
        self.engine.wait_ge(self.sem, self.base + self.n)

    def wait(self, last):
        self.engine.wait_ge(self.sem, self.base + self.n - last)

    @contextmanager
    def loop(self, start, end, per):
        before = self.base + self.n
        with self.engine.Fori(start, end) as i:
            self.base, self.n = before + per * (i - start), 0
            yield i
            assert self.n == per, (self.n, per)
        self.base, self.n = before + per * (end - start), 0


def trunk(nc, x_in, w_in, const_in, gain_in, conv_in, subln_in, lam_in, pos_in, pT_in, w1_in,
          cpos_in, w2_in, out):
    ctx = ExitStack()
    with ctx:
        def sb(name, shape, dt=F32, on=ctx):
            return on.enter_context(nc.sbuf_tensor(name, shape, dt))

        x = sb("x", [P, TT, D])
        nT_hi = sb("nT_hi", [P, KT, SEQ], F32R)
        nT_lo = sb("nT_lo", [P, KT, SEQ], F32R)
        w_raw = [sb(f"w_raw{i}", [P, D]) for i in range(RAW)]
        w_hi = [sb(f"w_hi{i}", [P, D], F32R) for i in range(RING)]
        w_lo = [sb(f"w_lo{i}", [P, D], F32R) for i in range(RING)]
        cosT = sb("cosT", [P, SEQ])
        sinT = sb("sinT", [P, SEQ])
        g_pre = sb("g_pre", [P, D])
        g_post = sb("g_post", [P, D])
        xn = sb("xn", [P, D])
        ident = sb("ident", [P, P])
        ident_b = sb("ident_b", [P, P], BF16)
        causal_b = sb("causal_b", [P, P], BF16)
        conv = sb("conv", [P, 4 * 2 * FT])
        eps = sb("eps", [P, 1])
        ss = sb("ss", [P, TT])
        std = sb("std", [P, TT])
        rinv = sb("rinv", [P, TT])
        yss = sb("yss", [P, 2, TT])
        yst = sb("yst", [P, 3, TT])
        subg = sb("subg", [P, 1])
        neg_lam = sb("neg_lam", [P, 1])
        lam = sb("lam", [P, 4])
        junk = sb("junk", [P, D], BF16)
        y0 = sb("y0", [P, TT, HALF])

        mx = sb("mx", [P, TT, 2])
        nm = sb("nm", [P, TT, 2])
        sums = sb("sums", [P, 2, TT, 2])
        st1 = sb("st1", [P, 4])
        osum = sb("osum", [P, 3, TT])
        coef = sb("coef", [P, 2, TT])
        st2 = sb("st2", [P, 2, TT, 2])
        cst = sb("cst", [P, 3, TT * GHEADS])

        def overlay(*parts):
            with ExitStack() as on:
                return [sb(*part, on=on) for part in parts]

        const, pos_i, ang, turn, xn0, red, lam_v, lam_p = overlay(
            ("const", [P, C_ALL], F32), ("pos_i", [P, SEQ], I32), ("ang", [P, SEQ], F32),
            ("turn", [P, SEQ], F32), ("xn0", [P, TT, D], F32), ("red", [P, SEQ], F32), ("lam_v", [P, 4, HEAD], F32), ("lam_p", [P, 2, HEAD], F32))
        (V, oT0_hi, oT0_lo, qT0, qT1, kT0, kT1, sh, t1, t2, pr, amix, pT, o_raw, o_nrm, o_sq) = overlay(
            ("V", [P, TT, D], F32), ("oT0_hi", [P, KT, SEQ], F32R), ("oT0_lo", [P, KT, SEQ], F32R),
            ("qT0", [P, SEQ], F32), ("qT1", [P, SEQ], F32), ("kT0", [P, SEQ], F32), ("kT1", [P, SEQ], F32),
            ("sh", [P, SEQ], F32), ("t1", [P, SEQ], F32), ("t2", [P, SEQ], F32),
            ("pr", [P, 2, 2, SEQ], F32), ("amix", [P, 2, SEQ], F32), ("pT", [P, 2, SEQ], F32),
            ("o_raw", [P, TT, P], F32), ("o_nrm", [P, TT, P], F32), ("o_sq", [P, TT, P], F32))
        qT, kT = [qT0, qT1], [kT0, kT1]
        hT_hi, hT_lo = overlay(("hT_hi", [P, FT, SEQ], F32R), ("hT_lo", [P, FT, SEQ], F32R))
        pe_raw, pe_hi, pe_lo, sg = overlay(
            ("pe_raw", [P, 2, SEQ], F32), ("pe_hi", [P, 2, SEQ], F32R), ("pe_lo", [P, 2, SEQ], F32R),
            ("sg", [P, TT, HALF], F32))
        keep1 = [("oT1_hi", [P, KT, SEQ], F32R), ("oT1_lo", [P, KT, SEQ], F32R),
                 ("kcmp", [HEAD, GROUPS, N_PAD], F32), ("Vblk", [P, GROUPS, GHEADS * HEAD], F32),
                 ("gates", [P, TT, 3 * D // HEAD], F32)]
        (oT1_hi, oT1_lo, kcmp, Vblk, gates, w1, zb, hid_k, hid_v, cpos, w2, ksh, kt1, kt2, kr) = overlay(
            *keep1, ("w1", [P, CMP_LEN, CMP_HIDDEN], F32), ("zb", [P, GROUPS, N_CMP, CMP_LEN], F32),
            ("hid_k", [P, GROUPS, N_PAD], F32), ("hid_v", [P, GROUPS, N_PAD], F32),
            ("cpos", [P, CMP_LEN], F32), ("w2", [P, 2, HEAD], F32),
            ("ksh", [HEAD, SEQ], F32), ("kt1", [HEAD, SEQ], F32), ("kt2", [HEAD, SEQ], F32),
            ("kr", [HEAD, SEQ], F32))
        (_, _, _, _, _, cm, Vg, vT, KK, Qa0, Qa1, Qx0, Qx1, gsh, gt1, gt2, gp, gpT, sc, pc, pcT, oc,
         og) = overlay(
            *[("again_" + n, s, d) for n, s, d in keep1],
            ("cm", [P, 2, TT * N_PAD], F32),
            ("Vg", [P, TT, P + HEAD], F32), ("vT", [P, SEQ], F32), ("KK", [P, SEQ], F32),
            ("Qa0", [P, SEQ], F32), ("Qa1", [P, SEQ], F32), ("Qx0", [P, SEQ], F32), ("Qx1", [P, SEQ], F32),
            ("gsh", [P, SEQ], F32), ("gt1", [P, SEQ], F32), ("gt2", [P, SEQ], F32),
            ("gp", [P, 2, 2, SEQ], F32), ("gpT", [P, 2, 2, SEQ], F32),
            ("sc", [P, TT, GHEADS, N_PAD], F32), ("pc", [P, TT, GHEADS, N_PAD], F32),
            ("pcT", [P, TT, P], F32), ("oc", [P, TT, GHEADS, HEAD], F32),
            ("og", [P, TT, P], F32))
        Qa, Qx = [Qa0, Qa1], [Qx0, Qx1]
        opair = y0
        banks_a = ctx.enter_context(nc.psum_tensor("banks_a", [P, 4, 512], F32))
        banks_b = ctx.enter_context(nc.psum_tensor("banks_b", [P, 4, 512], F32))
        A, B = [banks_a[:, n, :] for n in range(4)], [banks_b[:, n, :] for n in range(4)]
        names = """
        x_in0 x_in1 x_in2 x_in3 consts_in gain_in gpost_in conv_in lamv_in pos_in sub_in
        w_in0 w_in1 w_hi_done w_lo_done units_done tile_done
        consts_ready ang_ready rope_in rope_tab lam_sum lam_exp lam_ready start_done
        std_done xn_done xT_done nhi_done nlo_done x_updated
        y0_done ystd_done v_done
        rope_done scores_done negmax_done probs_done mix_done mixT_done ovar_done orinv_done pT_done pv_done
        oraw_done onrm_done oT_done oThi_done oTlo_done
        aff_done gateconv_done conv_done gelu_done h_done hhi_done hlo_done
        ple_in pehi_done pelo_done sig_done xhalf_done
        cmpw_in zb_done hid_done gelc_done kv_done kvc_done gates_done pad_ready cm_in
        groupkv_done gqx_done vT_done vTt_done vg_done
        csc_done cexp_in cexp_done cp_done cpT_done cpTc_done coc_done oc_done
        gscores_done gnegmax_done gprobs_done gT_done gpTa_done gpTv_done gpv_done
        oread_done opair_done goT_done goThi_done goTlo_done
        out_done chain_act chain_dve chain_pool
        """.split()
        S = {n: ctx.enter_context(nc.semaphore(n)) for n in names}
        block = ctx.enter_context(nc.Block())

        def tok(t):
            return slice(t * P, (t + 1) * P)

        def xT_banks(q, t):
            return ((A[0], A[1]), (A[2], A[3]), (B[0], B[1]), (B[2], B[3]))[t] if q == 0 else (B[0], B[1])

        def normed(q, t):
            return xn0[:, t, :] if q == 0 else xn[:, :]

        @block.sync
        def _(sp):
            for t in range(TT):
                sp.dma_start(x[:, t, :], x_in[:, t, :]).then_inc(S[f"x_in{t}"], 16)
                if t < RAW:
                    sp.dma_start(w_raw[t][:, :], w_in[t, :, :]).then_inc(S[f"w_in{t}"], 16)
            with sp.Fori(1, UNITS // RAW) as i:
                for r in range(RAW):
                    sp.wait_ge(S["w_lo_done"], i * RAW + (r + 1 - RAW))
                    sp.dma_start(w_raw[r][:, :], w_in[bass.ds(i * RAW + r, 1), :, :].rearrange("a p n -> (a p) n"))\
                        .then_inc(S[f"w_in{r}"], 16)
            for u in range(UNITS // RAW * RAW, UNITS):
                sp.wait_ge(S["w_lo_done"], u + 1 - RAW)
                sp.dma_start(w_raw[u % RAW][:, :], w_in[u, :, :]).then_inc(S[f"w_in{u % RAW}"], 16)
            for t in range(TT):
                sp.wait_ge(S["x_updated"], 4 * (3 * LAYERS - 1) + t + 1)
                sp.dma_start(out[:, t, :], x[:, t, :]).then_inc(S["out_done"], 16)
            sp.wait_ge(S["out_done"], 16 * TT)

        @block.gpsimd
        def _(pool):
            chain = Chain(pool, S["chain_pool"])
            link = chain.link
            for n, c in enumerate((-0.5, 1.5)):
                link(pool.memset(coef[:, n, :], c))

            def low(k, slot, u1):
                pool.wait_ge(S["w_hi_done"], u1)
                pool.tensor_tensor(w_lo[slot][:, :], w_raw[k % RAW][:, :], w_hi[slot][:, :].bitcast(F32),
                                   ALU.subtract).then_inc(S["w_lo_done"], 1)

            def lows(start, end):
                whole = (end - start) // RING
                with pool.Fori(0, whole) as i:
                    for k in range(RING):
                        low(start + k, (start + k) % RING, start + i * RING + (k + 1))
                for u in range(start + whole * RING, end):
                    low(u, u % RING, u + 1)

            def o_rinv(h):
                pool.wait_ge(S["ovar_done"], h + 1)
                v, e, y = osum[:, 0, :], osum[:, 1, :], osum[:, 2, :]
                link(pool.tensor_tensor(v, v, coef[:, 0, :], ALU.mult))
                for n in range(NEWTON):
                    link(pool.tensor_tensor(e, y, y, ALU.mult))
                    link(pool.tensor_tensor(e, e, v, ALU.mult))
                    link(pool.tensor_tensor(e, e, coef[:, 1, :], ALU.add))
                    last = pool.tensor_tensor(y, y, e, ALU.mult)
                    if n < NEWTON - 1:
                        link(last)
                last.then_inc(S["orinv_done"], 1)

            ahead = PLAN["qk"] + RING + 4
            lows(0, ahead)
            with chain.loop(0, (DIFF_HEADS - 2) // 2, 2 * 4 * NEWTON) as i:
                for p in range(2):
                    o_rinv(2 * i + p)
                    for k in range(2):
                        u = ahead + 2 * p + k
                        low(u, u % RING, u + 4 * i + 1)
            o_rinv(DIFF_HEADS - 2)
            o_rinv(DIFF_HEADS - 1)
            lows(ahead + 2 * (DIFF_HEADS - 2), UNITS)

        @block.scalar
        def _(act):
            chain = Chain(act, S["chain_act"])
            link = chain.link

            def signal(ins, name, value):
                ins.then_inc(S[name], 1)
                act.wait_ge(S[name], value)

            def w_high(u, i=0, per=0):
                if u >= UNITS:
                    return
                if u >= RING:
                    act.wait_ge(S["units_done"], u + 1 - RING + per * i)
                act.wait_ge(S[f"w_in{u % RAW}"], 16 * (u // RAW + 1) + 16 * (per // RAW) * i)
                act.activation(w_hi[u % RING][:, :], w_raw[u % RAW][:, :], ACT.Copy).then_inc(S["w_hi_done"], 1)

            def stats(q, t):
                if q == 0:
                    act.wait_ge(S[f"x_in{t}"], 16)
                else:
                    act.wait_ge(S["x_updated"], 4 * (q - 1) + t + 1)
                link(act.activation(junk[:, :], x[:, t, :], ACT.Square, accum_out=ss[:, t:t + 1]))
                signal(act.activation(std[:, t:t + 1], ss[:, t:t + 1], ACT.Sqrt, bias=eps[:, :], scale=1.0 / D),
                       "std_done", 4 * q + t + 1)

            def nT_high(q, t):
                for b, bank in enumerate(xT_banks(q, t)):
                    act.wait_ge(S["xT_done"], 8 * q + 2 * t + b + 1)
                    signal(act.activation(nT_hi[:, 4 * b:4 * b + 4, tok(t)],
                                          bank.rearrange("p (k n) -> p k n", k=4), ACT.Copy),
                           "nhi_done", 8 * q + 2 * t + b + 1)

            def gains(q, r):
                if q:
                    act.wait_ge(S["nlo_done"], 8 * q)
                act.dma_start(g_pre[:, :], gain_in[GAINS * (q // 3) + 2 * (q % 3), :, :]).then_inc(S["gain_in"], 16)
                if r is not None:
                    act.dma_start(g_post[:, :], gain_in[GAINS * (r // 2) + 1 + 2 * (r % 2), :, :])\
                        .then_inc(S["gpost_in"], 16)

            def output_norm(r, phase, name, n, q, asked=0):
                U = PLAN[name]
                for k in range(asked, n // 2):
                    w_high(U + k + RING)
                for t in range(TT):
                    act.wait_ge(S["y0_done"], 4 * r + t + 1)
                    link(act.activation(junk[:, 0:HALF], y0[:, t, :], ACT.Square, accum_out=yss[:, 0, t:t + 1]))
                    link(act.activation(yst[:, 0, t:t + 1], yss[:, 0, t:t + 1], ACT.Identity, bias=eps[:, :],
                                        scale=1.0 / D))
                for k in range(n // 2, n - 4):
                    w_high(U + k + RING)

                def y_std(t):
                    if t < TT - 1:
                        act.wait_ge(S["tile_done"], 3 * phase + t + 1)
                    else:
                        act.wait_ge(S["units_done"], U + n)
                    link(act.activation(junk[:, 0:HALF], A[t][:, :], ACT.Square, accum_out=yss[:, 1, t:t + 1]))
                    signal(act.activation(yst[:, 1, t:t + 1], yss[:, 1, t:t + 1], ACT.Sqrt,
                                          bias=yst[:, 0, t:t + 1], scale=1.0 / D), "ystd_done", 4 * r + t + 1)
                y_std(0)
                stats(q, 0)
                for t in range(1, TT):
                    y_std(t)
                    if t >= 2:
                        w_high(U + n + 2 * (t - 2))
                    nT_high(q, t - 1)
                    if t == 2:
                        w_high(U + n + 1)
                    stats(q, t)
                nT_high(q, TT - 1)
                w_high(U + n + 3)

            def mlp(layer, name):
                U = PLAN[name]

                def pair(i, p, peeled):
                    j = 2 * i + p
                    slot = (U + 2 * p) % RING
                    del slot
                    if not peeled:
                        act.wait_ge(S["hlo_done"], FT * layer + j - 1)

                    def affine(v, dst, bank):
                        act.wait_ge(S["units_done"], U + 2 * j + v + 1)
                        f = j + v * FT
                        signal(act.activation(dst, bank[:, :], ACT.Identity, bias=conv[:, bass.ds(4 * f + 3, 1)],
                                              scale=conv[:, bass.ds(4 * f + 2, 1)]),
                               "aff_done", 2 * FT * layer + 2 * j + v + 1)
                    affine(0, y0[:, p, :], A[2 * p])
                    w_high(U + RING + 2 * p, i, RING)
                    affine(1, y0[:, 2 + p, :], A[2 * p + 1])
                    act.wait_ge(S["gateconv_done"], FT * layer + j + 1)
                    signal(act.activation(y0[:, p, :], y0[:, p, :], ACT.Gelu_apprx_tanh), "gelu_done",
                           FT * layer + j + 1)
                    w_high(U + RING + 2 * p + 1, i, RING)
                    act.wait_ge(S["h_done"], FT * layer + j + 1)
                    signal(act.activation(hT_hi[:, bass.ds(j, 1), :].rearrange("p a n -> p (a n)"),
                                          y0[:, 2 + p, :], ACT.Copy), "hhi_done", FT * layer + j + 1)
                if layer == 0:
                    pass
                for p in range(2):
                    pair(0, p, True)
                with chain.loop(1, FT // 2, 0) as i:
                    for p in range(2):
                        pair(i, p, False)

            def embed(layer, q, phase):
                Ua, Up, Ub = (PLAN[f"gate{layer}a"], PLAN[f"ple{layer}"], PLAN[f"gate{layer}b"])
                act.wait_ge(S["units_done"], Ua)
                act.dma_start(pe_raw[:, :, :], pT_in[layer, :, :, :]).then_inc(S["ple_in"], 16)
                act.wait_ge(S["ple_in"], 16 * (layer + 1))
                signal(act.activation(pe_hi[:, :, :], pe_raw[:, :, :], ACT.Copy), "pehi_done", layer + 1)
                for k in range(4):
                    w_high(Ua + k + RING)

                def sigmoid(half, t, bank):
                    signal(act.activation(sg[:, t, :], bank[t][:, :], ACT.Sigmoid), "sig_done",
                           8 * layer + 4 * half + t + 1)
                for t in range(TT):
                    sigmoid(0, t, A)
                for k in range(2):
                    w_high(Up + k + RING)

                def second(t):
                    if t < TT - 1:
                        act.wait_ge(S["tile_done"], 3 * phase + t + 1)
                    else:
                        act.wait_ge(S["units_done"], Ub + 4)
                    act.wait_ge(S["xhalf_done"], 4 * layer + t + 1)
                    sigmoid(1, t, B)
                if layer == LAYERS - 1:
                    for t in range(TT):
                        second(t)
                    return
                second(0)
                stats(q, 0)
                for t in range(1, TT):
                    second(t)
                    if t >= 2:
                        w_high(Ub + 2 * t)
                    nT_high(q, t - 1)
                    if t == 2:
                        w_high(Ub + 5)
                    stats(q, t)
                nT_high(q, TT - 1)
                w_high(Ub + 7)

            act.dma_start(const[:, :], const_in).then_inc(S["consts_in"], 16)
            gains(0, 0)
            act.wait_ge(S["consts_ready"], 4)
            stats(0, 0)
            w_high(0)
            stats(0, 1)
            nT_high(0, 0)
            w_high(1)
            stats(0, 2)
            nT_high(0, 1)
            stats(0, 3)
            nT_high(0, 2)
            nT_high(0, 3)
            w_high(2)
            w_high(3)
            act.dma_start(pos_i[:, :], pos_in).then_inc(S["pos_in"], 16)
            act.dma_start(lam_v[:, :, :], lam_in).then_inc(S["lamv_in"], 16)
            act.dma_start(subg[:, :], subln_in).then_inc(S["sub_in"], 16)
            act.dma_start(conv[:, :], conv_in[0, :, :]).then_inc(S["conv_in"], 16)
            UV = PLAN["v"] + RING
            w_high(UV)
            w_high(UV + 1)
            act.wait_ge(S["rope_in"], 1)
            signal(act.activation(sinT[:, :], red[:, :], ACT.Sin, scale=const[:, C_SIGN:C_SIGN + 1]), "rope_tab", 1)
            act.wait_ge(S["rope_in"], 2)
            signal(act.activation(cosT[:, :], turn[:, :], ACT.Sin), "rope_tab", 2)
            w_high(UV + 2)
            w_high(UV + 3)
            act.wait_ge(S["lam_sum"], 1)
            signal(act.activation(lam[:, 2:4], lam[:, 0:2], ACT.Exp), "lam_exp", 1)
            for u in range(4, 8):
                w_high(UV + u)

            def exps(h, qt):
                for c in range(2):
                    act.wait_ge(S["negmax_done"], 4 * h + qt + 1)
                    if not (isinstance(h, int) and h == 0 and qt < 2):
                        act.wait_ge(S["mix_done"], 4 * h + qt - 1)
                    n = (qt + 1) * P
                    signal(act.activation(pr[:, qt % 2, c, 0:n], B[2 * (qt % 2) + c][:, 0:n], ACT.Exp,
                                          bias=nm[:, qt, c:c + 1], scale=SCALE,
                                          accum_out=sums[:, par(h), qt, c:c + 1]),
                           "probs_done", 8 * h + 2 * qt + c + 1)

            parity = [0]

            def par(h):
                return parity[0]

            def p_turned(h, qt):
                act.wait_ge(S["mixT_done"], 4 * h + qt + 1)
                if not (isinstance(h, int) and h == 0 and qt < 2):
                    act.wait_ge(S["pv_done"], 4 * h + qt - 1)
                n = (qt + 1) * P
                signal(act.activation(pT[:, qt % 2, 0:n], A[2][:, 0:n], ACT.Copy), "pT_done", 4 * h + qt + 1)

            def o_out(h):
                act.wait_ge(S["pv_done"], 4 * h + 4)
                if not (isinstance(h, int) and h == 0):
                    act.wait_ge(S["onrm_done"], h)
                link(act.activation(o_sq[:, :, :], A[3].rearrange("p (t n) -> p t n", t=TT), ACT.Square))
                signal(act.activation(o_raw[:, :, :], A[3].rearrange("p (t n) -> p t n", t=TT), ACT.Copy),
                       "oraw_done", h + 1)

            def oT_high(h):
                act.wait_ge(S["oT_done"], h + 1)
                signal(act.activation(oT0_hi[:, bass.ds(h, 1), :].rearrange("p a n -> p (a n)"), A[2][:, :],
                                      ACT.Identity, scale=subg[:, :]), "oThi_done", h + 1)

            def head(h, p, first=False, last=False, i=0, per=0, u=0):
                parity[0] = p
                exps(h, 0)
                exps(h, 1)
                if not first:
                    o_out(h - 1)
                p_turned(h, 0)
                exps(h, 2)
                p_turned(h, 1)
                if not last:
                    w_high(u, i, per)
                exps(h, 3)
                p_turned(h, 2)
                if not first:
                    oT_high(h - 1)
                if not last:
                    w_high(u + 1, i, per)
                p_turned(h, 3)

            UH = PLAN["qk"] + RING
            w_high(UH)
            w_high(UH + 1)
            act.wait_ge(S["lam_ready"], 1)
            head(0, 0, first=True, u=UH + 2)
            with chain.loop(0, (DIFF_HEADS - 2) // 2, 2) as i:
                for p in range(2):
                    head(2 * i + (p + 1), (p + 1) % 2, i=i, per=4, u=UH + 4 + 2 * p)
            head(DIFF_HEADS - 1, 1, last=True)
            o_out(DIFF_HEADS - 1)
            w_high(PLAN["out0"] + RING)
            oT_high(DIFF_HEADS - 1)

            gains(1, None)
            output_norm(0, 0, "out0", 8, 1, asked=1)
            gains(2, 1)
            mlp(0, "up0")
            output_norm(1, 1, "down0", FT, 2)
            gains(3, 2)
            act.dma_start(conv[:, :], conv_in[1, :, :]).then_inc(S["conv_in"], 16)
            embed(0, 3, 2)

            act.dma_start(w1[:, :, :], w1_in).then_inc(S["cmpw_in"], 16)
            act.dma_start(cpos[:, :], cpos_in).then_inc(S["cmpw_in"], 16)
            act.dma_start(w2[:, :, :], w2_in).then_inc(S["cmpw_in"], 16)
            gains(4, None)
            for k in range(GROUPS + 1):
                w_high(PLAN["cmp"] + RING + k)
            act.wait_ge(S["units_done"], PLAN["branch"] + 1)
            signal(act.activation(gates[:, :, :], B[2][:, 0:TT * 48].rearrange("p (t n) -> p t n", t=TT), ACT.Sigmoid),
                   "gates_done", 1)
            act.wait_ge(S["hid_done"], 2)
            act.wait_ge(S["pad_ready"], 1)
            for kv, dst in enumerate((hid_k, hid_v)):
                signal(act.activation(dst[:, :, 0:N_CMP], B[kv][:, 0:GROUPS * N_CMP].rearrange("p (g n) -> p g n", g=GROUPS),
                                      ACT.Gelu_apprx_tanh), "gelc_done", kv + 1)
            act.wait_ge(S["kv_done"], 2)
            link(act.activation(kcmp[:, :, :], B[3][0:HEAD, 0:P].rearrange("p (g n) -> p g n", g=GROUPS), ACT.Copy))
            for h in range(GHEADS):
                signal(act.activation(Vblk[32 * h:32 * h + 32, :, HEAD * h:HEAD * h + HEAD],
                                      B[3][0:N_PAD, P:P + GROUPS * HEAD].rearrange("p (g n) -> p g n", g=GROUPS),
                                      ACT.Copy), "kvc_done", h + 1)
            act.dma_start(cm[:, 0, :], const_in[:, C_CMP:C_ALL]).then_inc(S["cm_in"], 16)

            def goT_high(pair, m):
                act.wait_ge(S["goT_done"], pair + 1)
                signal(act.activation(oT1_hi[:, bass.ds(pair, 1), :].rearrange("p a n -> p (a n)"),
                                      A[2 + m], ACT.Copy), "goThi_done", pair + 1)

            def group(g, first, i=0, u=0, per=0):
                def step(h, k):
                    return 16 * g + 4 * h + k

                def gexps(h, k):
                    qt = ORDER[k]
                    n = (qt + 1) * P
                    for c in range(2):
                        act.wait_ge(S["gnegmax_done"], step(h, k) + 1)
                        if not (first and h == 0 and k < 2):
                            act.wait_ge(S["gT_done"], 2 * step(h, k) - 2)
                        signal(act.activation(gp[:, k % 2, c, 0:n], B[2 * (k % 2) + c][:, 0:n], ACT.Exp,
                                              bias=nm[:, qt, c:c + 1], scale=SCALE,
                                              accum_out=sums[:, h % 2, qt, c:c + 1]),
                               "gprobs_done", 2 * step(h, k) + c + 1)

                def gp_turned(h, k):
                    n = (ORDER[k] + 1) * P
                    act.wait_ge(S["gT_done"], 2 * step(h, k) + 1)
                    if not (first and h == 0 and k < 2):
                        act.wait_ge(S["gpv_done"], step(h, k) - 1)
                    signal(act.activation(gpT[:, k % 2, 0, 0:n], A[2][:, 0:n], ACT.Copy), "gpTa_done",
                           step(h, k) + 1)

                def swap(n):
                    act.wait_ge(S["groupkv_done"], 3 * g + 1 + n)
                    link(act.activation(Qx[n][0:HEAD, :], Qa[n][HEAD:P, :], ACT.Copy))
                    signal(act.activation(Qx[n][HEAD:P, :], Qa[n][0:HEAD, :], ACT.Copy), "gqx_done", 2 * g + n + 1)

                w_high(u, i, per)
                if not first:
                    for m in range(2):
                        goT_high(2 * g - 2 + m, m)
                swap(0)
                w_high(u + 1, i, per)
                swap(1)
                w_high(u + 2, i, per)
                act.wait_ge(S["cexp_in"], g + 1)
                signal(act.activation(pc[:, :, :, :], sc[:, :, :, :], ACT.Exp, scale=SCALE), "cexp_done", g + 1)
                seq = [(h, k) for h in range(GHEADS) for k in range(TT)]
                gexps(*seq[0])
                act.wait_ge(S["units_done"], PLAN["group"] + 4 * g + 4)
                signal(act.activation(vT[:, :], B[3], ACT.Copy), "vT_done", g + 1)
                act.wait_ge(S["cpT_done"], g + 1)
                signal(act.activation(pcT[:, :, :], A[3].rearrange("p (t n) -> p t n", t=TT), ACT.Copy),
                       "cpTc_done", g + 1)
                act.wait_ge(S["vTt_done"], g + 1)
                v3 = A[0].rearrange("p (t n) -> p t n", t=TT)
                link(act.activation(Vg[:, :, 0:P], v3, ACT.Copy))
                signal(act.activation(Vg[:, :, P:P + HEAD], v3[:, :, 0:HEAD], ACT.Copy), "vg_done", g + 1)
                gexps(*seq[1])
                for n, (h, k) in enumerate(seq):
                    gp_turned(h, k)
                    if n + 2 < len(seq):
                        gexps(*seq[n + 2])
                    if n == 1:
                        w_high(u + 3, i, per)

            UG = PLAN["group"] + RING
            group(0, True, u=UG)
            with chain.loop(1, GROUPS, 3) as g:
                group(g, False, i=g, u=UG, per=4)
            w_high(PLAN["out1"] + RING)
            for m in range(2):
                goT_high(2 * GROUPS - 2 + m, m)

            output_norm(2, 3, "out1", 8, 4, asked=1)
            gains(5, 3)
            mlp(1, "up1")
            output_norm(3, 4, "down1", FT, 5)
            embed(1, None, 5)

        @block.vector
        def _(dve):
            chain = Chain(dve, S["chain_dve"])
            link = chain.link

            def signal(ins, name, value):
                ins.then_inc(S[name], 1)
                dve.wait_ge(S[name], value)

            def prepare(q, t):
                if t == 0:
                    dve.wait_ge(S["gain_in"], 16 * (q + 1))
                elif q:
                    dve.wait_ge(S["xT_done"], 8 * q + 2 * t)
                dve.wait_ge(S["std_done"], 4 * q + t + 1)
                link(dve.reciprocal(rinv[:, t:t + 1], std[:, t:t + 1]))
                signal(dve.scalar_tensor_tensor(normed(q, t), x[:, t, :], rinv[:, t:t + 1], g_pre[:, :], ALU.mult,
                                                ALU.mult), "xn_done", 4 * q + t + 1)

            def nT_low(q, t):
                for b, bank in enumerate(xT_banks(q, t)):
                    dve.wait_ge(S["nhi_done"], 8 * q + 2 * t + b + 1)
                    signal(dve.tensor_tensor(nT_lo[:, 4 * b:4 * b + 4, tok(t)],
                                             bank.rearrange("p (k n) -> p k n", k=4),
                                             nT_hi[:, 4 * b:4 * b + 4, tok(t)].bitcast(F32), ALU.subtract),
                           "nlo_done", 8 * q + 2 * t + b + 1)

            def output_norm(r, phase, name, n, q):
                U = PLAN[name]
                dve.wait_ge(S["units_done"], U + n // 2)
                for t in range(TT):
                    signal(dve.tensor_copy(y0[:, t, :], B[t][:, :]), "y0_done", 4 * r + t + 1)
                dve.wait_ge(S["gpost_in"], 16 * (r + 1))

                def update(t):
                    dve.wait_ge(S["ystd_done"], 4 * r + t + 1)
                    link(dve.reciprocal(yst[:, 2, t:t + 1], yst[:, 1, t:t + 1]))
                    halves = (y0[:, t, :], slice(0, HALF)), (A[t], slice(HALF, D))
                    for y, cols in halves:
                        chain.step(dve.scalar_tensor_tensor(y, y, yst[:, 2, t:t + 1], g_post[:, cols], ALU.mult,
                                                            ALU.mult))
                    chain.wait(1)
                    chain.step(dve.tensor_tensor(x[:, t, 0:HALF], x[:, t, 0:HALF], y0[:, t, :], ALU.add))
                    chain.wait(1)
                    dve.tensor_tensor(x[:, t, HALF:D], x[:, t, HALF:D], A[t], ALU.add).then_inc(S["x_updated"], 1)
                    chain.wait(0)
                    dve.wait_ge(S["x_updated"], 4 * phase + t + 1)
                update(0)
                prepare(q, 0)
                for t in range(1, TT):
                    update(t)
                    nT_low(q, t - 1)
                    prepare(q, t)
                nT_low(q, TT - 1)

            def rope(bank, dst, name, value, rows=slice(0, P), tmp=None):
                s_, a_, b_ = tmp
                chain.step(dve.tensor_tensor(a_, bank[rows, :], cosT[rows, :], ALU.mult))
                link(dve.stream_shuffle(s_, bank[rows, :], [(n + 16) % 32 for n in range(32)]))
                link(dve.tensor_tensor(b_, s_, sinT[rows, :], ALU.mult))
                signal(dve.tensor_tensor(dst, a_, b_, ALU.add), name, value)

            def mlp(layer, name):
                U = PLAN[name]
                del U

                def pair(i, p):
                    j = 2 * i + p

                    def taps(v, dst, bank):
                        f = j + v * FT
                        dve.wait_ge(S["aff_done"], 2 * FT * layer + 2 * j + v + 1)
                        link(dve.scalar_tensor_tensor(dst[:, 1:SEQ], bank[:, 0:SEQ - 1], conv[:, bass.ds(4 * f + 1, 1)],
                                                      dst[:, 1:SEQ], ALU.mult, ALU.add))
                        last = dve.scalar_tensor_tensor(dst[:, 2:SEQ], bank[:, 0:SEQ - 2], conv[:, bass.ds(4 * f, 1)],
                                                        dst[:, 2:SEQ], ALU.mult, ALU.add)
                        signal(last, ("gateconv_done", "conv_done")[v], FT * layer + j + 1)
                    taps(0, y0[:, p, :], A[2 * p])
                    taps(1, y0[:, 2 + p, :], A[2 * p + 1])
                    dve.wait_ge(S["gelu_done"], FT * layer + j + 1)
                    signal(dve.tensor_tensor(y0[:, 2 + p, :], y0[:, 2 + p, :], y0[:, p, :], ALU.mult), "h_done",
                           FT * layer + j + 1)
                    dve.wait_ge(S["hhi_done"], FT * layer + j + 1)
                    signal(dve.tensor_tensor(hT_lo[:, bass.ds(j, 1), :].rearrange("p a n -> p (a n)"), y0[:, 2 + p, :],
                                             hT_hi[:, bass.ds(j, 1), :].rearrange("p a n -> p (a n)").bitcast(F32),
                                             ALU.subtract), "hlo_done", FT * layer + j + 1)
                dve.wait_ge(S["conv_in"], 16 * (layer + 1))
                with chain.loop(0, FT // 2, 4) as i:
                    for p in range(2):
                        pair(i, p)

            def embed(layer, q, phase):
                Up = PLAN[f"ple{layer}"]
                dve.wait_ge(S["pehi_done"], layer + 1)
                signal(dve.tensor_tensor(pe_lo[:, :, :], pe_raw[:, :, :], pe_hi[:, :, :].bitcast(F32), ALU.subtract),
                       "pelo_done", layer + 1)
                dve.wait_ge(S["units_done"], Up + 1)
                for t in range(TT):
                    dve.wait_ge(S["sig_done"], 8 * layer + t + 1)
                    link(dve.tensor_tensor(sg[:, t, :], sg[:, t, :], B[t][:, :], ALU.mult))
                    signal(dve.tensor_tensor(x[:, t, 0:HALF], x[:, t, 0:HALF], sg[:, t, :], ALU.add), "xhalf_done",
                           4 * layer + t + 1)
                dve.wait_ge(S["units_done"], Up + 2)

                def second(t):
                    dve.wait_ge(S["sig_done"], 8 * layer + 4 + t + 1)
                    link(dve.tensor_tensor(sg[:, t, :], sg[:, t, :], A[t][:, :], ALU.mult))
                    signal(dve.tensor_tensor(x[:, t, HALF:D], x[:, t, HALF:D], sg[:, t, :], ALU.add), "x_updated",
                           4 * phase + t + 1)
                if layer == LAYERS - 1:
                    for t in range(TT):
                        second(t)
                    return
                second(0)
                prepare(q, 0)
                for t in range(1, TT):
                    second(t)
                    nT_low(q, t - 1)
                    prepare(q, t)
                nT_low(q, TT - 1)

            dve.memset(eps[:, :], EPS).then_inc(S["consts_ready"], 1)
            dve.wait_ge(S["consts_in"], 16)
            dve.tensor_copy(ident[:, :], const[:, C_IDENT:C_IDENT + P]).then_inc(S["consts_ready"], 1)
            dve.tensor_copy(ident_b[:, :], const[:, C_IDENT:C_IDENT + P]).then_inc(S["consts_ready"], 1)
            dve.tensor_copy(causal_b[:, :], const[:, C_CAUSAL:C_CAUSAL + P]).then_inc(S["consts_ready"], 1)
            dve.wait_ge(S["consts_ready"], 4)
            for t in range(TT):
                prepare(0, t)
                if t:
                    nT_low(0, t - 1)
            nT_low(0, 3)
            dve.wait_ge(S["pos_in"], 16)
            link(dve.tensor_copy(ang[:, :], pos_i[:, :]))
            link(dve.tensor_scalar(ang[:, :], ang[:, :], const[:, C_INV:C_INV + 1], None, ALU.mult))
            for n, (r, shift) in enumerate(((red, 0.0), (turn, 0.25))):
                k = cosT if n == 0 else ang
                k = cosT
                link(dve.tensor_scalar(k[:, :], ang[:, :], 1.0 / TWO_PI, shift, ALU.mult, ALU.add))
                link(dve.tensor_scalar(k[:, :], k[:, :], ROUND, None, ALU.add))
                link(dve.tensor_scalar(k[:, :], k[:, :], ROUND, None, ALU.subtract))
                link(dve.scalar_tensor_tensor(r[:, :], k[:, :], -PI_1, ang[:, :], ALU.mult, ALU.add))
                link(dve.scalar_tensor_tensor(r[:, :], k[:, :], -PI_2, r[:, :], ALU.mult, ALU.add))
                link(dve.scalar_tensor_tensor(r[:, :], k[:, :], -PI_3, r[:, :], ALU.mult, ALU.add))
                link(dve.tensor_scalar(r[:, :], r[:, :], shift * TWO_PI, None, ALU.add))
                signal(dve.tensor_scalar(r[:, :], r[:, :], PI_MAX, -PI_MAX, ALU.min, ALU.max), "rope_in", n + 1)
            dve.wait_ge(S["lamv_in"], 16)
            dve.wait_ge(S["sub_in"], 16)
            for n in range(2):
                link(dve.tensor_tensor(lam_p[:, n, :], lam_v[:, 2 * n, :], lam_v[:, 2 * n + 1, :], ALU.mult))
            signal(dve.tensor_reduce(lam[:, 0:2], lam_p[:, :, :], AX.X, ALU.add), "lam_sum", 1)
            dve.wait_ge(S["lam_exp"], 1)
            link(dve.tensor_tensor(neg_lam[:, :], lam[:, 3:4], lam[:, 2:3], ALU.subtract))
            link(dve.tensor_scalar(neg_lam[:, :], neg_lam[:, :], -LAMBDA_INIT, None, ALU.add))
            signal(dve.tensor_scalar(subg[:, :], subg[:, :], 1.0 - LAMBDA_INIT, None, ALU.mult), "lam_ready", 1)
            dve.wait_ge(S["rope_tab"], 2)

            for half in range(2):
                dve.wait_ge(S["units_done"], PLAN["v"] + 4 * (half + 1))
                for t in range(TT):
                    signal(dve.tensor_copy(V[:, t, half * HALF:(half + 1) * HALF], (A, B)[half][t][:, :]), "v_done",
                           4 * half + t + 1)

            def maxima(qt, b, scores, negmax, step):
                n = (qt + 1) * P
                dve.wait_ge(S[scores], 2 * step + 2)
                link(dve.tensor_reduce(mx[:, qt, :], banks_b[:, b:b + 2, 0:n], AX.X, ALU.max))
                signal(dve.tensor_scalar(nm[:, qt, :], mx[:, qt, :], -SCALE, None, ALU.mult), negmax, step + 1)

            def mix(h, p, qt):
                n = (qt + 1) * P
                dve.wait_ge(S["probs_done"], 8 * h + 2 * qt + 2)
                link(dve.tensor_scalar(st1[:, 0:1], sums[:, p, qt, 1:2], 1e-30, None, ALU.max))
                link(dve.reciprocal(st1[:, 1:2], st1[:, 0:1]))
                link(dve.scalar_tensor_tensor(st1[:, 2:3], sums[:, p, qt, 0:1], neg_lam[:, :], st1[:, 1:2],
                                              ALU.mult, ALU.mult))
                if not (isinstance(h, int) and h == 0 and qt < 2):
                    dve.wait_ge(S["mixT_done"], 4 * h + qt - 1)
                signal(dve.scalar_tensor_tensor(amix[:, qt % 2, 0:n], pr[:, qt % 2, 1, 0:n], st1[:, 2:3],
                                                pr[:, qt % 2, 0, 0:n], ALU.mult, ALU.add),
                       "mix_done", 4 * h + qt + 1)

            def o_variance(h, p):
                dve.wait_ge(S["oraw_done"], h + 1)
                chain.step(dve.tensor_reduce(osum[:, 0, :], o_sq[:, :, :], AX.X, ALU.add))
                link(dve.tensor_scalar(osum[:, 1, :], sums[:, p, :, 0], 1e-30, None, ALU.max))
                link(dve.scalar_tensor_tensor(osum[:, 1, :], osum[:, 1, :], EPS, osum[:, 1, :], ALU.mult, ALU.mult))
                link(dve.scalar_tensor_tensor(osum[:, 0, :], osum[:, 0, :], 1.0 / P, osum[:, 1, :], ALU.mult,
                                              ALU.add))
                y = osum[:, 2, :].bitcast(I32)
                link(dve.tensor_scalar(y, osum[:, 0, :].bitcast(I32), 1, None, ALU.arith_shift_right))
                signal(dve.tensor_scalar(y, y, -1.0, float(0x5F3759DF), ALU.mult, ALU.add), "ovar_done", h + 1)

            def o_normed(h):
                dve.wait_ge(S["orinv_done"], h + 1)
                signal(dve.tensor_tensor(o_nrm[:, :, :], o_raw[:, :, :],
                                         osum[:, 2, :].unsqueeze(2).broadcast_to([P, TT, P]), ALU.mult),
                       "onrm_done", h + 1)

            def oT_low(h):
                dve.wait_ge(S["oThi_done"], h + 1)
                signal(dve.scalar_tensor_tensor(
                    oT0_lo[:, bass.ds(h, 1), :].rearrange("p a n -> p (a n)"), A[2][:, :], subg[:, :],
                    oT0_hi[:, bass.ds(h, 1), :].rearrange("p a n -> p (a n)").bitcast(F32), ALU.mult, ALU.subtract),
                    "oTlo_done", h + 1)

            def head_rope(h, p, k):
                dve.wait_ge(S["units_done"], PLAN["qk"] + 2 * h + k + 1)
                rope(A[k], (qT, kT)[k][p][:, :], "rope_done", 2 * h + k + 1, tmp=(sh[:, :], t1[:, :], t2[:, :]))

            def head(h, p, first=False, last=False):
                maxima(0, 0, "scores_done", "negmax_done", 4 * h)
                maxima(1, 2, "scores_done", "negmax_done", 4 * h + 1)
                mix(h, p, 0)
                mix(h, p, 1)
                maxima(2, 0, "scores_done", "negmax_done", 4 * h + 2)
                if not first:
                    o_variance(h - 1, 1 - p)
                mix(h, p, 2)
                maxima(3, 2, "scores_done", "negmax_done", 4 * h + 3)
                if not last:
                    head_rope(h + 1, 1 - p, 0)
                if not first:
                    o_normed(h - 1)
                mix(h, p, 3)
                if not first:
                    oT_low(h - 1)
                if not last:
                    head_rope(h + 1, 1 - p, 1)

            head_rope(0, 0, 0)
            head_rope(0, 0, 1)
            head(0, 0, first=True)
            with chain.loop(0, (DIFF_HEADS - 2) // 2, 2 * (4 + 12 + 6 + 5)) as i:
                for p in range(2):
                    head(2 * i + (p + 1), (p + 1) % 2)
            head(DIFF_HEADS - 1, 1, last=True)
            o_variance(DIFF_HEADS - 1, 1)
            o_normed(DIFF_HEADS - 1)
            oT_low(DIFF_HEADS - 1)

            output_norm(0, 0, "out0", 8, 1)
            mlp(0, "up0")
            output_norm(1, 1, "down0", FT, 2)
            embed(0, 3, 2)

            dve.wait_ge(S["cmpw_in"], 48)
            link(dve.memset(hid_k[:, :, N_CMP:N_PAD], 0.0))
            link(dve.memset(hid_v[:, :, N_CMP:N_PAD], 0.0))
            signal(dve.memset(Vblk[:, :, :], 0.0), "pad_ready", 1)
            for g in range(GROUPS):
                dve.wait_ge(S["units_done"], PLAN["cmp"] + g + 1)
                keys, values = slice(0, HEAD), slice(HEAD, P)
                link(dve.stream_shuffle(ksh[:, :], A[g][keys, :], [(n + 16) % 32 for n in range(32)]))
                link(dve.tensor_tensor(kt1[:, :], A[g][keys, :], cosT[keys, :], ALU.mult))
                link(dve.tensor_tensor(kt2[:, :], ksh[:, :], sinT[keys, :], ALU.mult))
                link(dve.tensor_tensor(kr[:, :], kt1[:, :], kt2[:, :], ALU.add))
                for rows, src in ((keys, kr), (values, A[g])):
                    for m in range(CMP_LEN // CMP_STRIDE):
                        win = (src[:, :] if rows is keys else src[rows, :]).rearrange("p (n l) -> p n l", l=CMP_STRIDE)
                        ls = slice(m * CMP_STRIDE, (m + 1) * CMP_STRIDE)
                        signal(dve.tensor_tensor(
                            zb[rows, g, :, ls], win[:, m:m + N_CMP, :],
                            cpos[rows, ls].unsqueeze(1).broadcast_to([HEAD, N_CMP, CMP_STRIDE]), ALU.add),
                            "zb_done", 4 * g + 2 * (rows is values) + m + 1)
            dve.wait_ge(S["cm_in"], 16)
            link(dve.tensor_scalar(cm[:, 1, :], cm[:, 0, :], -MASKED, MASKED, ALU.mult, ALU.add))

            def goT_low(pair, m):
                dve.wait_ge(S["goThi_done"], pair + 1)
                signal(dve.tensor_tensor(
                    oT1_lo[:, bass.ds(pair, 1), :].rearrange("p a n -> p (a n)"), A[2 + m],
                    oT1_hi[:, bass.ds(pair, 1), :].rearrange("p a n -> p (a n)").bitcast(F32), ALU.subtract),
                    "goTlo_done", pair + 1)

            def group(g, first):
                def step(h, k):
                    return 16 * g + 4 * h + k

                U = PLAN["group"]
                tmp = (gsh[:, :], gt1[:, :], gt2[:, :])
                flat = "p t h n -> p (t h) n"
                seq = [(h, k) for h in range(GHEADS) for k in range(TT)]

                def over_heads(mask):
                    return mask.rearrange("p (t n) -> p t n", t=TT)

                def gmaxima(h, k):
                    maxima(ORDER[k], 2 * (k % 2), "gscores_done", "gnegmax_done", step(h, k))

                def gp_turned(h, k):
                    n = (ORDER[k] + 1) * P
                    dve.wait_ge(S["gT_done"], 2 * step(h, k) + 2)
                    signal(dve.tensor_copy(gpT[:, k % 2, 1, 0:n], A[3][:, 0:n]), "gpTv_done", step(h, k) + 1)

                def post(h):
                    link(dve.tensor_scalar(st2[:, 0, :, :], sums[:, h % 2, :, :], 1e-30, None, ALU.max))
                    link(dve.reciprocal(st2[:, 1, :, :], st2[:, 0, :, :]))
                    link(dve.tensor_tensor(st2[:, 0, :, :], st2[:, 1, :, :], gates[:, :, bass.ds(12 * g + (3 * h + 1), 2)],
                                           ALU.mult))
                    dve.wait_ge(S["gpv_done"], step(h, TT - 1) + 1)
                    og4 = og[:, :, :].rearrange("p t (b n) -> p b t n", b=2)
                    for c in range(2):
                        ins = dve.tensor_tensor(og4[:, c, :, :], A[c].rearrange("p (t n) -> p t n", t=TT)[:, :, 0:HEAD],
                                                st2[:, 0, :, c].unsqueeze(2).broadcast_to([P, TT, HEAD]), ALU.mult)
                        signal(ins, "oread_done", 8 * g + 2 * h + c + 1)
                    link(dve.tensor_tensor(og[:, :, 0:HEAD], og[:, :, 0:HEAD], og[:, :, HEAD:P], ALU.add))
                    dst = opair[:, h // 2, :].rearrange("p (t n) -> p t n", t=TT)
                    signal(dve.tensor_tensor(dst[:, :, HEAD * (h % 2):HEAD * (h % 2) + HEAD], og[:, :, 0:HEAD],
                                             oc[:, :, h, :], ALU.add), "opair_done", 4 * g + h + 1)

                for n, dst in enumerate((Qa[0], Qa[1], KK)):
                    dve.wait_ge(S["units_done"], U + 4 * g + (n + 1))
                    rope(B[n], dst[:, :], "groupkv_done", 3 * g + n + 1, tmp=tmp)
                    if n == 0 and not first:
                        for m in range(2):
                            goT_low(2 * g - 2 + m, m)
                dve.wait_ge(S["csc_done"], g + 1)
                s4 = A[1].rearrange("p (t h n) -> p t h n", t=TT, h=GHEADS)
                for h in range(GHEADS):
                    chain.step(dve.tensor_tensor(sc[:, :, h, :], s4[:, :, h, :], over_heads(cm[:, 1, :]), ALU.add))
                chain.wait(0)
                link(dve.tensor_reduce(cst[:, 0, :], sc[:, :, :, :].rearrange(flat), AX.X, ALU.max))
                signal(dve.tensor_tensor(sc[:, :, :, :].rearrange(flat), sc[:, :, :, :].rearrange(flat),
                                         cst[:, 0, :].unsqueeze(2).broadcast_to([P, TT * GHEADS, N_PAD]), ALU.subtract),
                       "cexp_in", g + 1)
                gmaxima(*seq[0])
                dve.wait_ge(S["cexp_done"], g + 1)
                for h in range(GHEADS):
                    chain.step(dve.tensor_tensor(pc[:, :, h, :], pc[:, :, h, :], over_heads(cm[:, 0, :]), ALU.mult))
                chain.wait(0)
                signal(dve.tensor_reduce(cst[:, 1, :], pc[:, :, :, :].rearrange(flat), AX.X, ALU.add), "cp_done",
                       g + 1)
                link(dve.tensor_scalar(cst[:, 1, :], cst[:, 1, :], 1e-30, None, ALU.max))
                link(dve.reciprocal(cst[:, 2, :], cst[:, 1, :]))
                for t in range(TT):
                    ts_ = slice(t * GHEADS, (t + 1) * GHEADS)
                    chain.step(dve.tensor_tensor(
                        cst[:, 2, ts_], cst[:, 2, ts_],
                        gates[:, t, bass.ds(12 * g, 12)].rearrange("p (h b) -> p h b", b=3)[:, :, 0], ALU.mult))
                chain.wait(0)
                gmaxima(*seq[1])

                def blocks_out(m):
                    dve.wait_ge(S["coc_done"], 2 * g + m + 1)
                    src = A[1 - m].rearrange("p (th n) -> p th n", n=HEAD)
                    dst = oc[:, 2 * m:2 * m + 2, :, :].rearrange("p t h n -> p (t h) n")
                    signal(dve.tensor_tensor(
                        dst, src, cst[:, 2, 8 * m:8 * m + 8].unsqueeze(2).broadcast_to([P, 8, HEAD]), ALU.mult),
                        "oc_done", 2 * g + m + 1)

                blocks_out(0)
                for n, (h, k) in enumerate(seq):
                    gp_turned(h, k)
                    if n + 2 < len(seq):
                        gmaxima(*seq[n + 2])
                    if n == 0:
                        blocks_out(1)
                    if h and k == 0:
                        post(h - 1)
                post(GHEADS - 1)

            group(0, True)
            with chain.loop(1, GROUPS, 3 * 3 + 4 + 1 + 4 + 2 + TT + 16 + 4 * 4) as g:
                group(g, False)
            for m in range(2):
                goT_low(2 * GROUPS - 2 + m, m)

            output_norm(2, 3, "out1", 8, 4)
            mlp(1, "up1")
            output_norm(3, 4, "down1", FT, 5)
            embed(1, None, 5)

        @block.tensor
        def _(pe):
            def weights(u, u0=None):
                pe.wait_ge(S["w_lo_done"], u)

            def transpose(dst, src):
                return pe.matmul(dst, src, ident[:, :], start=True, stop=True, is_transpose=True)

            def transposes(q, t):
                pe.wait_ge(S["xn_done"], 4 * q + t + 1)
                if q and t:
                    pe.wait_ge(S["nlo_done"], 8 * q + 2 * t)
                for b, bank in enumerate(xT_banks(q, t)):
                    for k in range(4):
                        m = transpose(bank[:, k * P:(k + 1) * P], normed(q, t)[:, (4 * b + k) * P:(4 * b + k + 1) * P])
                    m.then_inc(S["xT_done"], 1)

            def features(bank, slot, rhs_hi, rhs_lo, part=None, cols=slice(0, SEQ)):
                steps = [(k, pas) for k in range(KT) for pas in range(3)]
                if part is not None:
                    steps = steps[8 * part:8 * part + 8]
                for k, pas in steps:
                    w = (w_hi, w_hi, w_lo)[pas][slot]
                    r = (rhs_hi, rhs_lo, rhs_hi)[pas]
                    m = pe.matmul(bank[:, cols], w[:, k * P:(k + 1) * P], r[:, k, cols], start=(k, pas) == (0, 0),
                                  stop=(k, pas) == (KT - 1, 2))
                return m

            def tokens(bank, slot, c, lhs_hi, lhs_lo, kk, t, n_k):
                for pas in range(3):
                    w = (w_hi, w_lo, w_hi)[pas][slot]
                    a = (lhs_hi, lhs_hi, lhs_lo)[pas]
                    m = pe.matmul(bank[:, :], a[:, kk, tok(t)], w[:, c * HALF:(c + 1) * HALF],
                                  start=(kk, pas) == (0, 0), stop=(kk, pas) == (n_k - 1, 2))
                return m

            def by_unit(U, units, banks, lhs_hi, lhs_lo, n_k, before=None):
                for n in units:
                    weights(U + n + 1)
                    if before:
                        before(n)
                    of_tiles(U, n, range(TT), banks, lhs_hi, lhs_lo, n_k).then_inc(S["units_done"], 1)

            def of_tiles(U, n, tiles, banks, lhs_hi, lhs_lo, n_k):
                for c in range(2):
                    kk = 2 * n + c - (n_k if 2 * n >= n_k else 0)
                    for t in tiles:
                        m = tokens(banks[t], (U + n) % RING, c, lhs_hi, lhs_lo, kk, t, n_k)
                return m

            def by_tile(U, units, banks, lhs_hi, lhs_lo, n_k, within, free=None):
                for t in range(TT):
                    if free:
                        free(t)
                    for n in units:
                        if t == 0:
                            weights(U + n + 1)
                        if n == units[2]:
                            within(t)
                        m = of_tiles(U, n, (t,), banks, lhs_hi, lhs_lo, n_k)
                        if t == TT - 1:
                            m.then_inc(S["units_done"], 1)
                    if t < TT - 1:
                        m.then_inc(S["tile_done"], 1)

            def cross(U, q, part):
                pe.wait_ge(S["nlo_done"], 8 * q + 4)
                weights(U + 1)
                part(0, 0)
                transposes(q, 2)
                weights(U + 2)
                part(1, 0)
                transposes(q, 3)
                weights(U + 3)
                part(2, 0)
                pe.wait_ge(S["nlo_done"], 8 * q + 8)
                for n in range(3):
                    part(n, 1).then_inc(S["units_done"], 1)

            def feature_part(U):
                return lambda n, m: features(A[n], (U + n) % RING, nT_hi, nT_lo, cols=slice(256 * m, 256 * m + 256))

            def feature_start(U, q):
                cross(U, q, feature_part(U))
                weights(U + 4)
                features(A[3], (U + 3) % RING, nT_hi, nT_lo).then_inc(S["units_done"], 1)

            def output(U, n, q, lhs_hi, lhs_lo, n_k, r, before=None):
                by_unit(U, range(n // 2), B, lhs_hi, lhs_lo, n_k, before)
                by_unit(U, range(n // 2, n - 4), A, lhs_hi, lhs_lo, n_k)

                def within(t):
                    if t >= 2:
                        if t == 2:
                            pe.wait_ge(S["y0_done"], 4 * r + 4)
                        transposes(q, t - 2)
                by_tile(U, range(n - 4, n), A, lhs_hi, lhs_lo, n_k, within)

            def mlp(layer, name, q):
                U = PLAN[name]
                feature_start(U, q)
                with pe.Fori(1, FT // 2) as i:
                    for p in range(2):
                        pe.wait_ge(S["conv_done"], FT * layer + 2 * i + (p - 1))
                        for v in range(2):
                            weights(U + (2 * p + v + 1) + 4 * i)
                            features(A[2 * p + v], (U + 2 * p + v) % RING, nT_hi, nT_lo).then_inc(S["units_done"], 1)

            def down(layer, name, q, r):
                def hidden(n):
                    pe.wait_ge(S["hlo_done"], FT * layer + min(2 * n + 2, FT))
                output(PLAN[name], FT, q, hT_hi, hT_lo, FT, r, hidden)

            def embed(layer, q, after_q):
                Ua, Up, Ub = PLAN[f"gate{layer}a"], PLAN[f"ple{layer}"], PLAN[f"gate{layer}b"]
                cross(Ua, after_q, lambda n, m: of_tiles(Ua, n, (2 * m, 2 * m + 1), A, nT_hi, nT_lo, KT))
                by_unit(Ua, (3,), A, nT_hi, nT_lo, KT)
                pe.wait_ge(S["pelo_done"], layer + 1)
                for half, banks in enumerate((B, A)):
                    weights(Up + half + 1)
                    for t in range(TT):
                        if half:
                            pe.wait_ge(S["sig_done"], 8 * layer + t + 1)
                        for c in range(2):
                            m = tokens(banks[t], (Up + half) % RING, c, pe_hi, pe_lo, c, t, 2)
                    m.then_inc(S["units_done"], 1)

                def free(t):
                    pe.wait_ge(S["xhalf_done"], 4 * layer + t + 1)

                def within(t):
                    if q is not None and t >= 2:
                        if t == 2:
                            pe.wait_ge(S["sig_done"], 8 * layer + 6)
                        transposes(q, t - 2)
                by_tile(Ub - 4, range(4, 8), B, nT_hi, nT_lo, KT, within, free)

            pe.wait_ge(S["consts_ready"], 4)
            for t in range(TT + 1):
                if t < TT:
                    transposes(0, t)
                if t:
                    pe.wait_ge(S["nlo_done"], 2 * t)
                    if t == 1:
                        weights(PLAN["v"] + 2)
                    for n in range(2):
                        m = of_tiles(PLAN["v"], n, (t - 1,), A, nT_hi, nT_lo, KT)
                        if t == TT:
                            m.then_inc(S["units_done"], 1)
            by_unit(PLAN["v"], range(2, 4), A, nT_hi, nT_lo, KT)
            by_unit(PLAN["v"], range(4, 8), B, nT_hi, nT_lo, KT)

            def project(h, part, p, U0):
                k = part // 3
                if part % 3 == 0:
                    pe.wait_ge(S["w_lo_done"], PLAN["qk"] + 2 * h + k + 1)
                    if not (isinstance(h, int) and h == 0):
                        pe.wait_ge(S["rope_done"], 2 * h + k - 1)
                m = features(A[k], (PLAN["qk"] + 2 * p + k) % RING, nT_hi, nT_lo, part % 3)
                if part % 3 == 2:
                    m.then_inc(S["units_done"], 1)

            def scores(h, p, qt):
                n = (qt + 1) * P
                if not (isinstance(h, int) and h == 0 and qt < 2):
                    pe.wait_ge(S["probs_done"], 8 * h + 2 * qt - 2)
                for c in range(2):
                    rows = slice(HEAD * c, HEAD * c + HEAD)
                    pe.matmul(B[2 * (qt % 2) + c][:, 0:n], qT[p][rows, tok(qt)], kT[p][rows, 0:n], start=True,
                              stop=False)
                for c in range(2):
                    pe.matmul(B[2 * (qt % 2) + c][:, n - P:n], ident_b[:, :], causal_b[:, :], start=False,
                              stop=True).then_inc(S["scores_done"], 1)

            def turn_mix(h, qt):
                pe.wait_ge(S["mix_done"], 4 * h + qt + 1)
                if not (isinstance(h, int) and h == 0 and qt == 0):
                    pe.wait_ge(S["pT_done"], 4 * h + qt)
                for kb in range(qt + 1):
                    m = transpose(A[2][:, kb * P:(kb + 1) * P], amix[:, qt % 2, kb * P:(kb + 1) * P])
                m.then_inc(S["mixT_done"], 1)

            def values(h, qt):
                pe.wait_ge(S["pT_done"], 4 * h + qt + 1)
                if qt == 0 and not (isinstance(h, int) and h == 0):
                    pe.wait_ge(S["oraw_done"], h)
                for kb in range(qt + 1):
                    m = pe.matmul(A[3][:, tok(qt)], pT[:, qt % 2, kb * P:(kb + 1) * P],
                                  V[:, kb, bass.ds(h * P, P)], start=kb == 0, stop=kb == qt)
                m.then_inc(S["pv_done"], 1)

            def turn_o(h):
                pe.wait_ge(S["onrm_done"], h + 1)
                for t in range(TT):
                    m = transpose(A[2][:, tok(t)], o_nrm[:, t, :])
                m.then_inc(S["oT_done"], 1)

            def head(h, p, first=False, last=False):
                def proj(*parts):
                    if not last:
                        for part in parts:
                            project(h + 1, part, 1 - p, None)
                pe.wait_ge(S["rope_done"], 2 * h + 2)
                scores(h, p, 0)
                scores(h, p, 1)
                proj(0)
                turn_mix(h, 0)
                scores(h, p, 2)
                proj(1)
                values(h, 0)
                turn_mix(h, 1)
                scores(h, p, 3)
                proj(2)
                values(h, 1)
                turn_mix(h, 2)
                proj(3)
                if not first:
                    pe.wait_ge(S["pT_done"], 4 * h + 3)
                    turn_o(h - 1)
                proj(4, 5)
                if not first:
                    pe.wait_ge(S["oTlo_done"], h)
                turn_mix(h, 3)
                values(h, 2)
                values(h, 3)

            pe.wait_ge(S["v_done"], 4)
            for part in range(6):
                project(0, part, 0, None)
            pe.wait_ge(S["v_done"], 8)
            head(0, 0, first=True)
            with pe.Fori(0, (DIFF_HEADS - 2) // 2) as i:
                for p in range(2):
                    head(2 * i + (p + 1), (p + 1) % 2)
            head(DIFF_HEADS - 1, 1, last=True)

            def last_head(n):
                if n == 2:
                    turn_o(DIFF_HEADS - 1)
                if n == 3:
                    pe.wait_ge(S["oTlo_done"], DIFF_HEADS)
            output(PLAN["out0"], 8, 1, oT0_hi, oT0_lo, KT, 0, last_head)
            mlp(0, "up0", 1)
            down(0, "down0", 2, 1)
            embed(0, 3, 2)

            feature_start(PLAN["cmp"], 3)
            U = PLAN["branch"]
            weights(U + 1)
            slot = U % RING
            for t in range(TT):
                for k in range(KT):
                    for pas in range(3):
                        w = (w_hi, w_lo, w_hi)[pas][slot]
                        a = (nT_hi, nT_hi, nT_lo)[pas]
                        m = pe.matmul(B[2][:, 48 * t:48 * t + 48], a[:, k, tok(t)], w[:, k * P:k * P + 48],
                                      start=(k, pas) == (0, 0), stop=(k, pas) == (KT - 1, 2))
            m.then_inc(S["units_done"], 1)
            pe.wait_ge(S["cmpw_in"], 48)
            pe.wait_ge(S["zb_done"], 4 * GROUPS)
            for el in range(CMP_LEN):
                for kv in range(2):
                    rows = slice(HEAD * kv, HEAD * kv + HEAD)
                    m = pe.matmul(B[kv][:, 0:GROUPS * N_CMP], w1[rows, el, :], zb[rows, :, :, el],
                                  start=el == 0, stop=el == CMP_LEN - 1)
                    if el == CMP_LEN - 1:
                        m.then_inc(S["hid_done"], 1)
            pe.wait_ge(S["gelc_done"], 2)
            pe.matmul(B[3][0:HEAD, 0:P], w2[:, 0, :], hid_k[:, :, :].rearrange("p g n -> p (g n)"), start=True,
                      stop=True).then_inc(S["kv_done"], 1)
            for g in range(GROUPS):
                m = pe.matmul(B[3][0:N_PAD, P + HEAD * g:P + HEAD * g + HEAD], hid_v[:, g, :], w2[:, 1, :],
                              start=True, stop=True)
            m.then_inc(S["kv_done"], 1)
            pe.wait_ge(S["kvc_done"], GHEADS)

            def gturn_o(m):
                for t in range(TT):
                    mm = transpose(A[2 + m][:, tok(t)], opair[:, m, tok(t)])
                mm.then_inc(S["goT_done"], 1)

            def group(g, first):
                def step(h, k):
                    return 16 * g + 4 * h + k

                def compressed_scores():
                    pe.wait_ge(S["gqx_done"], 2 * g + 2)
                    if not first:
                        pe.wait_ge(S["oread_done"], 8 * g)
                    for t in range(TT):
                        for h in range(GHEADS):
                            q = (Qa, Qx)[h % 2][h // 2]
                            m = pe.matmul(A[1][:, (t * GHEADS + h) * N_PAD:(t * GHEADS + h + 1) * N_PAD],
                                          q[0:HEAD, tok(t)], kcmp[:, bass.ds(g, 1), :].rearrange("p a n -> p (a n)"),
                                          start=True, stop=True)
                    m.then_inc(S["csc_done"], 1)

                def cturn():
                    pe.wait_ge(S["cp_done"], g + 1)
                    if not first:
                        pe.wait_ge(S["goTlo_done"], 2 * g)
                    for t in range(TT):
                        m = transpose(A[3][:, tok(t)], pc[:, t, :, :].rearrange("p h n -> p (h n)"))
                    m.then_inc(S["cpT_done"], 1)

                def vturn():
                    pe.wait_ge(S["vT_done"], g + 1)
                    for t in range(TT):
                        m = transpose(A[0][:, tok(t)], vT[:, tok(t)])
                    m.then_inc(S["vTt_done"], 1)

                def cvalues(m):
                    if m == 0:
                        pe.wait_ge(S["cpTc_done"], g + 1)
                    else:
                        pe.wait_ge(S["vg_done"], g + 1)
                    for t in range(2):
                        mm = pe.matmul(A[1 - m][:, 256 * t:256 * t + 256], pcT[:, 2 * m + t, :],
                                       Vblk[:, bass.ds(g, 1), :].rearrange("p a n -> p (a n)"), start=True, stop=True)
                    mm.then_inc(S["coc_done"], 1)

                def gscores(h, k):
                    qt = ORDER[k]
                    n = (qt + 1) * P
                    if (h, k) == (0, 0):
                        pe.wait_ge(S["groupkv_done"], 3 * g + 3)
                    elif (h, k) != (0, 1):
                        pe.wait_ge(S["gprobs_done"], 2 * step(h, k) - 2)
                    for c in range(2):
                        rows = slice(HEAD * c, HEAD * c + HEAD)
                        q = (Qa, Qx)[(h + c) % 2][h // 2]
                        pe.matmul(B[2 * (k % 2) + c][:, 0:n], q[rows, tok(qt)], KK[rows, 0:n], start=True, stop=False)
                    for c in range(2):
                        pe.matmul(B[2 * (k % 2) + c][:, n - P:n], ident_b[:, :], causal_b[:, :], start=False,
                                  stop=True).then_inc(S["gscores_done"], 1)

                def gturn(h, k):
                    pe.wait_ge(S["gprobs_done"], 2 * step(h, k) + 2)
                    if not (first and h == 0 and k == 0):
                        pe.wait_ge(S["gpTa_done"], step(h, k))
                        pe.wait_ge(S["gpTv_done"], step(h, k))
                    for c in range(2):
                        for kb in range(ORDER[k] + 1):
                            m = transpose(A[2 + c][:, kb * P:(kb + 1) * P], gp[:, k % 2, c, kb * P:(kb + 1) * P])
                        m.then_inc(S["gT_done"], 1)

                def gvalues(h, k):
                    qt = ORDER[k]
                    pe.wait_ge(S["gpTa_done"], step(h, k) + 1)
                    pe.wait_ge(S["gpTv_done"], step(h, k) + 1)
                    if (h, k) == (0, 0):
                        pe.wait_ge(S["oc_done"], 2 * g + 2)
                    elif k == 0:
                        pe.wait_ge(S["oread_done"], 8 * g + 2 * h)
                    for c in range(2):
                        for kb in range(qt + 1):
                            m = pe.matmul(A[c][:, tok(qt)], gpT[:, k % 2, c, kb * P:(kb + 1) * P],
                                          Vg[:, kb, HEAD * c:HEAD * c + P], start=kb == 0, stop=kb == qt)
                    m.then_inc(S["gpv_done"], 1)

                U = PLAN["group"]
                seq = [(h, k) for h in range(GHEADS) for k in range(TT)]
                for n in range(4):
                    weights(4 * g + (U + n + 1))
                    features(B[n], (U + n) % RING, nT_hi, nT_lo).then_inc(S["units_done"], 1)
                    if n == 0 and not first:
                        pe.wait_ge(S["opair_done"], 4 * g)
                        for m in range(2):
                            gturn_o(m)
                    if n == 2:
                        compressed_scores()
                        gscores(*seq[0])
                cturn()
                vturn()
                gscores(*seq[1])
                cvalues(0)
                for n, (h, k) in enumerate(seq):
                    gturn(h, k)
                    if n + 2 < len(seq):
                        gscores(*seq[n + 2])
                    if n:
                        gvalues(*seq[n - 1])
                    else:
                        cvalues(1)
                gvalues(*seq[-1])

            group(0, True)
            with pe.Fori(1, GROUPS) as g:
                group(g, False)

            def last_pairs(n):
                if n == 1:
                    pe.wait_ge(S["opair_done"], 4 * GROUPS)
                    for m in range(2):
                        gturn_o(m)
                if n == 3:
                    pe.wait_ge(S["goTlo_done"], 2 * GROUPS)
            output(PLAN["out1"], 8, 4, oT1_hi, oT1_lo, KT, 2, last_pairs)
            mlp(1, "up1", 4)
            down(1, "down1", 5, 3)
            embed(1, None, 5)


def by_features(w):
    k, n = w.shape
    return w.reshape(k // P, P, n // P, P).transpose(2, 1, 0, 3).reshape(n // P, P, D)


def by_tokens(w):
    k = w.shape[0]
    return w.reshape(k // (2 * P), 2, P, 2, HALF).transpose(3, 0, 2, 1, 4).reshape(-1, P, D)


def rotary(w):
    k, n = w.shape
    return w.reshape(k, n // HEAD, 2, 2, 16).transpose(0, 1, 3, 2, 4).reshape(k, n)


def pack(i):
    H = 2 * DIFF_HEADS * HEAD
    dw = i["diff_w_in"][0]
    units = [by_tokens(dw[:, 2 * H:])]
    q, k = by_features(rotary(dw[:, :H])), by_features(rotary(dw[:, H:2 * H]))
    units.append(np.stack([q, k], 1).reshape(-1, P, D))
    nw = i["nsa_w_in"][0]
    kv = GROUPS * HEAD
    at = D + kv * np.arange(7)
    part = {n: nw[:, at[j]:at[j + 1]] for j, n in enumerate(("kc", "vc", "ks", "vs", "kw", "vw"))}
    for n in ("kc", "ks", "kw"):
        part[n] = rotary(part[n])
    pair = lambda a, b, g: np.concatenate([part[a][:, g * HEAD:(g + 1) * HEAD], part[b][:, g * HEAD:(g + 1) * HEAD]], 1)
    for layer in range(LAYERS):
        if layer == 1:
            units += [by_features(pair("kc", "vc", g)) for g in range(GROUPS)]
            wide = np.zeros((D, P), np.float32)
            wide[:, :3 * D // HEAD] = nw[:, at[6]:]
            units.append(by_features(wide))
            nq = by_features(rotary(nw[:, :D]))
            for g in range(GROUPS):
                units += [nq[2 * g:2 * g + 2], by_features(pair("ks", "kw", g)), by_features(pair("vs", "vw", g))]
        units.append(by_tokens((i["diff_w_out"], i["nsa_w_out"])[layer][0]))
        up = by_features(i["ffn_w_up"][layer])
        units.append(np.stack([up[:FT], up[FT:]], 1).reshape(-1, P, D))
        units.append(by_tokens(i["ffn_w_down"][layer]))
        gate = by_tokens(i["ple_gate_w"][layer])
        units += [gate[:4], by_tokens(i["ple_proj_w"][layer]), gate[4:]]
    return np.concatenate(units, 0)


def constants():
    c = np.zeros((P, C_ALL), np.float32)
    row = np.arange(P) % HEAD
    freq = 16 * (row // 32) + row % 16
    c[:, C_INV] = np.float32(THETA) ** (-(2 * freq).astype(np.float32) / np.float32(HEAD))
    c[:, C_SIGN] = np.where(row % 32 < 16, -1.0, 1.0)
    c[:, C_IDENT:C_IDENT + P] = np.eye(P)
    c[:, C_CAUSAL:C_CAUSAL + P] = np.where(np.arange(P)[None, :] <= np.arange(P)[:, None], 0.0, MASKED)
    t = np.arange(TT)[None, :, None] * P + np.arange(P)[:, None, None]
    last = np.arange(N_PAD) * CMP_STRIDE + CMP_LEN - 1
    ok = (last <= t) & (np.arange(N_PAD) < N_CMP)
    c[:, C_CMP:] = ok.reshape(P, TT * N_PAD)
    return c


def kernel(**inputs):
    import concourse.bacc as bacc
    from concourse.bass_utils import run_bass_kernel_spmd as run

    i = {k: np.asarray(v) for k, v in inputs.items()}
    perm = np.arange(HEAD).reshape(2, 2, 16).transpose(1, 0, 2).reshape(-1)
    gains = np.concatenate([i["norm_gains"], i["ple_norm_g"][:, None]], 1).reshape(LAYERS * GAINS, 1, D)
    taps = np.concatenate([i["ffn_conv_w"], i["ffn_conv_b"][:, None]], 1)
    arrays = {
        "x": i["x"].reshape(TT, P, D).transpose(1, 0, 2),
        "w": pack(i),
        "const": constants(),
        "gains": np.broadcast_to(gains, (LAYERS * GAINS, P, D)),
        "conv": taps.reshape(LAYERS, 4, 2 * FT, P).transpose(0, 3, 2, 1).reshape(LAYERS, P, 8 * FT),
        "subln": i["diff_subln_g"][0].reshape(P, 1),
        "lam": np.broadcast_to(np.stack([i[f"diff_lam_{n}"][0] for n in ("q1", "k1", "q2", "k2")])[None], (P, 4, HEAD)),
        "pos": np.broadcast_to(i["positions"].reshape(1, SEQ), (P, SEQ)),
        "pT": i["p"][:, 0].reshape(LAYERS, SEQ, 2, P).transpose(0, 3, 2, 1),
        "w1": np.concatenate([i["nsa_ck_w1"][0].transpose(1, 0, 2)[perm], i["nsa_cv_w1"][0].transpose(1, 0, 2)], 0),
        "cpos": np.concatenate([i["nsa_ck_pos"][0].T[perm], i["nsa_cv_pos"][0].T], 0),
        "w2": np.stack([i["nsa_ck_w2"][0][:, perm], i["nsa_cv_w2"][0]], 1),
    }
    nc = bacc.Bacc("TRN2", target_bir_lowering=False, num_devices=1)
    feeds, args = {}, []
    for name, a in arrays.items():
        feeds["in_" + name] = np.ascontiguousarray(a)
        args.append(nc.dram_tensor("in_" + name, a.shape, mybir.dt.from_np(a.dtype), kind="ExternalInput").ap())
    out = nc.dram_tensor("out", (P, TT, D), F32, kind="ExternalOutput").ap()
    trunk(nc, *args, out)
    got = run(nc, [feeds], core_ids=[0]).results[0]["out"]
    return got.transpose(1, 0, 2).reshape(1, SEQ, D)
```

```python
from contextlib import ExitStack, contextmanager
import math

import numpy as np

import concourse.bass as bass
import concourse.mybir as mybir

F32 = mybir.dt.float32
F32R = mybir.dt.float32r
BF16 = mybir.dt.bfloat16
I32 = mybir.dt.int32
ALU = mybir.AluOpType
ACT = mybir.ActivationFunctionType
AX = mybir.AxisListType

P = 128
SEQ = 512
D = 1024
TT = SEQ // P
KT = D // P
HEAD = 64
HALF = D // 2
LAYERS = 2
EPS = 1e-6
SCALE = HEAD ** -0.5
MASKED = -1e30
THETA = 10000.0

NEWTON = 3
DIFF_HEADS = D // (2 * HEAD)
LAMBDA_INIT = 0.8 - 0.6 * math.exp(-0.3 * 0)

GROUPS = 4
GHEADS = D // HEAD // GROUPS
ORDER = (0, 3, 1, 2)
CMP_LEN = 32
CMP_STRIDE = 16
N_CMP = (SEQ - CMP_LEN) // CMP_STRIDE + 1
N_PAD = 32
CMP_HIDDEN = 128

FF = 2816
FT = FF // P
PLE = 256

RING = 4
RAW = 2
PLAN, _at = {}, 0
for _name, _n in (("v", 8), ("qk", 2 * DIFF_HEADS), ("out0", 8), ("up0", 2 * FT), ("down0", FT),
                  ("gate0a", 4), ("ple0", 2), ("gate0b", 4),
                  ("cmp", GROUPS), ("branch", 1), ("group", 4 * GROUPS), ("out1", 8), ("up1", 2 * FT),
                  ("down1", FT), ("gate1a", 4), ("ple1", 2), ("gate1b", 4)):
    PLAN[_name] = _at
    _at += _n
UNITS = _at

C_INV, C_SIGN, C_IDENT, C_CAUSAL, C_CMP = 0, 1, 2, 2 + P, 2 + 2 * P
C_ALL = C_CMP + TT * N_PAD
GAINS = 5
TWO_PI = 2 * math.pi
PI_1 = 6.28125
PI_2 = float(np.float32(TWO_PI - PI_1))
PI_3 = float(np.float32(TWO_PI - PI_1 - PI_2))
ROUND = 1.5 * 2.0 ** 23
PI_MAX = float(np.nextafter(np.float32(math.pi), np.float32(0)))


class Chain:

    def __init__(self, engine, sem):
        self.engine, self.sem, self.base, self.n = engine, sem, 0, 0

    def step(self, ins):
        ins.then_inc(self.sem, 1)
        self.n += 1

    def link(self, ins):
        self.step(ins)
        self.engine.wait_ge(self.sem, self.base + self.n)

    def wait(self, last):
        self.engine.wait_ge(self.sem, self.base + self.n - last)

    @contextmanager
    def loop(self, start, end, per):
        before = self.base + self.n
        with self.engine.Fori(start, end) as i:
            self.base, self.n = before + per * (i - start), 0
            yield i
            assert self.n == per, (self.n, per)
        self.base, self.n = before + per * (end - start), 0


def trunk(nc, x_in, w_in, const_in, gain_in, conv_in, subln_in, lam_in, pos_in, pT_in, w1_in,
          cpos_in, w2_in, out):
    ctx = ExitStack()
    with ctx:
        def sb(name, shape, dt=F32, on=ctx):
            return on.enter_context(nc.sbuf_tensor(name, shape, dt))

        x = sb("x", [P, TT, D])
        nT_hi = sb("nT_hi", [P, KT, SEQ], F32R)
        nT_lo = sb("nT_lo", [P, KT, SEQ], F32R)
        w_raw = [sb(f"w_raw{i}", [P, D]) for i in range(RAW)]
        w_hi = [sb(f"w_hi{i}", [P, D], F32R) for i in range(RING)]
        w_lo = [sb(f"w_lo{i}", [P, D], F32R) for i in range(RING)]
        cosT = sb("cosT", [P, SEQ])
        sinT = sb("sinT", [P, SEQ])
        g_pre = sb("g_pre", [P, D])
        g_post = sb("g_post", [P, D])
        xn = sb("xn", [P, D])
        ident = sb("ident", [P, P])
        ident_b = sb("ident_b", [P, P], BF16)
        causal_b = sb("causal_b", [P, P], BF16)
        conv = sb("conv", [P, 4 * 2 * FT])
        eps = sb("eps", [P, 1])
        ss = sb("ss", [P, TT])
        std = sb("std", [P, TT])
        rinv = sb("rinv", [P, TT])
        yss = sb("yss", [P, 2, TT])
        yst = sb("yst", [P, 3, TT])
        subg = sb("subg", [P, 1])
        neg_lam = sb("neg_lam", [P, 1])
        lam = sb("lam", [P, 4])
        junk = sb("junk", [P, D], BF16)
        y0 = sb("y0", [P, TT, HALF])

        nm = sb("nm", [P, TT, 2])
        sums = sb("sums", [P, 2, TT, 2])
        st1 = sb("st1", [P, 4])
        osum = sb("osum", [P, 3, TT])
        coef = sb("coef", [P, 2, TT])
        st2 = sb("st2", [P, 2, TT, 2])
        cst = sb("cst", [P, 3, TT * GHEADS])

        def overlay(*parts):
            with ExitStack() as on:
                return [sb(*part, on=on) for part in parts]

        const, pos_i, ang, turn, xn0, red, lam_v, lam_p = overlay(
            ("const", [P, C_ALL], F32), ("pos_i", [P, SEQ], I32), ("ang", [P, SEQ], F32),
            ("turn", [P, SEQ], F32), ("xn0", [P, TT, D], F32), ("red", [P, SEQ], F32), ("lam_v", [P, 4, HEAD], F32), ("lam_p", [P, 2, HEAD], F32))
        (V, oT0_hi, oT0_lo, qT0, qT1, kT0, kT1, sh, t1, t2, q_sh, q_t1, pr, amix, pT, o_raw, o_nrm, o_sq) = overlay(
            ("V", [P, TT, D], F32), ("oT0_hi", [P, KT, SEQ], F32R), ("oT0_lo", [P, KT, SEQ], F32R),
            ("qT0", [P, SEQ], F32), ("qT1", [P, SEQ], F32), ("kT0", [P, SEQ], F32), ("kT1", [P, SEQ], F32),
            ("sh", [P, SEQ], F32), ("t1", [P, SEQ], F32), ("t2", [P, SEQ], F32),
            ("q_sh", [P, SEQ], F32), ("q_t1", [P, SEQ], F32),
            ("pr", [P, 2, 2, SEQ], F32), ("amix", [P, 2, SEQ], F32), ("pT", [P, 2, SEQ], F32),
            ("o_raw", [P, TT, P], F32), ("o_nrm", [P, TT, P], F32), ("o_sq", [P, TT, P], F32))
        qT, kT = [qT0, qT1], [kT0, kT1]
        hT_hi, hT_lo = overlay(("hT_hi", [P, FT, SEQ], F32R), ("hT_lo", [P, FT, SEQ], F32R))
        pe_raw, pe_hi, pe_lo, sg = overlay(
            ("pe_raw", [P, 2, SEQ], F32), ("pe_hi", [P, 2, SEQ], F32R), ("pe_lo", [P, 2, SEQ], F32R),
            ("sg", [P, TT, HALF], F32))
        keep1 = [("oT1_hi", [P, KT, SEQ], F32R), ("oT1_lo", [P, KT, SEQ], F32R),
                 ("kcmp", [P, GROUPS, N_PAD], F32), ("kc", [P, GROUPS, 2, N_PAD], F32R), ("Vblk", [P, GROUPS, GHEADS * HEAD], F32),
                 ("gates", [P, TT, 3 * D // HEAD], F32)]
        (oT1_hi, oT1_lo, kcmp, kc, Vblk, gates, w1k, w1v, KR, VR, hid_k, hid_v, w2, cbias, gT, ksh, kt1, kt2) = overlay(
            *keep1, ("w1k", [P, CMP_LEN // 2, CMP_HIDDEN], F32), ("w1v", [P, CMP_LEN // 2, CMP_HIDDEN], F32),
            ("KR", [P, GROUPS + 1, SEQ], F32), ("VR", [P, GROUPS + 1, SEQ], F32),
            ("hid_k", [P, GROUPS, N_PAD], F32), ("hid_v", [P, GROUPS, N_PAD], F32),
            ("w2", [P, 2, HEAD], F32), ("cbias", [P, 2], F32), ("gT", [P, SEQ], F32),
            ("ksh", [HEAD, SEQ], F32), ("kt1", [HEAD, SEQ], F32), ("kt2", [HEAD, SEQ], F32))
        (_, _, _, _, _, _, cm, Vg, vT, Kh, Kl, Q0, Q1, Q2, Q3, gp, gpT, sc, pc, pcT, oc,
         og) = overlay(
            *[("again_" + n, s, d) for n, s, d in keep1],
            ("cm", [P, 2, TT * N_PAD], F32),
            ("Vg", [P, TT, P + HEAD], F32), ("vT", [P, SEQ], F32),
            ("Kh", [P, 2, SEQ], F32R), ("Kl", [P, 2, SEQ], F32R),
            ("Q0", [P, SEQ], F32R), ("Q1", [P, SEQ], F32R), ("Q2", [P, SEQ], F32R), ("Q3", [P, SEQ], F32R),
            ("gp", [P, 2, 2, SEQ], F32), ("gpT", [P, 2, 2, SEQ], F32),
            ("sc", [P, TT, GHEADS, N_PAD], F32), ("pc", [P, TT, GHEADS, N_PAD], F32),
            ("pcT", [P, TT, P], F32), ("oc", [P, TT, GHEADS, HEAD], F32),
            ("og", [P, TT, P], F32))
        Q = [Q0, Q1, Q2, Q3]
        gsh, gt1 = xn[:, 0:SEQ], xn[:, SEQ:2 * SEQ]
        rot = [y0[:, 2, :], y0[:, 3, :], vT[:, :]]
        opair = y0
        banks_a = ctx.enter_context(nc.psum_tensor("banks_a", [P, 4, 512], F32))
        banks_b = ctx.enter_context(nc.psum_tensor("banks_b", [P, 4, 512], F32))
        A, B = [banks_a[:, n, :] for n in range(4)], [banks_b[:, n, :] for n in range(4)]
        names = """
        x_in0 x_in1 x_in2 x_in3 consts_in gain_in gpost_in conv_in lamv_in pos_in sub_in
        w_in0 w_in1 w_hi_done w_lo_done units_done tile_done
        consts_ready rope_in rope_tab lam_sum lam_exp lam_ready
        std_done xn_done xT_done nhi_done nlo_done x_updated
        y0_done ystd_done v_done
        qhalf_done qrope_done krope_done scores_done negmax_done probs_done mix_done mixT_done ovar_done orinv_done pT_done pv_done
        oraw_done onrm_done oT_done oThi_done oTlo_done
        aff_done gateconv_done conv_done gelu_done h_done hhi_done hlo_done
        ple_in pehi_done pelo_done sig_done xhalf_done
        cmpw_in kr_done shifted_done gsig_done gatesT_done hid_done gelc_done kv_done kvc_done kchi_done kclo_done pad_ready cm_in
        groupkv_done ghi_done glo_done gkx_done vT_done vTt_done vg_done
        csc_done cexp_in cexp_done cp_done cpT_done cpTc_done coc_done oc_done
        gscores_done gnegmax_done gprobs_done gT_done gpTa_done gpTv_done gpv_done
        oread_done opair_done goT_done goThi_done goTlo_done
        out_done chain_act chain_dve chain_pool
        """.split()
        S = {n: ctx.enter_context(nc.semaphore(n)) for n in names}
        block = ctx.enter_context(nc.Block())

        def tok(t):
            return slice(t * P, (t + 1) * P)

        def side(m):
            return slice(m * HEAD, (m + 1) * HEAD)

        def xT_banks(q, t):
            return ((A[0], A[1]), (A[2], A[3]), (B[0], B[1]), (B[2], B[3]))[t] if q == 0 else (B[0], B[1])

        def normed(q, t):
            return xn0[:, t, :] if q == 0 else xn[:, :]

        @block.sync
        def _(sp):
            for t in range(TT):
                sp.dma_start(x[:, t, :], x_in[:, t, :]).then_inc(S[f"x_in{t}"], 16)
                if t < RAW:
                    sp.dma_start(w_raw[t][:, :], w_in[t, :, :]).then_inc(S[f"w_in{t}"], 16)
            with sp.Fori(1, UNITS // RAW) as i:
                for r in range(RAW):
                    sp.wait_ge(S["w_lo_done"], i * RAW + (r + 1 - RAW))
                    sp.dma_start(w_raw[r][:, :], w_in[bass.ds(i * RAW + r, 1), :, :].rearrange("a p n -> (a p) n"))\
                        .then_inc(S[f"w_in{r}"], 16)
            for u in range(UNITS // RAW * RAW, UNITS):
                sp.wait_ge(S["w_lo_done"], u + 1 - RAW)
                sp.dma_start(w_raw[u % RAW][:, :], w_in[u, :, :]).then_inc(S[f"w_in{u % RAW}"], 16)
            for t in range(TT):
                sp.wait_ge(S["x_updated"], 4 * (3 * LAYERS - 1) + t + 1)
                sp.dma_start(out[:, t, :], x[:, t, :]).then_inc(S["out_done"], 16)
            sp.wait_ge(S["out_done"], 16 * TT)

        @block.gpsimd
        def _(pool):
            chain = Chain(pool, S["chain_pool"])
            link = chain.link
            for n, c in enumerate((-0.5, 1.5)):
                link(pool.memset(coef[:, n, :], c))

            def low(k, slot, u1):
                pool.wait_ge(S["w_hi_done"], u1)
                pool.tensor_tensor(w_lo[slot][:, :], w_raw[k % RAW][:, :], w_hi[slot][:, :].bitcast(F32),
                                   ALU.subtract).then_inc(S["w_lo_done"], 1)

            def lows(start, end):
                whole = (end - start) // RING
                with pool.Fori(0, whole) as i:
                    for k in range(RING):
                        low(start + k, (start + k) % RING, start + i * RING + (k + 1))
                for u in range(start + whole * RING, end):
                    low(u, u % RING, u + 1)

            def o_normed(h):
                pool.wait_ge(S["ovar_done"], h + 1)
                v, e, y = osum[:, 0, :], osum[:, 1, :], osum[:, 2, :]
                link(pool.tensor_tensor(v, v, coef[:, 0, :], ALU.mult))
                for n in range(NEWTON):
                    link(pool.tensor_tensor(e, y, y, ALU.mult))
                    link(pool.tensor_tensor(e, e, v, ALU.mult))
                    link(pool.tensor_tensor(e, e, coef[:, 1, :], ALU.add))
                    last = pool.tensor_tensor(y, y, e, ALU.mult)
                    if n < NEWTON - 1:
                        link(last)
                last.then_inc(S["orinv_done"], 1)
                pool.wait_ge(S["orinv_done"], h + 1)
                pool.wait_ge(S["oraw_done"], h + 1)
                pool.tensor_tensor(o_nrm[:, :, :], o_raw[:, :, :], y.unsqueeze(2).broadcast_to([P, TT, P]),
                                   ALU.mult).then_inc(S["onrm_done"], 1)

            def query_rope(h, p):
                pool.wait_ge(S["qhalf_done"], h - 1)
                link(pool.tensor_tensor(q_sh[:, :], q_sh[:, :], sinT[:, :], ALU.mult))
                pool.tensor_tensor(qT[p][:, :], q_t1[:, :], q_sh[:, :], ALU.add).then_inc(S["qrope_done"], 1)

            ahead = PLAN["qk"] + RING + 4
            lows(0, ahead)
            with chain.loop(0, (DIFF_HEADS - 2) // 2, 2 * (4 * NEWTON + 1)) as i:
                for p in range(2):
                    o_normed(2 * i + p)
                    query_rope(2 * i + (p + 2), p)
                    for k in range(2):
                        u = ahead + 2 * p + k
                        low(u, u % RING, u + 4 * i + 1)
            o_normed(DIFF_HEADS - 2)
            o_normed(DIFF_HEADS - 1)
            lows(ahead + 2 * (DIFF_HEADS - 2), UNITS)

        @block.scalar
        def _(act):
            chain = Chain(act, S["chain_act"])
            link = chain.link

            def signal(ins, name, value):
                ins.then_inc(S[name], 1)
                act.wait_ge(S[name], value)

            def w_high(u, i=0, per=0):
                if u >= UNITS:
                    return
                if u >= RING:
                    act.wait_ge(S["units_done"], u + 1 - RING + per * i)
                act.wait_ge(S[f"w_in{u % RAW}"], 16 * (u // RAW + 1) + 16 * (per // RAW) * i)
                act.activation(w_hi[u % RING][:, :], w_raw[u % RAW][:, :], ACT.Copy).then_inc(S["w_hi_done"], 1)

            def stats(q, t):
                if q == 0:
                    act.wait_ge(S[f"x_in{t}"], 16)
                else:
                    act.wait_ge(S["x_updated"], 4 * (q - 1) + t + 1)
                link(act.activation(junk[:, :], x[:, t, :], ACT.Square, accum_out=ss[:, t:t + 1]))
                signal(act.activation(std[:, t:t + 1], ss[:, t:t + 1], ACT.Sqrt, bias=eps[:, :], scale=1.0 / D),
                       "std_done", 4 * q + t + 1)

            def nT_high(q, t):
                for b, bank in enumerate(xT_banks(q, t)):
                    act.wait_ge(S["xT_done"], 8 * q + 2 * t + b + 1)
                    signal(act.activation(nT_hi[:, 4 * b:4 * b + 4, tok(t)],
                                          bank.rearrange("p (k n) -> p k n", k=4), ACT.Copy),
                           "nhi_done", 8 * q + 2 * t + b + 1)

            def gains(q, r):
                if q:
                    act.wait_ge(S["nlo_done"], 8 * q)
                act.dma_start(g_pre[:, :], gain_in[GAINS * (q // 3) + 2 * (q % 3), :, :]).then_inc(S["gain_in"], 16)
                if r is not None:
                    act.dma_start(g_post[:, :], gain_in[GAINS * (r // 2) + 1 + 2 * (r % 2), :, :])\
                        .then_inc(S["gpost_in"], 16)

            def output_norm(r, phase, name, n, q, asked=0):
                U = PLAN[name]
                for k in range(asked, n // 2):
                    w_high(U + k + RING)
                for t in range(TT):
                    act.wait_ge(S["y0_done"], 4 * r + t + 1)
                    link(act.activation(junk[:, 0:HALF], y0[:, t, :], ACT.Square, accum_out=yss[:, 0, t:t + 1]))
                    link(act.activation(yst[:, 0, t:t + 1], yss[:, 0, t:t + 1], ACT.Identity, bias=eps[:, :],
                                        scale=1.0 / D))
                for k in range(n // 2, n - 4):
                    w_high(U + k + RING)

                def y_std(t):
                    if t < TT - 1:
                        act.wait_ge(S["tile_done"], 3 * phase + t + 1)
                    else:
                        act.wait_ge(S["units_done"], U + n)
                    link(act.activation(junk[:, 0:HALF], A[t][:, :], ACT.Square, accum_out=yss[:, 1, t:t + 1]))
                    signal(act.activation(yst[:, 1, t:t + 1], yss[:, 1, t:t + 1], ACT.Sqrt,
                                          bias=yst[:, 0, t:t + 1], scale=1.0 / D), "ystd_done", 4 * r + t + 1)
                y_std(0)
                stats(q, 0)
                for t in range(1, TT):
                    y_std(t)
                    if t >= 2:
                        w_high(U + n + 2 * (t - 2))
                    nT_high(q, t - 1)
                    if t == 2:
                        w_high(U + n + 1)
                    stats(q, t)
                nT_high(q, TT - 1)
                w_high(U + n + 3)

            def mlp(layer, name):
                U = PLAN[name]

                def pair(i, p, peeled):
                    j = 2 * i + p
                    if not peeled:
                        act.wait_ge(S["hlo_done"], FT * layer + j - 1)

                    def affine(v, dst, bank):
                        act.wait_ge(S["units_done"], U + 2 * j + v + 1)
                        f = j + v * FT
                        signal(act.activation(dst, bank[:, :], ACT.Identity, bias=conv[:, bass.ds(4 * f + 3, 1)],
                                              scale=conv[:, bass.ds(4 * f + 2, 1)]),
                               "aff_done", 2 * FT * layer + 2 * j + v + 1)
                    affine(0, y0[:, p, :], A[2 * p])
                    w_high(U + RING + 2 * p, i, RING)
                    affine(1, y0[:, 2 + p, :], A[2 * p + 1])
                    act.wait_ge(S["gateconv_done"], FT * layer + j + 1)
                    signal(act.activation(y0[:, p, :], y0[:, p, :], ACT.Gelu_apprx_tanh), "gelu_done",
                           FT * layer + j + 1)
                    w_high(U + RING + 2 * p + 1, i, RING)
                    act.wait_ge(S["h_done"], FT * layer + j + 1)
                    signal(act.activation(hT_hi[:, bass.ds(j, 1), :].rearrange("p a n -> p (a n)"),
                                          y0[:, 2 + p, :], ACT.Copy), "hhi_done", FT * layer + j + 1)
                for p in range(2):
                    pair(0, p, True)
                with chain.loop(1, FT // 2, 0) as i:
                    for p in range(2):
                        pair(i, p, False)

            def embed(layer, q, phase):
                Ua, Up, Ub = (PLAN[f"gate{layer}a"], PLAN[f"ple{layer}"], PLAN[f"gate{layer}b"])
                act.wait_ge(S["units_done"], Ua)
                act.dma_start(pe_raw[:, :, :], pT_in[layer, :, :, :]).then_inc(S["ple_in"], 16)
                act.wait_ge(S["ple_in"], 16 * (layer + 1))
                signal(act.activation(pe_hi[:, :, :], pe_raw[:, :, :], ACT.Copy), "pehi_done", layer + 1)
                for k in range(4):
                    w_high(Ua + k + RING)

                def sigmoid(half, t, bank):
                    signal(act.activation(sg[:, t, :], bank[t][:, :], ACT.Sigmoid), "sig_done",
                           8 * layer + 4 * half + t + 1)
                for t in range(TT):
                    sigmoid(0, t, A)
                for k in range(2):
                    w_high(Up + k + RING)

                def second(t):
                    if t < TT - 1:
                        act.wait_ge(S["tile_done"], 3 * phase + t + 1)
                    else:
                        act.wait_ge(S["units_done"], Ub + 4)
                    act.wait_ge(S["xhalf_done"], 4 * layer + t + 1)
                    sigmoid(1, t, B)
                if layer == LAYERS - 1:
                    for t in range(TT):
                        second(t)
                    return
                second(0)
                stats(q, 0)
                for t in range(1, TT):
                    second(t)
                    if t >= 2:
                        w_high(Ub + 2 * t)
                    nT_high(q, t - 1)
                    if t == 2:
                        w_high(Ub + 5)
                    stats(q, t)
                nT_high(q, TT - 1)
                w_high(Ub + 7)

            act.dma_start(const[:, :], const_in).then_inc(S["consts_in"], 16)
            gains(0, 0)
            act.wait_ge(S["consts_ready"], 4)
            stats(0, 0)
            w_high(0)
            stats(0, 1)
            nT_high(0, 0)
            w_high(1)
            stats(0, 2)
            nT_high(0, 1)
            stats(0, 3)
            nT_high(0, 2)
            nT_high(0, 3)
            w_high(2)
            w_high(3)
            act.dma_start(pos_i[:, :], pos_in).then_inc(S["pos_in"], 16)
            act.dma_start(lam_v[:, :, :], lam_in).then_inc(S["lamv_in"], 16)
            act.dma_start(subg[:, :], subln_in).then_inc(S["sub_in"], 16)
            act.dma_start(conv[:, :], conv_in[0, :, :]).then_inc(S["conv_in"], 16)
            UV = PLAN["v"] + RING
            w_high(UV)
            w_high(UV + 1)
            act.wait_ge(S["rope_in"], 1)
            signal(act.activation(sinT[:, :], red[:, :], ACT.Sin, scale=const[:, C_SIGN:C_SIGN + 1]), "rope_tab", 1)
            act.wait_ge(S["rope_in"], 2)
            signal(act.activation(cosT[:, :], turn[:, :], ACT.Sin), "rope_tab", 2)
            w_high(UV + 2)
            w_high(UV + 3)
            act.wait_ge(S["lam_sum"], 1)
            signal(act.activation(lam[:, 2:4], lam[:, 0:2], ACT.Exp), "lam_exp", 1)
            for u in range(4, 8):
                w_high(UV + u)

            def exps(h, p, qt):
                for c in range(2):
                    act.wait_ge(S["negmax_done"], 4 * h + qt + 1)
                    if not (isinstance(h, int) and h == 0 and qt < 2):
                        act.wait_ge(S["mix_done"], 4 * h + qt - 1)
                    n = (qt + 1) * P
                    signal(act.activation(pr[:, qt % 2, c, 0:n], B[2 * (qt % 2) + c][:, 0:n], ACT.Exp,
                                          bias=nm[:, qt, c:c + 1],
                                          accum_out=sums[:, p, qt, c:c + 1]),
                           "probs_done", 8 * h + 2 * qt + c + 1)

            def p_turned(h, qt):
                act.wait_ge(S["mixT_done"], 4 * h + qt + 1)
                if not (isinstance(h, int) and h == 0 and qt < 2):
                    act.wait_ge(S["pv_done"], 4 * h + qt - 1)
                n = (qt + 1) * P
                signal(act.activation(pT[:, qt % 2, 0:n], A[2][:, 0:n], ACT.Copy), "pT_done", 4 * h + qt + 1)

            def o_out(h):
                act.wait_ge(S["pv_done"], 4 * h + 4)
                if not (isinstance(h, int) and h == 0):
                    act.wait_ge(S["onrm_done"], h)
                link(act.activation(o_sq[:, :, :], A[3].rearrange("p (t n) -> p t n", t=TT), ACT.Square))
                signal(act.activation(o_raw[:, :, :], A[3].rearrange("p (t n) -> p t n", t=TT), ACT.Copy),
                       "oraw_done", h + 1)

            def oT_high(h):
                act.wait_ge(S["oT_done"], h + 1)
                signal(act.activation(oT0_hi[:, bass.ds(h, 1), :].rearrange("p a n -> p (a n)"), A[2][:, :],
                                      ACT.Identity, scale=subg[:, :]), "oThi_done", h + 1)

            def head(h, p, first=False, last=False, i=0, per=0, u=0):
                exps(h, p, 0)
                exps(h, p, 1)
                if not first:
                    o_out(h - 1)
                p_turned(h, 0)
                exps(h, p, 2)
                p_turned(h, 1)
                if not last:
                    w_high(u, i, per)
                p_turned(h, 2)
                exps(h, p, 3)
                if not first:
                    oT_high(h - 1)
                if not last:
                    w_high(u + 1, i, per)
                p_turned(h, 3)

            UH = PLAN["qk"] + RING
            w_high(UH)
            w_high(UH + 1)
            act.wait_ge(S["lam_ready"], 1)
            head(0, 0, first=True, u=UH + 2)
            with chain.loop(0, (DIFF_HEADS - 2) // 2, 2) as i:
                for p in range(2):
                    head(2 * i + (p + 1), (p + 1) % 2, i=i, per=4, u=UH + 4 + 2 * p)
            head(DIFF_HEADS - 1, 1, last=True)
            o_out(DIFF_HEADS - 1)
            w_high(PLAN["out0"] + RING)
            oT_high(DIFF_HEADS - 1)

            gains(1, None)
            output_norm(0, 0, "out0", 8, 1, asked=1)
            gains(2, 1)
            mlp(0, "up0")
            output_norm(1, 1, "down0", FT, 2)
            gains(3, 2)
            act.dma_start(conv[:, :], conv_in[1, :, :]).then_inc(S["conv_in"], 16)
            embed(0, 3, 2)

            for dst, src in ((w1k[:, :, :], w1_in[0, :, :, :]), (w1v[:, :, :], w1_in[1, :, :, :]), (w2[:, :, :], w2_in),
                             (KR[:, GROUPS, 0:CMP_LEN], cpos_in[0, :, :]), (VR[:, GROUPS, 0:CMP_LEN], cpos_in[1, :, :])):
                act.dma_start(dst, src).then_inc(S["cmpw_in"], 16)
            gains(4, None)
            for g in range(GROUPS):
                w_high(PLAN["cmp"] + RING + g)
                act.activation(VR[0:HEAD, g, :], A[g][HEAD:P, :], ACT.Copy).then_inc(S["shifted_done"], 1)
                act.activation(VR[HEAD:P, g, 0:SEQ - 1], A[g][HEAD:P, 1:SEQ], ACT.Copy).then_inc(S["shifted_done"], 1)
                act.wait_ge(S["kr_done"], g + 1)
                act.activation(KR[HEAD:P, g, 0:SEQ - 1], KR[0:HEAD, g, 1:SEQ], ACT.Copy)\
                    .then_inc(S["shifted_done"], 1)
            w_high(PLAN["cmp"] + RING + GROUPS)
            act.wait_ge(S["units_done"], PLAN["branch"] + 1)
            signal(act.activation(gT[:, :], B[2], ACT.Sigmoid), "gsig_done", 1)
            act.wait_ge(S["hid_done"], 2)
            act.wait_ge(S["pad_ready"], 1)
            for kv, dst in enumerate((hid_k, hid_v)):
                link(act.activation(cbias[:, kv:kv + 1], A[kv][:, GROUPS * N_CMP:GROUPS * N_CMP + 1], ACT.Copy))
                signal(act.activation(dst[:, :, 0:N_CMP], A[kv][:, 0:GROUPS * N_CMP].rearrange("p (g n) -> p g n", g=GROUPS),
                                      ACT.Gelu_apprx_tanh, bias=cbias[:, kv:kv + 1]), "gelc_done", kv + 1)
            act.wait_ge(S["gatesT_done"], 1)
            link(act.activation(gates[:, :, :], A[3].rearrange("p (t n) -> p t n", t=TT)[:, :, 0:3 * D // HEAD],
                                ACT.Copy))
            act.wait_ge(S["kv_done"], 2)
            for m in range(2):
                chain.step(act.activation(kcmp[side(m), :, :], A[2][0:HEAD, 0:P].rearrange("p (g n) -> p g n", g=GROUPS),
                                          ACT.Copy))
            chain.wait(0)
            signal(act.activation(kc[:, :, 0, :], kcmp[:, :, :], ACT.Copy), "kchi_done", 1)
            for h in range(GHEADS):
                signal(act.activation(Vblk[32 * h:32 * h + 32, :, HEAD * h:HEAD * h + HEAD],
                                      A[2][0:N_PAD, P:P + GROUPS * HEAD].rearrange("p (g n) -> p g n", g=GROUPS),
                                      ACT.Copy), "kvc_done", h + 1)
            act.dma_start(cm[:, 0, :], const_in[:, C_CMP:C_ALL]).then_inc(S["cm_in"], 16)

            def goT_high(pair, m):
                act.wait_ge(S["goT_done"], pair + 1)
                signal(act.activation(oT1_hi[:, bass.ds(pair, 1), :].rearrange("p a n -> p (a n)"),
                                      A[2 + m], ACT.Copy), "goThi_done", pair + 1)

            def group(g, first, i=0, u=0, per=0):
                def step(h, k):
                    return 16 * g + 4 * h + k

                def gexps(h, k):
                    qt = ORDER[k]
                    n = (qt + 1) * P
                    for c in range(2):
                        act.wait_ge(S["gnegmax_done"], step(h, k) + 1)
                        if not (first and h == 0 and k < 2):
                            act.wait_ge(S["gT_done"], 2 * step(h, k) - 2)
                        signal(act.activation(gp[:, k % 2, c, 0:n], B[2 * (k % 2) + c][:, 0:n], ACT.Exp,
                                              bias=nm[:, qt, c:c + 1],
                                              accum_out=sums[:, h % 2, qt, c:c + 1]),
                               "gprobs_done", 2 * step(h, k) + c + 1)

                def gp_turned(h, k):
                    n = (ORDER[k] + 1) * P
                    act.wait_ge(S["gT_done"], 2 * step(h, k) + 1)
                    if not (first and h == 0 and k < 2):
                        act.wait_ge(S["gpv_done"], step(h, k) - 1)
                    signal(act.activation(gpT[:, k % 2, 0, 0:n], A[2][:, 0:n], ACT.Copy), "gpTa_done",
                           step(h, k) + 1)

                def query_high(n):
                    act.wait_ge(S["groupkv_done"], 3 * g + 1 + n)
                    for m in range(2):
                        signal(act.activation(Q[2 * n + m][side(m), :], rot[n][side(m), :], ACT.Copy), "ghi_done",
                               8 * g + 2 * n + m + 1)

                w_high(u, i, per)
                if not first:
                    for m in range(2):
                        goT_high(2 * g - 2 + m, m)
                query_high(0)
                w_high(u + 1, i, per)
                query_high(1)
                w_high(u + 2, i, per)
                act.wait_ge(S["groupkv_done"], 3 * g + 3)
                for own in (True, False):
                    for c in range(2):
                        m = c if own else 1 - c
                        signal(act.activation(Kh[side(m), c, :], rot[2][side(c), :], ACT.Copy), "ghi_done",
                               8 * g + 4 + 2 * (not own) + c + 1)
                act.wait_ge(S["cexp_in"], g + 1)
                signal(act.activation(pc[:, :, :, :], sc[:, :, :, :], ACT.Exp), "cexp_done", g + 1)
                act.wait_ge(S["glo_done"], 6 * g + 6)
                for c in range(2):
                    signal(act.activation(Kl[side(1 - c), c, :], Kl[side(c), c, :].bitcast(F32), ACT.Copy), "gkx_done",
                           2 * g + c + 1)
                seq = [(h, k) for h in range(GHEADS) for k in range(TT)]
                act.wait_ge(S["units_done"], PLAN["group"] + 4 * g + 4)
                signal(act.activation(vT[:, :], B[3], ACT.Copy), "vT_done", g + 1)
                act.wait_ge(S["cpT_done"], g + 1)
                signal(act.activation(pcT[:, :, :], A[3].rearrange("p (t n) -> p t n", t=TT), ACT.Copy),
                       "cpTc_done", g + 1)
                gexps(*seq[0])
                act.wait_ge(S["vTt_done"], g + 1)
                v3 = A[0].rearrange("p (t n) -> p t n", t=TT)
                link(act.activation(Vg[:, :, 0:P], v3, ACT.Copy))
                signal(act.activation(Vg[:, :, P:P + HEAD], v3[:, :, 0:HEAD], ACT.Copy), "vg_done", g + 1)
                gexps(*seq[1])
                for n, (h, k) in enumerate(seq):
                    gp_turned(h, k)
                    if n + 2 < len(seq):
                        gexps(*seq[n + 2])
                    if n == 1:
                        w_high(u + 3, i, per)

            UG = PLAN["group"] + RING
            group(0, True, u=UG)
            with chain.loop(1, GROUPS, 1) as g:
                group(g, False, i=g, u=UG, per=4)
            w_high(PLAN["out1"] + RING)
            for m in range(2):
                goT_high(2 * GROUPS - 2 + m, m)

            output_norm(2, 3, "out1", 8, 4, asked=1)
            gains(5, 3)
            mlp(1, "up1")
            output_norm(3, 4, "down1", FT, 5)
            embed(1, None, 5)

        @block.vector
        def _(dve):
            chain = Chain(dve, S["chain_dve"])
            link = chain.link

            def signal(ins, name, value):
                ins.then_inc(S[name], 1)
                dve.wait_ge(S[name], value)

            def prepare(q, t):
                if t == 0:
                    dve.wait_ge(S["gain_in"], 16 * (q + 1))
                elif q:
                    dve.wait_ge(S["xT_done"], 8 * q + 2 * t)
                dve.wait_ge(S["std_done"], 4 * q + t + 1)
                link(dve.reciprocal(rinv[:, t:t + 1], std[:, t:t + 1]))
                signal(dve.scalar_tensor_tensor(normed(q, t), x[:, t, :], rinv[:, t:t + 1], g_pre[:, :], ALU.mult,
                                                ALU.mult), "xn_done", 4 * q + t + 1)

            def nT_low(q, t):
                for b, bank in enumerate(xT_banks(q, t)):
                    dve.wait_ge(S["nhi_done"], 8 * q + 2 * t + b + 1)
                    signal(dve.tensor_tensor(nT_lo[:, 4 * b:4 * b + 4, tok(t)],
                                             bank.rearrange("p (k n) -> p k n", k=4),
                                             nT_hi[:, 4 * b:4 * b + 4, tok(t)].bitcast(F32), ALU.subtract),
                           "nlo_done", 8 * q + 2 * t + b + 1)

            def output_norm(r, phase, name, n, q):
                U = PLAN[name]
                dve.wait_ge(S["units_done"], U + n // 2)
                for t in range(TT):
                    signal(dve.tensor_copy(y0[:, t, :], B[t][:, :]), "y0_done", 4 * r + t + 1)
                dve.wait_ge(S["gpost_in"], 16 * (r + 1))

                def update(t):
                    dve.wait_ge(S["ystd_done"], 4 * r + t + 1)
                    link(dve.reciprocal(yst[:, 2, t:t + 1], yst[:, 1, t:t + 1]))
                    halves = (y0[:, t, :], slice(0, HALF)), (A[t], slice(HALF, D))
                    for y, cols in halves:
                        chain.step(dve.scalar_tensor_tensor(y, y, yst[:, 2, t:t + 1], g_post[:, cols], ALU.mult,
                                                            ALU.mult))
                    chain.wait(1)
                    chain.step(dve.tensor_tensor(x[:, t, 0:HALF], x[:, t, 0:HALF], y0[:, t, :], ALU.add))
                    chain.wait(1)
                    dve.tensor_tensor(x[:, t, HALF:D], x[:, t, HALF:D], A[t], ALU.add).then_inc(S["x_updated"], 1)
                    chain.wait(0)
                    dve.wait_ge(S["x_updated"], 4 * phase + t + 1)
                update(0)
                prepare(q, 0)
                for t in range(1, TT):
                    update(t)
                    nT_low(q, t - 1)
                    prepare(q, t)
                nT_low(q, TT - 1)

            def rope(bank, dst, name, value, rows=slice(0, P), tmp=None, scale=1.0):
                s_, a_, b_ = tmp
                chain.step(dve.tensor_tensor(a_, bank[rows, :], cosT[rows, :], ALU.mult))
                link(dve.stream_shuffle(s_, bank[rows, :], [(n + 16) % 32 for n in range(32)]))
                link(dve.scalar_tensor_tensor(b_, s_, scale, sinT[rows, :], ALU.mult, ALU.mult))
                signal(dve.scalar_tensor_tensor(dst, a_, scale, b_, ALU.mult, ALU.add), name, value)

            def mlp(layer, name):
                def pair(i, p):
                    j = 2 * i + p

                    def taps(v, dst, bank):
                        f = j + v * FT
                        dve.wait_ge(S["aff_done"], 2 * FT * layer + 2 * j + v + 1)
                        link(dve.scalar_tensor_tensor(dst[:, 1:SEQ], bank[:, 0:SEQ - 1], conv[:, bass.ds(4 * f + 1, 1)],
                                                      dst[:, 1:SEQ], ALU.mult, ALU.add))
                        last = dve.scalar_tensor_tensor(dst[:, 2:SEQ], bank[:, 0:SEQ - 2], conv[:, bass.ds(4 * f, 1)],
                                                        dst[:, 2:SEQ], ALU.mult, ALU.add)
                        signal(last, ("gateconv_done", "conv_done")[v], FT * layer + j + 1)
                    taps(0, y0[:, p, :], A[2 * p])
                    taps(1, y0[:, 2 + p, :], A[2 * p + 1])
                    dve.wait_ge(S["gelu_done"], FT * layer + j + 1)
                    signal(dve.tensor_tensor(y0[:, 2 + p, :], y0[:, 2 + p, :], y0[:, p, :], ALU.mult), "h_done",
                           FT * layer + j + 1)
                    dve.wait_ge(S["hhi_done"], FT * layer + j + 1)
                    signal(dve.tensor_tensor(hT_lo[:, bass.ds(j, 1), :].rearrange("p a n -> p (a n)"), y0[:, 2 + p, :],
                                             hT_hi[:, bass.ds(j, 1), :].rearrange("p a n -> p (a n)").bitcast(F32),
                                             ALU.subtract), "hlo_done", FT * layer + j + 1)
                dve.wait_ge(S["conv_in"], 16 * (layer + 1))
                with chain.loop(0, FT // 2, 4) as i:
                    for p in range(2):
                        pair(i, p)

            def embed(layer, q, phase):
                Up = PLAN[f"ple{layer}"]
                dve.wait_ge(S["pehi_done"], layer + 1)
                signal(dve.tensor_tensor(pe_lo[:, :, :], pe_raw[:, :, :], pe_hi[:, :, :].bitcast(F32), ALU.subtract),
                       "pelo_done", layer + 1)
                dve.wait_ge(S["units_done"], Up + 1)
                for t in range(TT):
                    dve.wait_ge(S["sig_done"], 8 * layer + t + 1)
                    link(dve.tensor_tensor(sg[:, t, :], sg[:, t, :], B[t][:, :], ALU.mult))
                    signal(dve.tensor_tensor(x[:, t, 0:HALF], x[:, t, 0:HALF], sg[:, t, :], ALU.add), "xhalf_done",
                           4 * layer + t + 1)
                dve.wait_ge(S["units_done"], Up + 2)

                def second(t):
                    dve.wait_ge(S["sig_done"], 8 * layer + 4 + t + 1)
                    link(dve.tensor_tensor(sg[:, t, :], sg[:, t, :], A[t][:, :], ALU.mult))
                    signal(dve.tensor_tensor(x[:, t, HALF:D], x[:, t, HALF:D], sg[:, t, :], ALU.add), "x_updated",
                           4 * phase + t + 1)
                if layer == LAYERS - 1:
                    for t in range(TT):
                        second(t)
                    return
                second(0)
                prepare(q, 0)
                for t in range(1, TT):
                    second(t)
                    nT_low(q, t - 1)
                    prepare(q, t)
                nT_low(q, TT - 1)

            dve.memset(eps[:, :], EPS).then_inc(S["consts_ready"], 1)
            dve.wait_ge(S["consts_in"], 16)
            dve.tensor_copy(ident[:, :], const[:, C_IDENT:C_IDENT + P]).then_inc(S["consts_ready"], 1)
            dve.tensor_copy(ident_b[:, :], const[:, C_IDENT:C_IDENT + P]).then_inc(S["consts_ready"], 1)
            dve.tensor_copy(causal_b[:, :], const[:, C_CAUSAL:C_CAUSAL + P]).then_inc(S["consts_ready"], 1)
            dve.wait_ge(S["consts_ready"], 4)
            for t in range(TT):
                prepare(0, t)
                if t:
                    nT_low(0, t - 1)
            nT_low(0, 3)
            dve.wait_ge(S["pos_in"], 16)
            link(dve.tensor_copy(ang[:, :], pos_i[:, :]))
            link(dve.tensor_scalar(ang[:, :], ang[:, :], const[:, C_INV:C_INV + 1], None, ALU.mult))
            for n, (r, shift) in enumerate(((red, 0.0), (turn, 0.25))):
                k = cosT
                link(dve.tensor_scalar(k[:, :], ang[:, :], 1.0 / TWO_PI, shift, ALU.mult, ALU.add))
                link(dve.tensor_scalar(k[:, :], k[:, :], ROUND, None, ALU.add))
                link(dve.tensor_scalar(k[:, :], k[:, :], ROUND, None, ALU.subtract))
                link(dve.scalar_tensor_tensor(r[:, :], k[:, :], -PI_1, ang[:, :], ALU.mult, ALU.add))
                link(dve.scalar_tensor_tensor(r[:, :], k[:, :], -PI_2, r[:, :], ALU.mult, ALU.add))
                link(dve.scalar_tensor_tensor(r[:, :], k[:, :], -PI_3, r[:, :], ALU.mult, ALU.add))
                link(dve.tensor_scalar(r[:, :], r[:, :], shift * TWO_PI, None, ALU.add))
                signal(dve.tensor_scalar(r[:, :], r[:, :], PI_MAX, -PI_MAX, ALU.min, ALU.max), "rope_in", n + 1)
            dve.wait_ge(S["lamv_in"], 16)
            dve.wait_ge(S["sub_in"], 16)
            for n in range(2):
                link(dve.tensor_tensor(lam_p[:, n, :], lam_v[:, 2 * n, :], lam_v[:, 2 * n + 1, :], ALU.mult))
            signal(dve.tensor_reduce(lam[:, 0:2], lam_p[:, :, :], AX.X, ALU.add), "lam_sum", 1)
            dve.wait_ge(S["lam_exp"], 1)
            link(dve.tensor_tensor(neg_lam[:, :], lam[:, 3:4], lam[:, 2:3], ALU.subtract))
            link(dve.tensor_scalar(neg_lam[:, :], neg_lam[:, :], -LAMBDA_INIT, None, ALU.add))
            signal(dve.tensor_scalar(subg[:, :], subg[:, :], 1.0 - LAMBDA_INIT, None, ALU.mult), "lam_ready", 1)
            dve.wait_ge(S["rope_tab"], 2)

            for half in range(2):
                dve.wait_ge(S["units_done"], PLAN["v"] + 4 * (half + 1))
                for t in range(TT):
                    signal(dve.tensor_copy(V[:, t, half * HALF:(half + 1) * HALF], (A, B)[half][t][:, :]), "v_done",
                           4 * half + t + 1)

            def maxima(qt, b, scores, negmax, step):
                n = (qt + 1) * P
                dve.wait_ge(S[scores], 2 * step + 2)
                signal(dve.tensor_reduce(nm[:, qt, :], banks_b[:, b:b + 2, 0:n], AX.X, ALU.max, negate=True), negmax,
                       step + 1)

            def mix(h, p, qt):
                n = (qt + 1) * P
                dve.wait_ge(S["probs_done"], 8 * h + 2 * qt + 2)
                link(dve.tensor_scalar(st1[:, 0:1], sums[:, p, qt, 1:2], 1e-30, None, ALU.max))
                link(dve.reciprocal(st1[:, 1:2], st1[:, 0:1]))
                link(dve.scalar_tensor_tensor(st1[:, 2:3], sums[:, p, qt, 0:1], neg_lam[:, :], st1[:, 1:2],
                                              ALU.mult, ALU.mult))
                if not (isinstance(h, int) and h == 0 and qt < 2):
                    dve.wait_ge(S["mixT_done"], 4 * h + qt - 1)
                signal(dve.scalar_tensor_tensor(amix[:, qt % 2, 0:n], pr[:, qt % 2, 1, 0:n], st1[:, 2:3],
                                                pr[:, qt % 2, 0, 0:n], ALU.mult, ALU.add),
                       "mix_done", 4 * h + qt + 1)

            def o_variance(h, p):
                dve.wait_ge(S["oraw_done"], h + 1)
                chain.step(dve.tensor_reduce(osum[:, 0, :], o_sq[:, :, :], AX.X, ALU.add))
                link(dve.tensor_scalar(osum[:, 1, :], sums[:, p, :, 0], 1e-30, None, ALU.max))
                link(dve.scalar_tensor_tensor(osum[:, 1, :], osum[:, 1, :], EPS, osum[:, 1, :], ALU.mult, ALU.mult))
                link(dve.scalar_tensor_tensor(osum[:, 0, :], osum[:, 0, :], 1.0 / P, osum[:, 1, :], ALU.mult,
                                              ALU.add))
                y = osum[:, 2, :].bitcast(I32)
                link(dve.tensor_scalar(y, osum[:, 0, :].bitcast(I32), 1, None, ALU.arith_shift_right))
                signal(dve.tensor_scalar(y, y, -1.0, float(0x5F3759DF), ALU.mult, ALU.add), "ovar_done", h + 1)

            def oT_low(h):
                dve.wait_ge(S["oThi_done"], h + 1)
                signal(dve.scalar_tensor_tensor(
                    oT0_lo[:, bass.ds(h, 1), :].rearrange("p a n -> p (a n)"), A[2][:, :], subg[:, :],
                    oT0_hi[:, bass.ds(h, 1), :].rearrange("p a n -> p (a n)").bitcast(F32), ALU.mult, ALU.subtract),
                    "oTlo_done", h + 1)

            def query_half(h):
                dve.wait_ge(S["units_done"], PLAN["qk"] + 2 * h + 1)
                chain.step(dve.tensor_tensor(q_t1[:, :], A[0], cosT[:, :], ALU.mult))
                signal(dve.stream_shuffle(q_sh[:, :], A[0], [(n + 16) % 32 for n in range(32)]), "qhalf_done", h - 1)
                chain.wait(0)

            def head_rope(h, p, k):
                dve.wait_ge(S["units_done"], PLAN["qk"] + 2 * h + k + 1)
                rope(A[k], (qT, kT)[k][p][:, :], ("qrope_done", "krope_done")[k], h + 1,
                     tmp=(sh[:, :], t1[:, :], t2[:, :]), scale=(1.0, SCALE)[k])

            def head(h, p, first=False, last=False):
                maxima(0, 0, "scores_done", "negmax_done", 4 * h)
                maxima(1, 2, "scores_done", "negmax_done", 4 * h + 1)
                mix(h, p, 0)
                mix(h, p, 1)
                maxima(2, 0, "scores_done", "negmax_done", 4 * h + 2)
                if not first:
                    o_variance(h - 1, 1 - p)
                mix(h, p, 2)
                maxima(3, 2, "scores_done", "negmax_done", 4 * h + 3)
                if first:
                    head_rope(h + 1, 1 - p, 0)
                elif not last:
                    query_half(h + 1)
                mix(h, p, 3)
                if not first:
                    oT_low(h - 1)
                if not last:
                    head_rope(h + 1, 1 - p, 1)

            head_rope(0, 0, 0)
            head_rope(0, 0, 1)
            head(0, 0, first=True)
            with chain.loop(0, (DIFF_HEADS - 2) // 2, 2 * (12 + 3 + 1 + 5)) as i:
                for p in range(2):
                    head(2 * i + (p + 1), (p + 1) % 2)
            head(DIFF_HEADS - 1, 1, last=True)
            o_variance(DIFF_HEADS - 1, 1)
            oT_low(DIFF_HEADS - 1)

            output_norm(0, 0, "out0", 8, 1)
            mlp(0, "up0")
            output_norm(1, 1, "down0", FT, 2)
            embed(0, 3, 2)

            for g in range(GROUPS):
                dve.wait_ge(S["units_done"], PLAN["cmp"] + g + 1)
                rope(A[g], KR[0:HEAD, g, :], "kr_done", g + 1, rows=slice(0, HEAD),
                     tmp=(ksh[:, :], kt1[:, :], kt2[:, :]))
                if g == 0:
                    for pad in (hid_k[:, :, N_CMP:N_PAD], hid_v[:, :, N_CMP:N_PAD], KR[:, GROUPS, CMP_LEN:SEQ],
                                VR[:, GROUPS, CMP_LEN:SEQ]):
                        chain.step(dve.memset(pad, 0.0))
                    chain.wait(0)
                    signal(dve.memset(Vblk[:, :, :], 0.0), "pad_ready", 1)

            def goT_low(pair, m):
                dve.wait_ge(S["goThi_done"], pair + 1)
                signal(dve.tensor_tensor(
                    oT1_lo[:, bass.ds(pair, 1), :].rearrange("p a n -> p (a n)"), A[2 + m],
                    oT1_hi[:, bass.ds(pair, 1), :].rearrange("p a n -> p (a n)").bitcast(F32), ALU.subtract),
                    "goTlo_done", pair + 1)

            def group(g, first):
                def step(h, k):
                    return 16 * g + 4 * h + k

                U = PLAN["group"]
                tmp = (gsh, gt1, gsh)
                flat = "p t h n -> p (t h) n"
                seq = [(h, k) for h in range(GHEADS) for k in range(TT)]

                def over_heads(mask):
                    return mask.rearrange("p (t n) -> p t n", t=TT).unsqueeze(2).broadcast_to([P, TT, GHEADS, N_PAD])

                def gmaxima(h, k):
                    maxima(ORDER[k], 2 * (k % 2), "gscores_done", "gnegmax_done", step(h, k))

                def gp_turned(h, k):
                    n = (ORDER[k] + 1) * P
                    dve.wait_ge(S["gT_done"], 2 * step(h, k) + 2)
                    signal(dve.tensor_copy(gpT[:, k % 2, 1, 0:n], A[3][:, 0:n]), "gpTv_done", step(h, k) + 1)

                def weights_of_branches(h):
                    link(dve.tensor_scalar(st2[:, 0, :, :], sums[:, h % 2, :, :], 1e-30, None, ALU.max))
                    link(dve.reciprocal(st2[:, 1, :, :], st2[:, 0, :, :]))
                    link(dve.tensor_tensor(st2[:, 0, :, :], st2[:, 1, :, :], gates[:, :, bass.ds(12 * g + (3 * h + 1), 2)],
                                           ALU.mult))

                def read_branches(h):
                    dve.wait_ge(S["gpv_done"], step(h, TT - 1) + 1)
                    og4 = og[:, :, :].rearrange("p t (b n) -> p b t n", b=2)
                    for c in range(2):
                        ins = dve.tensor_tensor(og4[:, c, :, :], A[c].rearrange("p (t n) -> p t n", t=TT)[:, :, 0:HEAD],
                                                st2[:, 0, :, c].unsqueeze(2).broadcast_to([P, TT, HEAD]), ALU.mult)
                        signal(ins, "oread_done", 8 * g + 2 * h + c + 1)

                def add_branches(h):
                    link(dve.tensor_tensor(og[:, :, 0:HEAD], og[:, :, 0:HEAD], og[:, :, HEAD:P], ALU.add))
                    dst = opair[:, h // 2, :].rearrange("p (t n) -> p t n", t=TT)
                    signal(dve.tensor_tensor(dst[:, :, HEAD * (h % 2):HEAD * (h % 2) + HEAD], og[:, :, 0:HEAD],
                                             oc[:, :, h, :], ALU.add), "opair_done", 4 * g + h + 1)

                for n in range(3):
                    dve.wait_ge(S["units_done"], U + 4 * g + (n + 1))
                    rope(B[n], rot[n], "groupkv_done", 3 * g + n + 1, tmp=tmp, scale=(SCALE, SCALE, 1.0)[n])
                    if n == 0 and not first:
                        for m in range(2):
                            goT_low(2 * g - 2 + m, m)
                    if n < 2:
                        for m in range(2):
                            dve.wait_ge(S["ghi_done"], 8 * g + 2 * n + m + 1)
                            signal(dve.tensor_tensor(Q[2 * n + m][side(1 - m), :], rot[n][side(m), :],
                                                     Q[2 * n + m][side(m), :].bitcast(F32), ALU.subtract), "glo_done",
                                   6 * g + 2 * n + m + 1)
                    if n == 1 and first:
                        dve.wait_ge(S["kchi_done"], 1)
                        dve.tensor_tensor(kc[:, :, 1, :], kcmp[:, :, :], kc[:, :, 0, :].bitcast(F32), ALU.subtract)\
                            .then_inc(S["kclo_done"], 1)
                        dve.wait_ge(S["cm_in"], 16)
                        link(dve.tensor_scalar(cm[:, 1, :], cm[:, 0, :], -MASKED, MASKED, ALU.mult, ALU.add))
                dve.wait_ge(S["csc_done"], g + 1)
                for m in range(2):
                    ts_ = slice(2 * m, 2 * m + 2)
                    both = A[m].rearrange("p (t h b n) -> p t h b n", t=2, h=GHEADS, b=2)
                    for b, other in ((1, over_heads(cm[:, 1, :])[:, ts_]), (0, sc[:, ts_, :, :])):
                        link(dve.tensor_tensor(sc[:, ts_, :, :], both[:, :, :, b, :], other, ALU.add))
                link(dve.tensor_reduce(cst[:, 0, :], sc[:, :, :, :].rearrange(flat), AX.X, ALU.max))
                signal(dve.tensor_tensor(sc[:, :, :, :].rearrange(flat), sc[:, :, :, :].rearrange(flat),
                                         cst[:, 0, :].unsqueeze(2).broadcast_to([P, TT * GHEADS, N_PAD]), ALU.subtract),
                       "cexp_in", g + 1)
                for c in range(2):
                    dve.wait_ge(S["ghi_done"], 8 * g + 4 + c + 1)
                    dve.tensor_tensor(Kl[side(c), c, :], rot[2][side(c), :], Kh[side(c), c, :].bitcast(F32),
                                      ALU.subtract).then_inc(S["glo_done"], 1)
                dve.wait_ge(S["cexp_done"], g + 1)
                dve.tensor_tensor(pc[:, :, :, :], pc[:, :, :, :], over_heads(cm[:, 0, :]), ALU.mult)\
                    .then_inc(S["cp_done"], 1)
                gmaxima(*seq[0])
                dve.wait_ge(S["cp_done"], g + 1)
                link(dve.tensor_reduce(cst[:, 1, :], pc[:, :, :, :].rearrange(flat), AX.X, ALU.add))
                link(dve.tensor_scalar(cst[:, 1, :], cst[:, 1, :], 1e-30, None, ALU.max))
                link(dve.reciprocal(cst[:, 2, :], cst[:, 1, :]))
                for t in range(TT):
                    ts_ = slice(t * GHEADS, (t + 1) * GHEADS)
                    chain.step(dve.tensor_tensor(
                        cst[:, 2, ts_], cst[:, 2, ts_],
                        gates[:, t, bass.ds(12 * g, 12)].rearrange("p (h b) -> p h b", b=3)[:, :, 0], ALU.mult))
                chain.wait(0)
                gmaxima(*seq[1])

                def blocks_out(m):
                    dve.wait_ge(S["coc_done"], 2 * g + m + 1)
                    src = A[1 - m].rearrange("p (th n) -> p th n", n=HEAD)
                    dst = oc[:, 2 * m:2 * m + 2, :, :].rearrange("p t h n -> p (t h) n")
                    signal(dve.tensor_tensor(
                        dst, src, cst[:, 2, 8 * m:8 * m + 8].unsqueeze(2).broadcast_to([P, 8, HEAD]), ALU.mult),
                        "oc_done", 2 * g + m + 1)

                blocks_out(0)
                for n, (h, k) in enumerate(seq):
                    gp_turned(h, k)
                    if n + 2 < len(seq):
                        gmaxima(*seq[n + 2])
                    if n == 0:
                        blocks_out(1)
                    if k == TT - 1:
                        weights_of_branches(h)
                    if h and k == 0:
                        read_branches(h - 1)
                    if h and k == 1:
                        add_branches(h - 1)
                read_branches(GHEADS - 1)
                add_branches(GHEADS - 1)

            group(0, True)
            with chain.loop(1, GROUPS, 3 * 3 + 4 + 1 + 1 + 2 + TT + 4 * 4) as g:
                group(g, False)
            for m in range(2):
                goT_low(2 * GROUPS - 2 + m, m)

            output_norm(2, 3, "out1", 8, 4)
            mlp(1, "up1")
            output_norm(3, 4, "down1", FT, 5)
            embed(1, None, 5)

        @block.tensor
        def _(pe):
            def weights(u):
                pe.wait_ge(S["w_lo_done"], u)

            def transpose(dst, src):
                return pe.matmul(dst, src, ident[:, :], start=True, stop=True, is_transpose=True)

            def transposes(q, t):
                pe.wait_ge(S["xn_done"], 4 * q + t + 1)
                if q and t:
                    pe.wait_ge(S["nlo_done"], 8 * q + 2 * t)
                for b, bank in enumerate(xT_banks(q, t)):
                    for k in range(4):
                        m = transpose(bank[:, k * P:(k + 1) * P], normed(q, t)[:, (4 * b + k) * P:(4 * b + k + 1) * P])
                    m.then_inc(S["xT_done"], 1)

            def features(bank, slot, rhs_hi, rhs_lo, part=None, cols=slice(0, SEQ)):
                steps = [(k, pas) for k in range(KT) for pas in range(3)]
                if part is not None:
                    steps = steps[8 * part:8 * part + 8]
                for k, pas in steps:
                    w = (w_hi, w_hi, w_lo)[pas][slot]
                    r = (rhs_hi, rhs_lo, rhs_hi)[pas]
                    m = pe.matmul(bank[:, cols], w[:, k * P:(k + 1) * P], r[:, k, cols], start=(k, pas) == (0, 0),
                                  stop=(k, pas) == (KT - 1, 2))
                return m

            def tokens(bank, slot, c, lhs_hi, lhs_lo, kk, t, n_k):
                for pas in range(3):
                    w = (w_hi, w_lo, w_hi)[pas][slot]
                    a = (lhs_hi, lhs_hi, lhs_lo)[pas]
                    m = pe.matmul(bank[:, :], a[:, kk, tok(t)], w[:, c * HALF:(c + 1) * HALF],
                                  start=(kk, pas) == (0, 0), stop=(kk, pas) == (n_k - 1, 2))
                return m

            def by_unit(U, units, banks, lhs_hi, lhs_lo, n_k, before=None):
                for n in units:
                    weights(U + n + 1)
                    if before:
                        before(n)
                    of_tiles(U, n, range(TT), banks, lhs_hi, lhs_lo, n_k).then_inc(S["units_done"], 1)

            def of_tiles(U, n, tiles, banks, lhs_hi, lhs_lo, n_k):
                for c in range(2):
                    kk = 2 * n + c - (n_k if 2 * n >= n_k else 0)
                    for t in tiles:
                        m = tokens(banks[t], (U + n) % RING, c, lhs_hi, lhs_lo, kk, t, n_k)
                return m

            def by_tile(U, units, banks, lhs_hi, lhs_lo, n_k, within, free=None):
                for t in range(TT):
                    if free:
                        free(t)
                    for n in units:
                        if t == 0:
                            weights(U + n + 1)
                        if n == units[2]:
                            within(t)
                        m = of_tiles(U, n, (t,), banks, lhs_hi, lhs_lo, n_k)
                        if t == TT - 1:
                            m.then_inc(S["units_done"], 1)
                    if t < TT - 1:
                        m.then_inc(S["tile_done"], 1)

            def cross(U, q, part):
                pe.wait_ge(S["nlo_done"], 8 * q + 4)
                weights(U + 1)
                part(0, 0)
                transposes(q, 2)
                weights(U + 2)
                part(1, 0)
                transposes(q, 3)
                weights(U + 3)
                part(2, 0)
                pe.wait_ge(S["nlo_done"], 8 * q + 8)
                for n in range(3):
                    part(n, 1).then_inc(S["units_done"], 1)

            def feature_part(U):
                return lambda n, m: features(A[n], (U + n) % RING, nT_hi, nT_lo, cols=slice(256 * m, 256 * m + 256))

            def feature_start(U, q):
                cross(U, q, feature_part(U))
                weights(U + 4)
                features(A[3], (U + 3) % RING, nT_hi, nT_lo).then_inc(S["units_done"], 1)

            def output(U, n, q, lhs_hi, lhs_lo, n_k, r, before=None):
                by_unit(U, range(n // 2), B, lhs_hi, lhs_lo, n_k, before)
                by_unit(U, range(n // 2, n - 4), A, lhs_hi, lhs_lo, n_k)

                def within(t):
                    if t >= 2:
                        if t == 2:
                            pe.wait_ge(S["y0_done"], 4 * r + 4)
                        transposes(q, t - 2)
                by_tile(U, range(n - 4, n), A, lhs_hi, lhs_lo, n_k, within)

            def mlp(layer, name, q):
                U = PLAN[name]
                feature_start(U, q)
                with pe.Fori(1, FT // 2) as i:
                    for p in range(2):
                        pe.wait_ge(S["conv_done"], FT * layer + 2 * i + (p - 1))
                        for v in range(2):
                            weights(U + (2 * p + v + 1) + 4 * i)
                            features(A[2 * p + v], (U + 2 * p + v) % RING, nT_hi, nT_lo).then_inc(S["units_done"], 1)

            def down(layer, name, q, r):
                def hidden(n):
                    pe.wait_ge(S["hlo_done"], FT * layer + min(2 * n + 2, FT))
                output(PLAN[name], FT, q, hT_hi, hT_lo, FT, r, hidden)

            def embed(layer, q, after_q):
                Ua, Up, Ub = PLAN[f"gate{layer}a"], PLAN[f"ple{layer}"], PLAN[f"gate{layer}b"]
                cross(Ua, after_q, lambda n, m: of_tiles(Ua, n, (2 * m, 2 * m + 1), A, nT_hi, nT_lo, KT))
                by_unit(Ua, (3,), A, nT_hi, nT_lo, KT)
                pe.wait_ge(S["pelo_done"], layer + 1)
                for half, banks in enumerate((B, A)):
                    weights(Up + half + 1)
                    for t in range(TT):
                        if half:
                            pe.wait_ge(S["sig_done"], 8 * layer + t + 1)
                        for c in range(2):
                            m = tokens(banks[t], (Up + half) % RING, c, pe_hi, pe_lo, c, t, 2)
                    m.then_inc(S["units_done"], 1)

                def free(t):
                    pe.wait_ge(S["xhalf_done"], 4 * layer + t + 1)

                def within(t):
                    if q is not None and t >= 2:
                        if t == 2:
                            pe.wait_ge(S["sig_done"], 8 * layer + 6)
                        transposes(q, t - 2)
                by_tile(Ub - 4, range(4, 8), B, nT_hi, nT_lo, KT, within, free)

            pe.wait_ge(S["consts_ready"], 4)
            for t in range(TT + 1):
                if t < TT:
                    transposes(0, t)
                if t:
                    pe.wait_ge(S["nlo_done"], 2 * t)
                    if t == 1:
                        weights(PLAN["v"] + 2)
                    for n in range(2):
                        m = of_tiles(PLAN["v"], n, (t - 1,), A, nT_hi, nT_lo, KT)
                        if t == TT:
                            m.then_inc(S["units_done"], 1)
            by_unit(PLAN["v"], range(2, 4), A, nT_hi, nT_lo, KT)
            by_unit(PLAN["v"], range(4, 8), B, nT_hi, nT_lo, KT)

            def project(h, part, p):
                k = part // 3
                if part % 3 == 0:
                    pe.wait_ge(S["w_lo_done"], PLAN["qk"] + 2 * h + k + 1)
                    if not (isinstance(h, int) and h == 0):
                        pe.wait_ge(S[("qrope_done", "krope_done")[k]], h)
                m = features(A[k], (PLAN["qk"] + 2 * p + k) % RING, nT_hi, nT_lo, part % 3)
                if part % 3 == 2:
                    m.then_inc(S["units_done"], 1)

            def scores(h, p, qt):
                n = (qt + 1) * P
                if not (isinstance(h, int) and h == 0 and qt < 2):
                    pe.wait_ge(S["probs_done"], 8 * h + 2 * qt - 2)
                for c in range(2):
                    rows = slice(HEAD * c, HEAD * c + HEAD)
                    pe.matmul(B[2 * (qt % 2) + c][:, 0:n], qT[p][rows, tok(qt)], kT[p][rows, 0:n], start=True,
                              stop=False)
                for c in range(2):
                    pe.matmul(B[2 * (qt % 2) + c][:, n - P:n], ident_b[:, :], causal_b[:, :], start=False,
                              stop=True).then_inc(S["scores_done"], 1)

            def turn_mix(h, qt):
                pe.wait_ge(S["mix_done"], 4 * h + qt + 1)
                if not (isinstance(h, int) and h == 0 and qt == 0):
                    pe.wait_ge(S["pT_done"], 4 * h + qt)
                for kb in range(qt + 1):
                    m = transpose(A[2][:, kb * P:(kb + 1) * P], amix[:, qt % 2, kb * P:(kb + 1) * P])
                m.then_inc(S["mixT_done"], 1)

            def values(h, qt):
                pe.wait_ge(S["pT_done"], 4 * h + qt + 1)
                if qt == 0 and not (isinstance(h, int) and h == 0):
                    pe.wait_ge(S["oraw_done"], h)
                for kb in range(qt + 1):
                    m = pe.matmul(A[3][:, tok(qt)], pT[:, qt % 2, kb * P:(kb + 1) * P],
                                  V[:, kb, bass.ds(h * P, P)], start=kb == 0, stop=kb == qt)
                m.then_inc(S["pv_done"], 1)

            def turn_o(h):
                pe.wait_ge(S["onrm_done"], h + 1)
                for t in range(TT):
                    m = transpose(A[2][:, tok(t)], o_nrm[:, t, :])
                m.then_inc(S["oT_done"], 1)

            def head(h, p, first=False, last=False):
                def proj(*parts):
                    if not last:
                        for part in parts:
                            project(h + 1, part, 1 - p)
                pe.wait_ge(S["qrope_done"], h + 1)
                pe.wait_ge(S["krope_done"], h + 1)
                scores(h, p, 0)
                scores(h, p, 1)
                proj(0, 1)
                turn_mix(h, 0)
                scores(h, p, 2)
                values(h, 0)
                turn_mix(h, 1)
                scores(h, p, 3)
                proj(2)
                values(h, 1)
                turn_mix(h, 2)
                proj(3)
                if not first:
                    pe.wait_ge(S["pT_done"], 4 * h + 3)
                    turn_o(h - 1)
                proj(4, 5)
                if not first:
                    pe.wait_ge(S["oTlo_done"], h)
                turn_mix(h, 3)
                values(h, 2)
                values(h, 3)

            pe.wait_ge(S["v_done"], 4)
            for part in range(6):
                project(0, part, 0)
            pe.wait_ge(S["v_done"], 8)
            head(0, 0, first=True)
            with pe.Fori(0, (DIFF_HEADS - 2) // 2) as i:
                for p in range(2):
                    head(2 * i + (p + 1), (p + 1) % 2)
            head(DIFF_HEADS - 1, 1, last=True)

            def last_head(n):
                if n == 2:
                    turn_o(DIFF_HEADS - 1)
                if n == 3:
                    pe.wait_ge(S["oTlo_done"], DIFF_HEADS)
            output(PLAN["out0"], 8, 1, oT0_hi, oT0_lo, KT, 0, last_head)
            mlp(0, "up0", 1)
            down(0, "down0", 2, 1)
            embed(0, 3, 2)

            feature_start(PLAN["cmp"], 3)
            U = PLAN["branch"]
            weights(U + 1)
            features(B[2], U % RING, nT_hi, nT_lo).then_inc(S["units_done"], 1)
            pe.wait_ge(S["kr_done"], GROUPS)
            pe.wait_ge(S["shifted_done"], 3 * GROUPS)
            pe.wait_ge(S["cmpw_in"], 80)
            pe.wait_ge(S["pad_ready"], 1)
            for kv, (w1, Z) in enumerate(((w1k, KR), (w1v, VR))):
                tokens_ = Z[:, :, :].rearrange("p g (n l) -> p g n l", l=CMP_STRIDE)
                for m in range(CMP_LEN // 2):
                    l = 2 * m
                    ins = pe.matmul(A[kv][:, 0:(GROUPS + 1) * N_CMP], w1[:, m, :],
                                    tokens_[:, :, l // CMP_STRIDE:l // CMP_STRIDE + N_CMP, l % CMP_STRIDE],
                                    start=m == 0, stop=m == CMP_LEN // 2 - 1)
                ins.then_inc(S["hid_done"], 1)
            pe.wait_ge(S["gsig_done"], 1)
            for t in range(TT):
                m = transpose(A[3][:, tok(t)], gT[:, tok(t)])
            m.then_inc(S["gatesT_done"], 1)

            def compressed_kv():
                pe.wait_ge(S["gelc_done"], 2)
                pe.matmul(A[2][0:HEAD, 0:P], w2[:, 0, :], hid_k[:, :, :].rearrange("p g n -> p (g n)"), start=True,
                          stop=True).then_inc(S["kv_done"], 1)
                for g in range(GROUPS):
                    m = pe.matmul(A[2][0:N_PAD, P + HEAD * g:P + HEAD * g + HEAD], hid_v[:, g, :], w2[:, 1, :],
                                  start=True, stop=True)
                m.then_inc(S["kv_done"], 1)

            def gturn_o(m):
                for t in range(TT):
                    mm = transpose(A[2 + m][:, tok(t)], opair[:, m, tok(t)])
                mm.then_inc(S["goT_done"], 1)

            def group(g, first):
                def step(h, k):
                    return 16 * g + 4 * h + k

                def compressed_scores():
                    pe.wait_ge(S["glo_done"], 6 * g + 4)
                    if first:
                        pe.wait_ge(S["kvc_done"], GHEADS)
                        pe.wait_ge(S["kclo_done"], 1)
                    else:
                        pe.wait_ge(S["oread_done"], 8 * g)
                    for t in range(TT):
                        for h in range(GHEADS):
                            n = (t % 2) * GHEADS + h
                            m = pe.matmul(A[t // 2][:, n * 2 * N_PAD:(n + 1) * 2 * N_PAD], Q[h][:, tok(t)],
                                          kc[:, bass.ds(g, 1), :, :].rearrange("p a b n -> p (a b n)"), start=True,
                                          stop=True)
                    m.then_inc(S["csc_done"], 1)

                def cturn():
                    pe.wait_ge(S["cp_done"], g + 1)
                    if not first:
                        pe.wait_ge(S["goTlo_done"], 2 * g)
                    for t in range(TT):
                        m = transpose(A[3][:, tok(t)], pc[:, t, :, :].rearrange("p h n -> p (h n)"))
                    m.then_inc(S["cpT_done"], 1)

                def vturn():
                    pe.wait_ge(S["vT_done"], g + 1)
                    for t in range(TT):
                        m = transpose(A[0][:, tok(t)], vT[:, tok(t)])
                    m.then_inc(S["vTt_done"], 1)

                def cvalues(m):
                    if m == 0:
                        pe.wait_ge(S["cpTc_done"], g + 1)
                    else:
                        pe.wait_ge(S["vg_done"], g + 1)
                    for t in range(2):
                        mm = pe.matmul(A[1 - m][:, 256 * t:256 * t + 256], pcT[:, 2 * m + t, :],
                                       Vblk[:, bass.ds(g, 1), :].rearrange("p a n -> p (a n)"), start=True, stop=True)
                    mm.then_inc(S["coc_done"], 1)

                def gscores(h, k):
                    qt = ORDER[k]
                    n = (qt + 1) * P
                    if (h, k) == (0, 0):
                        pe.wait_ge(S["ghi_done"], 8 * g + 8)
                        pe.wait_ge(S["gkx_done"], 2 * g + 2)
                    elif (h, k) != (0, 1):
                        pe.wait_ge(S["gprobs_done"], 2 * step(h, k) - 2)
                    for c in range(2):
                        for rows, K in ((slice(0, P), Kh), (side(h % 2), Kl)):
                            pe.matmul(B[2 * (k % 2) + c][:, 0:n], Q[h][rows, tok(qt)], K[rows, c, 0:n],
                                      start=K is Kh, stop=False)
                    for c in range(2):
                        pe.matmul(B[2 * (k % 2) + c][:, n - P:n], ident_b[:, :], causal_b[:, :], start=False,
                                  stop=True).then_inc(S["gscores_done"], 1)

                def gturn(h, k):
                    pe.wait_ge(S["gprobs_done"], 2 * step(h, k) + 2)
                    if not (first and h == 0 and k == 0):
                        pe.wait_ge(S["gpTa_done"], step(h, k))
                        pe.wait_ge(S["gpTv_done"], step(h, k))
                    for c in range(2):
                        for kb in range(ORDER[k] + 1):
                            m = transpose(A[2 + c][:, kb * P:(kb + 1) * P], gp[:, k % 2, c, kb * P:(kb + 1) * P])
                        m.then_inc(S["gT_done"], 1)

                def gvalues(h, k):
                    qt = ORDER[k]
                    pe.wait_ge(S["gpTa_done"], step(h, k) + 1)
                    pe.wait_ge(S["gpTv_done"], step(h, k) + 1)
                    if (h, k) == (0, 0):
                        pe.wait_ge(S["oc_done"], 2 * g + 2)
                    elif k == 0:
                        pe.wait_ge(S["oread_done"], 8 * g + 2 * h)
                    for c in range(2):
                        for kb in range(qt + 1):
                            m = pe.matmul(A[c][:, tok(qt)], gpT[:, k % 2, c, kb * P:(kb + 1) * P],
                                          Vg[:, kb, HEAD * c:HEAD * c + P], start=kb == 0, stop=kb == qt)
                    m.then_inc(S["gpv_done"], 1)

                U = PLAN["group"]
                seq = [(h, k) for h in range(GHEADS) for k in range(TT)]
                for n in range(4):
                    weights(4 * g + (U + n + 1))
                    features(B[n], (U + n) % RING, nT_hi, nT_lo).then_inc(S["units_done"], 1)
                    if n == 0 and first:
                        compressed_kv()
                    if n == 0 and not first:
                        pe.wait_ge(S["opair_done"], 4 * g)
                        for m in range(2):
                            gturn_o(m)
                    if n == 2:
                        compressed_scores()
                cturn()
                gscores(*seq[0])
                vturn()
                gscores(*seq[1])
                cvalues(0)
                for n, (h, k) in enumerate(seq):
                    gturn(h, k)
                    if n + 2 < len(seq):
                        gscores(*seq[n + 2])
                    if n:
                        gvalues(*seq[n - 1])
                    else:
                        cvalues(1)
                gvalues(*seq[-1])

            group(0, True)
            with pe.Fori(1, GROUPS) as g:
                group(g, False)

            def last_pairs(n):
                if n == 1:
                    pe.wait_ge(S["opair_done"], 4 * GROUPS)
                    for m in range(2):
                        gturn_o(m)
                if n == 3:
                    pe.wait_ge(S["goTlo_done"], 2 * GROUPS)
            output(PLAN["out1"], 8, 4, oT1_hi, oT1_lo, KT, 2, last_pairs)
            mlp(1, "up1", 4)
            down(1, "down1", 5, 3)
            embed(1, None, 5)


def by_features(w):
    k, n = w.shape
    return w.reshape(k // P, P, n // P, P).transpose(2, 1, 0, 3).reshape(n // P, P, D)


def by_tokens(w):
    k = w.shape[0]
    return w.reshape(k // (2 * P), 2, P, 2, HALF).transpose(3, 0, 2, 1, 4).reshape(-1, P, D)


def rotary(w):
    k, n = w.shape
    return w.reshape(k, n // HEAD, 2, 2, 16).transpose(0, 1, 3, 2, 4).reshape(k, n)


def pack(i):
    H = 2 * DIFF_HEADS * HEAD
    dw = i["diff_w_in"][0]
    units = [by_tokens(dw[:, 2 * H:])]
    q, k = by_features(rotary(dw[:, :H])), by_features(rotary(dw[:, H:2 * H]))
    units.append(np.stack([q, k], 1).reshape(-1, P, D))
    nw = i["nsa_w_in"][0]
    kv = GROUPS * HEAD
    at = D + kv * np.arange(7)
    part = {n: nw[:, at[j]:at[j + 1]] for j, n in enumerate(("kc", "vc", "ks", "vs", "kw", "vw"))}
    for n in ("kc", "ks", "kw"):
        part[n] = rotary(part[n])
    pair = lambda a, b, g: np.concatenate([part[a][:, g * HEAD:(g + 1) * HEAD], part[b][:, g * HEAD:(g + 1) * HEAD]], 1)
    for layer in range(LAYERS):
        if layer == 1:
            units += [by_features(pair("kc", "vc", g)) for g in range(GROUPS)]
            wide = np.zeros((D, P), np.float32)
            wide[:, :3 * D // HEAD] = nw[:, at[6]:]
            units.append(by_features(wide))
            nq = by_features(rotary(nw[:, :D]))
            for g in range(GROUPS):
                units += [nq[2 * g:2 * g + 2], by_features(pair("ks", "kw", g)), by_features(pair("vs", "vw", g))]
        units.append(by_tokens((i["diff_w_out"], i["nsa_w_out"])[layer][0]))
        up = by_features(i["ffn_w_up"][layer])
        units.append(np.stack([up[:FT], up[FT:]], 1).reshape(-1, P, D))
        units.append(by_tokens(i["ffn_w_down"][layer]))
        gate = by_tokens(i["ple_gate_w"][layer])
        units += [gate[:4], by_tokens(i["ple_proj_w"][layer]), gate[4:]]
    return np.concatenate(units, 0)


def constants():
    c = np.zeros((P, C_ALL), np.float32)
    row = np.arange(P) % HEAD
    freq = 16 * (row // 32) + row % 16
    c[:, C_INV] = np.float32(THETA) ** (-(2 * freq).astype(np.float32) / np.float32(HEAD))
    c[:, C_SIGN] = np.where(row % 32 < 16, -1.0, 1.0)
    c[:, C_IDENT:C_IDENT + P] = np.eye(P)
    c[:, C_CAUSAL:C_CAUSAL + P] = np.where(np.arange(P)[None, :] <= np.arange(P)[:, None], 0.0, MASKED)
    t = np.arange(TT)[None, :, None] * P + np.arange(P)[:, None, None]
    last = np.arange(N_PAD) * CMP_STRIDE + CMP_LEN - 1
    ok = (last <= t) & (np.arange(N_PAD) < N_CMP)
    c[:, C_CMP:] = ok.reshape(P, TT * N_PAD)
    return c


def kernel(**inputs):
    import concourse.bacc as bacc
    from concourse.bass_utils import run_bass_kernel_spmd as run

    i = {k: np.asarray(v) for k, v in inputs.items()}
    perm = np.arange(HEAD).reshape(2, 2, 16).transpose(1, 0, 2).reshape(-1)
    gains = np.concatenate([i["norm_gains"], i["ple_norm_g"][:, None]], 1).reshape(LAYERS * GAINS, 1, D)
    taps = np.concatenate([i["ffn_conv_w"], i["ffn_conv_b"][:, None]], 1)
    arrays = {
        "x": i["x"].reshape(TT, P, D).transpose(1, 0, 2),
        "w": pack(i),
        "const": constants(),
        "gains": np.broadcast_to(gains, (LAYERS * GAINS, P, D)),
        "conv": taps.reshape(LAYERS, 4, 2 * FT, P).transpose(0, 3, 2, 1).reshape(LAYERS, P, 8 * FT),
        "subln": i["diff_subln_g"][0].reshape(P, 1),
        "lam": np.broadcast_to(np.stack([i[f"diff_lam_{n}"][0] for n in ("q1", "k1", "q2", "k2")])[None], (P, 4, HEAD)),
        "pos": np.broadcast_to(i["positions"].reshape(1, SEQ), (P, SEQ)),
        "pT": i["p"][:, 0].reshape(LAYERS, SEQ, 2, P).transpose(0, 3, 2, 1),
        "w1": np.stack([i[f"nsa_{n}_w1"][0].reshape(CMP_LEN // 2, 2, HEAD, CMP_HIDDEN)[:, :, order]
                        .transpose(1, 2, 0, 3).reshape(P, CMP_LEN // 2, CMP_HIDDEN)
                        for n, order in (("ck", perm), ("cv", np.arange(HEAD)))]),
        "cpos": np.stack([np.concatenate([pos.T, np.roll(pos, -1, axis=0).T]) for pos in
                          (i["nsa_ck_pos"][0][:, perm], i["nsa_cv_pos"][0])]),
        "w2": np.stack([i["nsa_ck_w2"][0][:, perm], i["nsa_cv_w2"][0]], 1),
    }
    nc = bacc.Bacc("TRN2", target_bir_lowering=False, num_devices=1)
    feeds, args = {}, []
    for name, a in arrays.items():
        feeds["in_" + name] = np.ascontiguousarray(a)
        args.append(nc.dram_tensor("in_" + name, a.shape, mybir.dt.from_np(a.dtype), kind="ExternalInput").ap())
    out = nc.dram_tensor("out", (P, TT, D), F32, kind="ExternalOutput").ap()
    trunk(nc, *args, out)
    got = run(nc, [feeds], core_ids=[0]).results[0]["out"]
    return got.transpose(1, 0, 2).reshape(1, SEQ, D)
```
